# Optimizing a Trainium2 kernel written in Bass

```python
import jax, jax.numpy as jnp
from jax import lax
import numpy as np

D_MODEL = 1024
BATCH = 1
SEQ = 512
DEPTH = 2

N_MIXERS = 2
N_DN_LAYERS = (DEPTH + 1) // 2
N_MLA_LAYERS = DEPTH // 2
DN_NK = 8
DN_NV = 16
DN_DK = 128
DN_DV = 128
DN_K_DIM = DN_NK * DN_DK
DN_V_DIM = DN_NV * DN_DV
DN_CONV_CH = 2 * DN_K_DIM + DN_V_DIM
DN_IN = DN_CONV_CH + DN_V_DIM + 4 * DN_NV
DN_CONV_W = 5
DN_CONV_PAD = DN_CONV_W // 2
DN_CHUNK = 64
MLA_H = 8
MLA_NOPE = 128
MLA_ROPE = 64
MLA_V = 128
MLA_QR = 384
MLA_KVR = 256
MLA_IN = MLA_QR + MLA_KVR + MLA_ROPE
MLA_ROPE_THETA = 10000.0
MLA_QBLOCK = 128
N_EXPERTS = 16
N_GROUPS = 4
EXPERTS_PER_GROUP = N_EXPERTS // N_GROUPS
TOP_K = 2
D_FF_EXPERT = 256
DEEPNORM_ALPHA = (2 * DEPTH) ** 0.25
DEEPNORM_BETA = (8 * DEPTH) ** -0.25
LN_EPS = 1e-5
RMS_EPS = 1e-6

kernel_name = "hybrid_deltanet_mla_grouped_moe_deepnorm"

def _layernorm(x, g, b):
    xf = x.astype(jnp.float32)
    mu = jnp.mean(xf, -1, keepdims=True)
    var = jnp.mean(jnp.square(xf - mu), -1, keepdims=True)
    y = (xf - mu) * lax.rsqrt(var + LN_EPS) * g.astype(jnp.float32) + b.astype(jnp.float32)
    return y.astype(x.dtype)

def _rmsnorm_f32(x, w):
    xf = x.astype(jnp.float32)
    return xf * lax.rsqrt(jnp.mean(xf * xf, -1, keepdims=True) + RMS_EPS) * w.astype(jnp.float32)

def _l2norm(x):
    return x * lax.rsqrt(jnp.sum(x * x, -1, keepdims=True) + RMS_EPS)

def _short_conv(x, w):
    return lax.conv_general_dilated(x, w[:, None, :], window_strides=(1,),
                                    padding=((DN_CONV_PAD, DN_CONV_PAD),),
                                    dimension_numbers=('NWC', 'WIO', 'NWC'),
                                    feature_group_count=x.shape[-1])

def _gated_delta_rule_chunked(q, k, v, g, beta):
    bsz, nh, seqlen, dk = q.shape
    dv = v.shape[-1]
    n = seqlen // DN_CHUNK

    def chunks(t):
        return jnp.moveaxis(t.reshape(bsz, nh, n, DN_CHUNK, *t.shape[3:]), 2, 0)

    q, k, v, g, beta = (chunks(t) for t in (q, k, v, g, beta))
    g = jnp.cumsum(g, axis=-1)
    idx = jnp.arange(DN_CHUNK)
    lower = idx[:, None] >= idx[None, :]
    strict = idx[:, None] > idx[None, :]
    decay = jnp.exp(jnp.where(lower, g[..., :, None] - g[..., None, :], -jnp.inf))
    k_beta = k * beta[..., None]
    a = jnp.where(strict, jnp.einsum('nbhcd,nbhsd->nbhcs', k_beta, k) * decay, 0.0)
    eye = jnp.eye(DN_CHUNK, dtype=q.dtype)
    t_inv = lax.linalg.triangular_solve(a + eye, jnp.broadcast_to(eye, a.shape),
                                        left_side=True, lower=True, unit_diagonal=True)
    u = jnp.einsum('nbhcs,nbhsd->nbhcd', t_inv, v * beta[..., None])
    w = jnp.einsum('nbhcs,nbhsd->nbhcd', t_inv, k_beta * jnp.exp(g)[..., None])
    qk = jnp.einsum('nbhcd,nbhsd->nbhcs', q, k) * decay

    def step(state, inp):
        q_c, k_c, u_c, w_c, g_c, qk_c = inp
        v_new = u_c - jnp.einsum('bhcd,bhde->bhce', w_c, state)
        o_c = (jnp.einsum('bhcd,bhde->bhce', q_c * jnp.exp(g_c)[..., None], state)
               + jnp.einsum('bhcs,bhse->bhce', qk_c, v_new))
        g_last = g_c[..., -1:]
        state = (state * jnp.exp(g_last)[..., None]
                 + jnp.einsum('bhcd,bhce->bhde', k_c * jnp.exp(g_last - g_c)[..., None], v_new))
        return state, o_c

    state0 = jnp.zeros((bsz, nh, dk, dv), q.dtype)
    _, o = lax.scan(step, state0, (q, k, u, w, g, qk))
    return jnp.moveaxis(o, 0, 2).reshape(bsz, nh, seqlen, dv)

def _gated_deltanet_mixer(x, w_in, conv_w, a_log, dt_bias, norm_w, w_out):
    bsz, seqlen, _ = x.shape
    h = x @ w_in
    qkv, z, b, a = jnp.split(h, [DN_CONV_CH, DN_CONV_CH + DN_V_DIM, DN_CONV_CH + DN_V_DIM + 2 * DN_NV], axis=-1)
    qkv = jax.nn.silu(_short_conv(qkv, conv_w))
    q, k, v = jnp.split(qkv.astype(jnp.float32), [DN_K_DIM, 2 * DN_K_DIM], axis=-1)
    rep = DN_NV // DN_NK
    q = jnp.repeat(_l2norm(q.reshape(bsz, seqlen, DN_NK, DN_DK)) * (DN_DK ** -0.5), rep, axis=2)
    k = jnp.repeat(_l2norm(k.reshape(bsz, seqlen, DN_NK, DN_DK)), rep, axis=2)
    v = v.reshape(bsz, seqlen, DN_NV, DN_DV)
    q, k, v = (t.transpose(0, 2, 1, 3) for t in (q, k, v))
    beta = jax.nn.sigmoid(b.astype(jnp.float32).reshape(bsz, seqlen, 2, DN_NV))
    g = -jnp.exp(a_log.astype(jnp.float32)) * jax.nn.softplus(
        a.astype(jnp.float32).reshape(bsz, seqlen, 2, DN_NV) + dt_bias.astype(jnp.float32))
    o = jnp.zeros_like(v)
    for d in range(2):
        g_d = g[:, :, d].transpose(0, 2, 1)
        b_d = beta[:, :, d].transpose(0, 2, 1)
        if d == 0:
            o = o + _gated_delta_rule_chunked(q, k, v, g_d, b_d)
        else:
            fl = lambda t: jnp.flip(t, axis=2)
            o = o + fl(_gated_delta_rule_chunked(fl(q), fl(k), fl(v), fl(g_d), fl(b_d)))
    o = o.transpose(0, 2, 1, 3)
    o = _rmsnorm_f32(o, norm_w) * jax.nn.silu(z.astype(jnp.float32).reshape(bsz, seqlen, DN_NV, DN_DV))
    return o.reshape(bsz, seqlen, DN_V_DIM).astype(x.dtype) @ w_out

def _rope_tables(positions):
    inv_freq = 1.0 / (MLA_ROPE_THETA ** (jnp.arange(0, MLA_ROPE, 2, dtype=jnp.float32) / MLA_ROPE))
    ang = positions.astype(jnp.float32)[..., None] * inv_freq
    return jnp.cos(ang), jnp.sin(ang)

def _apply_rope(t, cos, sin):
    tf = t.astype(jnp.float32)
    t1, t2 = jnp.split(tf, 2, axis=-1)
    return jnp.concatenate([t1 * cos - t2 * sin, t2 * cos + t1 * sin], -1).astype(t.dtype)

def _block_attention(q_nope, q_rope, k_nope, k_rope, v):
    bsz, nh, seqlen, _ = q_nope.shape
    scale = (MLA_NOPE + MLA_ROPE) ** -0.5

    def blk(i):
        s = i * MLA_QBLOCK
        qn = lax.dynamic_slice_in_dim(q_nope, s, MLA_QBLOCK, axis=2)
        qr = lax.dynamic_slice_in_dim(q_rope, s, MLA_QBLOCK, axis=2)
        sc = (jnp.einsum('bhqd,bhkd->bhqk', qn, k_nope)
              + jnp.einsum('bhqd,bkd->bhqk', qr, k_rope)).astype(jnp.float32) * scale
        p = jax.nn.softmax(sc, axis=-1)
        return jnp.einsum('bhqk,bhkd->bhqd', p.astype(v.dtype), v)

    o = lax.map(blk, jnp.arange(seqlen // MLA_QBLOCK))
    return o.transpose(1, 2, 0, 3, 4).reshape(bsz, nh, seqlen, MLA_V)

def _mla_mixer(x, cos, sin, w_in, q_norm_w, w_qb, kv_norm_w, w_kvb, w_out):
    bsz, seqlen, _ = x.shape
    h = x @ w_in
    c_q, c_kv, k_rope = jnp.split(h, [MLA_QR, MLA_QR + MLA_KVR], axis=-1)
    q = (_rmsnorm_f32(c_q, q_norm_w).astype(x.dtype) @ w_qb).reshape(bsz, seqlen, MLA_H, MLA_NOPE + MLA_ROPE)
    kv = (_rmsnorm_f32(c_kv, kv_norm_w).astype(x.dtype) @ w_kvb).reshape(bsz, seqlen, MLA_H, MLA_NOPE + MLA_V)
    q_nope, q_rope = q[..., :MLA_NOPE], q[..., MLA_NOPE:]
    k_nope, v = kv[..., :MLA_NOPE], kv[..., MLA_NOPE:]
    q_rope = _apply_rope(q_rope, cos[:, :, None], sin[:, :, None])
    k_rope = _apply_rope(k_rope, cos, sin)
    q_nope, q_rope, k_nope, v = (t.transpose(0, 2, 1, 3) for t in (q_nope, q_rope, k_nope, v))
    o = _block_attention(q_nope, q_rope, k_nope, k_rope, v)
    return o.transpose(0, 2, 1, 3).reshape(bsz, seqlen, MLA_H * MLA_V) @ w_out

def _grouped_moe(x, router_w, router_bias, w_gate, w_up, w_down):
    bsz, seqlen, d = x.shape
    t = x.reshape(-1, d)
    scores = jax.nn.sigmoid((t @ router_w).astype(jnp.float32))
    sel = (scores + router_bias.astype(jnp.float32)).reshape(-1, N_GROUPS, EXPERTS_PER_GROUP)
    group_score = jnp.sum(lax.top_k(sel, TOP_K)[0], axis=-1)
    _, gidx = lax.top_k(group_score, 1)
    in_group = jax.nn.one_hot(gidx[:, 0], N_GROUPS, dtype=jnp.bool_)[:, :, None]
    masked = jnp.where(in_group, sel, -jnp.inf).reshape(-1, N_EXPERTS)
    _, eidx = lax.top_k(masked, TOP_K)
    wts = jnp.take_along_axis(scores, eidx, axis=-1)
    wts = wts / jnp.sum(wts, -1, keepdims=True)
    gates = jnp.sum(jax.nn.one_hot(eidx, N_EXPERTS, dtype=jnp.float32) * wts[..., None], axis=1)
    hid = jax.nn.silu(jnp.einsum('td,edf->tef', t, w_gate)) * jnp.einsum('td,edf->tef', t, w_up)
    y = jnp.einsum('tef,efd->td', hid * gates.astype(hid.dtype)[..., None], w_down)
    return y.reshape(bsz, seqlen, d)

def setup_inputs(seed: int = 0) -> dict:
    key = jax.random.key(seed)
    ks = jax.random.split(key, 24)
    nrm = lambda k, shape, s: jax.random.normal(k, shape, jnp.float32) * s
    D = D_MODEL
    x = jax.random.normal(ks[0], (BATCH, SEQ, D), jnp.float32)
    positions = (jnp.arange(SEQ, dtype=jnp.int32)[None, :]
                 + jax.random.randint(ks[1], (BATCH, 1), 0, SEQ, dtype=jnp.int32))
    dn_w_in = nrm(ks[2], (N_DN_LAYERS, D, DN_IN), D ** -0.5)
    dn_conv_w = nrm(ks[3], (N_DN_LAYERS, DN_CONV_W, DN_CONV_CH), DN_CONV_W ** -0.5)
    dn_a_log = jnp.log(jax.random.uniform(ks[4], (N_DN_LAYERS, 2, DN_NV), jnp.float32, 1.0, 16.0))
    dt = jnp.exp(jax.random.uniform(ks[5], (N_DN_LAYERS, 2, DN_NV), jnp.float32, np.log(1e-3), np.log(1e-1)))
    dn_dt_bias = dt + jnp.log(-jnp.expm1(-dt))
    dn_norm_w = 1.0 + nrm(ks[6], (N_DN_LAYERS, DN_DV), 0.02)
    dn_w_out = nrm(ks[7], (N_DN_LAYERS, DN_V_DIM, D), DN_V_DIM ** -0.5 * DEEPNORM_BETA)
    mla_w_in = nrm(ks[8], (N_MLA_LAYERS, D, MLA_IN), D ** -0.5)
    mla_q_norm = 1.0 + nrm(ks[9], (N_MLA_LAYERS, MLA_QR), 0.02)
    mla_w_qb = nrm(ks[10], (N_MLA_LAYERS, MLA_QR, MLA_H * (MLA_NOPE + MLA_ROPE)), MLA_QR ** -0.5)
    mla_kv_norm = 1.0 + nrm(ks[11], (N_MLA_LAYERS, MLA_KVR), 0.02)
    mla_w_kvb = nrm(ks[12], (N_MLA_LAYERS, MLA_KVR, MLA_H * (MLA_NOPE + MLA_V)), MLA_KVR ** -0.5)
    mla_w_out = nrm(ks[13], (N_MLA_LAYERS, MLA_H * MLA_V, D), (MLA_H * MLA_V) ** -0.5 * DEEPNORM_BETA)
    ln1_g = 1.0 + nrm(ks[14], (DEPTH, D), 0.02)
    ln1_b = nrm(ks[15], (DEPTH, D), 0.02)
    ln2_g = 1.0 + nrm(ks[16], (DEPTH, D), 0.02)
    ln2_b = nrm(ks[17], (DEPTH, D), 0.02)
    router_w = nrm(ks[18], (D, N_EXPERTS), D ** -0.5)
    router_bias = nrm(ks[19], (N_EXPERTS,), 0.01)
    moe_w_gate = nrm(ks[20], (DEPTH, N_EXPERTS, D, D_FF_EXPERT), D ** -0.5)
    moe_w_up = nrm(ks[21], (DEPTH, N_EXPERTS, D, D_FF_EXPERT), D ** -0.5)
    moe_w_down = nrm(ks[22], (DEPTH, N_EXPERTS, D_FF_EXPERT, D), D_FF_EXPERT ** -0.5 * DEEPNORM_BETA)
    return {"x": x, "positions": positions,
            "dn_w_in": dn_w_in, "dn_conv_w": dn_conv_w, "dn_a_log": dn_a_log, "dn_dt_bias": dn_dt_bias,
            "dn_norm_w": dn_norm_w, "dn_w_out": dn_w_out,
            "mla_w_in": mla_w_in, "mla_q_norm": mla_q_norm, "mla_w_qb": mla_w_qb,
            "mla_kv_norm": mla_kv_norm, "mla_w_kvb": mla_w_kvb, "mla_w_out": mla_w_out,
            "ln1_g": ln1_g, "ln1_b": ln1_b, "ln2_g": ln2_g, "ln2_b": ln2_b,
            "router_w": router_w, "router_bias": router_bias,
            "moe_w_gate": moe_w_gate, "moe_w_up": moe_w_up, "moe_w_down": moe_w_down}

def reference(x, positions, dn_w_in, dn_conv_w, dn_a_log, dn_dt_bias, dn_norm_w, dn_w_out,
              mla_w_in, mla_q_norm, mla_w_qb, mla_kv_norm, mla_w_kvb, mla_w_out,
              ln1_g, ln1_b, ln2_g, ln2_b, router_w, router_bias, moe_w_gate, moe_w_up, moe_w_down):
    cos, sin = _rope_tables(positions)
    for i in range(DEPTH):
        j = i // N_MIXERS
        if i % N_MIXERS == 0:
            y = _gated_deltanet_mixer(x, dn_w_in[j], dn_conv_w[j], dn_a_log[j], dn_dt_bias[j],
                                      dn_norm_w[j], dn_w_out[j])
        else:
            y = _mla_mixer(x, cos, sin, mla_w_in[j], mla_q_norm[j], mla_w_qb[j],
                           mla_kv_norm[j], mla_w_kvb[j], mla_w_out[j])
        x = _layernorm(DEEPNORM_ALPHA * x + y.astype(x.dtype), ln1_g[i], ln1_b[i])
        y = _grouped_moe(x, router_w, router_bias, moe_w_gate[i], moe_w_up[i], moe_w_down[i])
        x = _layernorm(DEEPNORM_ALPHA * x + y.astype(x.dtype), ln2_g[i], ln2_b[i])
    return x


_drawn_inputs = setup_inputs


def setup_inputs(seed=0):
    import zlib

    import numpy as np

    out = dict(_drawn_inputs(seed))
    spreads = {}
    factors = {'dn_norm_w': 2.718, 'mla_q_norm': 8.0, 'mla_kv_norm': 8.0}
    for name, (base, spread) in spreads.items():
        noise = np.random.default_rng([zlib.crc32(name.encode()), seed]).standard_normal(out[name].shape)
        drawn = base * np.exp(spread * noise) if base else spread * noise
        out[name] = __import__('jax').numpy.asarray(drawn.astype(out[name].dtype))
    for name, factor in factors.items():
        out[name] = (out[name] * factor).astype(out[name].dtype)
    return out
```

```python
from contextlib import ExitStack

import numpy as np

import concourse.bass as bass
from concourse import mybir

ALU = mybir.AluOpType
ACT = mybir.ActivationFunctionType
AX = mybir.AxisListType
F32 = mybir.dt.float32

P = 128
D = 1024
SEQ = 512
TT = SEQ // P
KD = D // P
ALPHA = 4.0 ** 0.25
LN_EPS = 1e-5
RMS_EPS = 1e-6

NK, NV, DH = 8, 16, 128
K_OFF, V_OFF, Z_OFF, BA_OFF = NK * DH, 2 * NK * DH, 2 * NK * DH + NV * DH, 2 * NK * DH + 2 * NV * DH
TAPS = 5
LEVELS = 7
GRAW, NEG_EG, EG, BETA, COEF, EGL = range(6)

C_ID, C_ONE, C_TF, C_TB, C_SF, C_SB = (P * n for n in range(6))
C_LEV = 6 * P
C_JLT = C_LEV + 2 * LEVELS * 64
C_FREQ = C_JLT + 16
C_ALL = C_FREQ + 32


def constants():
    c = np.zeros((P, C_ALL), np.float32)
    r, q = np.arange(P)[:, None], np.arange(P)[None, :]
    c[:, C_ID:C_ID + P] = r == q
    c[:, C_ONE:C_ONE + P] = 1.0
    c[:, C_TF:C_TF + P] = r <= q
    c[:, C_TB:C_TB + P] = r >= q
    c[:, C_SF:C_SF + P] = r > q
    c[:, C_SB:C_SB + P] = r < q
    for d in range(2):
        for l in range(LEVELS):
            b = 1 << l
            m = (r // (2 * b) == q // (2 * b)) & ((r // b) % 2 == 1 - d) & ((q // b) % 2 == d)
            cols = [x for x in range(P) if (x // b) % 2 == d]
            at = C_LEV + (d * LEVELS + l) * 64
            c[:, at:at + 64] = m[:, cols]
    i, j = np.arange(4)[:, None], np.arange(4)[None, :]
    c[:, C_JLT:C_JLT + 16] = (j < i).reshape(1, 16)
    inv = (1.0 / (10000.0 ** (np.arange(0, 64, 2, dtype=np.float32) / np.float32(64)))).astype(np.float32)
    c[:, C_FREQ:C_FREQ + 32] = inv[None]
    return c




class Uses:

    def __init__(self, names):
        self.at, self.per, self.before, last = {}, {}, {}, {}
        for name, bank in names:
            self.before[name] = last.get(bank)
            last[bank] = name
            self.at[name] = (bank, self.per.get(bank, 0))
            self.per[bank] = self.per.get(bank, 0) + 1


PROJECT = [("proj0", 0), ("proj1", 1), ("proj2", 0), ("proj3", 1)]
def phase(nc, ctx, prefix=""):
    made = []

    def end():
        nc.clear_and_free_semaphores(made)
        nc.all_engine_barrier()

    def sem(name):
        made.append(nc.alloc_semaphore(name=prefix + name))
        return made[-1]

    ctx.callback(end)
    return sem


def dn_uses(with_next):
    names = [("taps", 2)] if with_next else []
    names += [("D0", 2), ("D1", 3)] + [(f"tr{c}", 2 + c % 2) for c in range(4)]
    names += [("D2", 2), ("D3", 3), ("kT", 2), ("qT", 3), ("KK", 2), ("KQ", 3)]
    if with_next:
        names += PROJECT
    for l in range(LEVELS):
        for g in range(4):
            names += [(f"X{l}{g}", 4 + g % 2), (f"U{l}{g}", 6 + g % 2)]
    names += [("z0", 0), ("z1", 1)]
    for s in range(4):
        for d in range(2):
            if s:
                names.append((f"kq{s}{d}", 4 + d))
            names += [(f"w{s}{d}", 2 + d), (f"os{s}{d}", 6 + d)]
    names += [("oT0", 2), ("oT1", 3)] + [(f"y{n}", n % 2) for n in range(8)]
    return Uses(names)


RSQRT_STEPS = 11


def rsqrt(nc, step, out, x, tmp):
    i32 = mybir.dt.int32
    step(nc.vector.tensor_scalar(out.bitcast(i32), x.bitcast(i32), 1, None, ALU.logical_shift_right))
    step(nc.vector.tensor_scalar(out.bitcast(i32), out.bitcast(i32), -1.0, float(0x5F3759DF), ALU.mult, ALU.add))
    for _ in range(3):
        step(nc.vector.tensor_tensor(tmp, out, out, ALU.mult))
        step(nc.vector.scalar_tensor_tensor(out=tmp, in0=tmp, scalar=-0.5, in1=x, op0=ALU.mult, op1=ALU.mult))
        step(nc.vector.scalar_tensor_tensor(out=out, in0=tmp, scalar=1.5, in1=out, op0=ALU.add, op1=ALU.mult))


def delta_net(nc, t, s, dram):
    F = Uses(PROJECT + [("taps", 2)])
    MAIN, LAST = dn_uses(True), dn_uses(False)
    c, ps, res, xT = t["const"], t["ps"], t["res"], t["xT"]
    ident, ones = c[:, C_ID:C_ID + P], c[:, C_ONE:C_ONE + P]
    tri = [c[:, C_TF:C_TF + P], c[:, C_TB:C_TB + P]]
    after = [c[:, C_SF:C_SF + P], c[:, C_SB:C_SB + P]]
    before = [after[1], after[0]]

    with ExitStack() as ctx:
        def sb(name, shape):
            return ctx.enter_context(nc.sbuf_tensor(name, shape, F32))

        sem = phase(nc, ctx)

        wqkv = sb("wqkv", [P, 4, KD, P])
        wz = sb("wz", [P, KD, 2 * P])
        wo = sb("wo", [P, 2, D])
        tapr = sb("tapr", [TAPS, 4, P])
        taps = sb("taps", [P, 4, TAPS])
        conv = sb("conv", [P, 4, SEQ])
        th = sb("th", [P, 2, SEQ])
        sq = sb("sq", [P, 2, SEQ])
        kq = sb("kq", [P, 2, TT, P])
        kqT = sb("kqT", [P, 2, TT, P])
        v = sb("v", [P, 2, TT, P])
        zs = sb("zs", [P, TT, 2, P])
        ss = sb("ss", [P, 8])
        rs = sb("rs", [P, 8])
        nt = sb("nt", [P, 8])
        triG = sb("triG", [P, 2, TT, P])
        dec = sb("dec", [P, 4, TT, P])
        kkm = sb("kkm", [P, 2, TT, P])
        kqm = sb("kqm", [P, 2, TT, P])
        A = sb("A", [P, 4, TT, P])
        T = sb("T", [P, 4, TT, P])
        U = sb("U", [P, 4, TT, P])
        X = sb("X", [P, LEVELS, 2, TT, P])
        St = sb("St", [P, 2, 2, P])
        r = sb("r", [P, 2, 2, P])
        vn = sb("vn", [P, 2, 2, P])
        vs = sb("vs", [P, 2, 2, P])
        o = sb("o", [P, TT, 2, P])
        oT = sb("oT", [P, 2, TT, P])
        gt = sb("gt", [P, 6, TT, 2 * NV])
        gb = sb("gb", [P, 6 * TT, 2, 2])
        nw = sb("nw", [P, 1])
        bvec = sb("bvec", [P, 2, 2 * NV])
        wba = sb("wba", [P, KD, 4 * NV])
        ba = sb("ba", [P, TT, 4 * NV])
        tmp = sb("tmp", [P, 4, TT, 2 * NV])

        full = [sem(f"dn_full{b}") for b in range(8)]
        x_in, small_in, ba_in = sem("x_in"), sem("small_in"), sem("ba_in")
        w_in = [sem(f"w_in{n}") for n in range(4)]
        z_in, o_in, taps_in = sem("z_in"), sem("o_in"), sem("taps_in")
        link, alink, plink = sem("dve_link"), sem("act_link"), sem("pool_link")
        x_turned = sem("x_turned")
        xT_ready = sem("xT_ready")
        gates_ready, raw_ready, beta_ready = sem("gates_ready"), sem("raw_ready"), sem("beta_ready")
        sums_ready = sem("sums_ready")
        gb_ready, triG_ready, dec_ready, at_ready, qkd_ready = (sem(n) for n in ("gb_ready", "triG_ready", "dec_ready", "at_ready", "qkd_ready"))
        eye_ready = sem("eye_ready")
        taps_ready, conv_ready, th_ready, silu_ready = (sem(n) for n in ("taps_ready", "conv_ready", "th_ready", "silu_ready"))
        sq_ready, ss_ready, rs_ready, kq_ready, kqT_ready, v_ready = (sem(n) for n in ("sq_ready", "ss_ready", "rs_ready", "kq_ready", "kqT_ready", "v_ready"))
        mask_ready = sem("mask_ready")
        xm_ready, upd_ready = sem("xm_ready"), sem("upd_ready")
        zt_ready, zs_ready = sem("zt_ready"), sem("zs_ready")
        r_ready, vs_ready, vn_ready, S_ready, o_step = (sem(n) for n in ("r_ready", "vs_ready", "vn_ready", "S_ready", "o_step"))
        oq_ready, ba_ready, dve_sums = sem("oq_ready"), sem("ba_ready"), sem("dve_sums")
        osq_ready, oss_ready, ors_ready, on_ready, og_ready, oT_ready, y_ready = (sem(n) for n in ("osq_ready", "oss_ready", "ors_ready", "on_ready", "og_ready", "oT_ready", "y_ready"))
        x_zero = sem("x_zero")

        base = {0: 2, 1: 2, 2: 2, 3: 1, 4: 4, 5: 4, 6: 0, 7: 0}

        def read_of(name, i):
            if name[:-1] in ("D", "tr", "proj", "z", "y", "oT"):
                n = int(name[-1])
                if name[:-1] == "tr":
                    return (v_ready, i * 2 + n - 1) if n >= 2 else (kq_ready, i * 2 + 2 - n)
                return {"D": (dec_ready, i * 4 + n + 1), "proj": (conv_ready, (i + 1) * 4 + n + 1), "z": (zs_ready, i * 2 + n + 1),
                        "y": (y_ready, 1 + i * 8 + n + 1), "oT": (oT_ready, 1 + i * 2 + n + 1)}[name[:-1]]
            if name in ("kT", "qT"):
                return kqT_ready, i * 2 + (1 if name == "kT" else 2)
            if name in ("KK", "KQ"):
                return mask_ready, i * 4 + (2 if name == "KK" else 4)
            if name == "taps":
                return taps_ready, i + 2
            a, b = int(name[-2]), int(name[-1])
            if name[0] in "XU":
                return (xm_ready if name[0] == "X" else upd_ready), i * 28 + a * 4 + b + 1
            if name[:2] == "kq":
                return oq_ready, i * 6 + (a - 1) * 2 + b + 1
            if name[0] == "w":
                return vn_ready, i * 8 + a * 2 + b + 1
            return o_step, 1 + i * 8 + a * 2 + b + 1

        last_read = {0: (y_ready, 8), 1: (y_ready, 8), 2: (oT_ready, 2), 3: (oT_ready, 2), 4: (o_step, 8), 5: (o_step, 8), 6: (o_step, 8), 7: (o_step, 8)}

        def nth(uses, name, i):
            b, k = uses.at[name]
            return b, base[b] + i * MAIN.per[b] + k

        def level(a, d, l, other=0):
            b = 1 << l
            return a.rearrange("p (a h b) -> p a h b", h=2, b=b)[:, :, (d + other) % 2, :]

        w_dram = dram["dn_w_in"][0].rearrange("(k p) n -> p k n", p=P)
        wo_dram = dram["dn_w_out"][0].rearrange("(h p) n -> p h n", p=P)
        cw_dram = dram["dn_conv_w"][0]

        block = ctx.enter_context(nc.Block())

        @block.sync
        def _(sp):
            x_dram = dram["x"][0].rearrange("(t p) n -> p t n", p=P)
            sp.dma_start(c[:], dram["const"]).then_inc(small_in, 16)
            for tt in range(TT):
                sp.dma_start(res[:, tt], x_dram[:, tt]).then_inc(t["x_in"][tt], 16)
            sp.dma_start(wba[:], w_dram[:, :, BA_OFF:BA_OFF + 4 * NV]).then_inc(ba_in, 16)
            sp.dma_start(bvec[:, 0], dram["dn_a_log"][0].rearrange("d h -> (d h)").partition_broadcast(P)).then_inc(small_in, 16)
            sp.dma_start(bvec[:, 1], dram["dn_dt_bias"][0].rearrange("d h -> (d h)").partition_broadcast(P)).then_inc(small_in, 16)
            sp.dma_start(nw[:], dram["dn_norm_w"].rearrange("a p -> p a")).then_inc(small_in, 16)

            def load_w(n, dynamic):
                at = (lambda off, w: bass.ds(off, w)) if dynamic else (lambda off, w: slice(off, off + w))
                for ct in range(4):
                    off = [n * P, K_OFF + n * P, V_OFF + n * 2 * P, V_OFF + n * 2 * P + P][ct]
                    if dynamic or n:
                        b, k = (F.at[f"proj{ct}"])
                        if dynamic:
                            sp.wait_ge(conv_ready, (n - 1) * 4 + ct + 1)
                    sp.dma_start(wqkv[:, ct], w_dram[:, :, at(off, P)]).then_inc(w_in[ct], 16)
                if dynamic:
                    sp.wait_ge(taps_ready, n)
                for a, (off, w) in enumerate([(n * P, P), (K_OFF + n * P, P), (V_OFF + n * 2 * P, 2 * P)]):
                    sp.dma_start(tapr[:, a:a + w // P].rearrange("p a b -> p (a b)"), cw_dram[:, at(off, w)]).then_inc(taps_in, 16)

            def load_late(n, dynamic):
                at = (lambda off, w: bass.ds(off, w)) if dynamic else (lambda off, w: slice(off, off + w))
                if dynamic:
                    sp.wait_ge(zs_ready, n * 2)
                sp.dma_start(wz[:], w_dram[:, :, at(Z_OFF + n * 2 * P, 2 * P)]).then_inc(z_in, 16)
                if dynamic:
                    sp.wait_ge(y_ready, 1 + n * 8)
                src = wo_dram[:, at(n * 2, 2), :]
                sp.dma_start(wo[:], src).then_inc(o_in, 16)

            load_w(0, False)
            load_late(0, False)
            with sp.Fori(1, NK) as n:
                load_w(n, True)
                load_late(n, True)

        @block.tensor
        def _(pe):
            def begin(uses, name, i):
                b, k = uses.at[name]
                if k == 0:
                    signal, per = last_read[b]
                    pe.wait_ge(signal, 1 + i * per)
                else:
                    pe.wait_ge(*read_of(uses.before[name], i))
                return ps[b]

            def done(mm, uses, name):
                mm.then_inc(full[uses.at[name][0]], 1)

            pe.wait_ge(small_in, 64)
            for n in range(8):
                tt, half = n // 2, n % 2
                if half == 0:
                    pe.wait_ge(t["x_in"][tt], 16)
                b = 4 + n % 2
                if n >= 2:
                    pe.wait_ge(xT_ready, n - 1)
                for k in range(4):
                    mm = pe.transpose(ps[b][:, k * P:(k + 1) * P], res[:, tt, (half * 4 + k) * P:(half * 4 + k + 1) * P], ident)
                mm.then_inc(full[b], 1)
            pe.wait_ge(ba_in, 16)
            pe.wait_ge(xT_ready, 8)
            for tt in range(TT):
                for k in range(KD):
                    mm = pe.matmul(ps[2][:, tt * 64:(tt + 1) * 64], xT[:, k, tt * P:(tt + 1) * P], wba[:, k], start=k == 0, stop=k == KD - 1)
            mm.then_inc(full[2], 1)

            def project(uses, i, n, ct, part=(0, KD)):
                if part[0] == 0:
                    pe.wait_ge(w_in[ct], (n + 1) * 16)
                    begin(uses, f"proj{ct}", i)
                bank = ps[uses.at[f"proj{ct}"][0]]
                for k in range(*part):
                    mm = pe.matmul(bank[:], wqkv[:, ct, k], xT[:, k], start=k == 0, stop=k == KD - 1)
                if part[1] == KD:
                    done(mm, uses, f"proj{ct}")

            def tap_rows(uses, i, n):
                pe.wait_ge(taps_in, (n + 1) * 48)
                bank = begin(uses, "taps", i)
                for ct in range(4):
                    mm = pe.matmul(bank[:, ct * TAPS:(ct + 1) * TAPS], tapr[:, ct], ident[0:TAPS, 0:TAPS], start=True, stop=True)
                done(mm, uses, "taps")

            pe.wait_ge(raw_ready, 1)
            for d in range(2):
                pe.matmul(ps[3][:, 0:P].rearrange("p (t g) -> p t g", t=TT)[:, :, d * NV:(d + 1) * NV], tri[d], gt[:, GRAW, :, d * NV:(d + 1) * NV], start=True, stop=True)
            mm = pe.matmul(ps[3][:, P:2 * P], ones, gt[:, GRAW].rearrange("p t g -> p (t g)"), start=True, stop=True)
            mm.then_inc(full[3], 1)

            pe.wait_ge(taps_in, 48)
            pe.wait_ge(ba_ready, 1)
            for ct in range(4):
                mm = pe.transpose(ps[2][:, ct * TAPS:(ct + 1) * TAPS], tapr[:, ct], ident[0:TAPS, 0:TAPS])
            mm.then_inc(full[2], 1)
            for ct in range(4):
                pe.wait_ge(w_in[ct], 16)
                b = ct % 2
                if ct >= 2:
                    pe.wait_ge(conv_ready, ct - 1)
                for kk in range(KD):
                    mm = pe.matmul(ps[b][:], wqkv[:, ct, kk], xT[:, kk], start=kk == 0, stop=kk == KD - 1)
                mm.then_inc(full[b], 1)

            def body(i, uses, with_next):
                fill = []
                if with_next:
                    for ct in range(4):
                        for a in range(0, KD, 2):
                            fill.append((project, (uses, i, i + 1, ct, (a, a + 2))))
                    tap_rows(uses, i, i + 1)

                def filler(n=1):
                    for _ in range(n):
                        if fill:
                            f, a = fill.pop(0)
                            f(*a)

                def decay(g):
                    pe.wait_ge(triG_ready, i * 4 + g + 1)
                    bank = begin(uses, f"D{g}", i)
                    done(pe.matmul(bank[:], after[g // 2], triG[:, g % 2].rearrange("p t n -> p (t n)"), start=True, stop=True), uses, f"D{g}")

                decay(0)
                decay(1)
                for ct in range(4):
                    pe.wait_ge(silu_ready, i * 4 + ct + 1)
                    bank = begin(uses, f"tr{ct}", i)
                    for tt in range(TT):
                        mm = pe.transpose(bank[:, tt * P:(tt + 1) * P], conv[:, ct, tt * P:(tt + 1) * P], ident)
                    done(mm, uses, f"tr{ct}")
                filler(2)
                decay(2)
                decay(3)
                filler(2)
                for n, ct in ((1, 1), (0, 0)):
                    name = "kT" if n else "qT"
                    pe.wait_ge(kq_ready, i * 2 + (1 if ct else 2))
                    bank = begin(uses, name, i)
                    for tt in range(TT):
                        mm = pe.transpose(bank[:, tt * P:(tt + 1) * P], kq[:, ct, tt], ident)
                    done(mm, uses, name)
                filler(1)
                pe.wait_ge(kqT_ready, i * 2 + 1)
                bank = begin(uses, "KK", i)
                for tt in range(TT):
                    mm = pe.matmul(bank[:, tt * P:(tt + 1) * P], kqT[:, 1, tt], kqT[:, 1, tt], start=True, stop=True)
                done(mm, uses, "KK")
                pe.wait_ge(kqT_ready, i * 2 + 2)
                bank = begin(uses, "KQ", i)
                for tt in range(TT):
                    mm = pe.matmul(bank[:, tt * P:(tt + 1) * P], kqT[:, 1, tt], kqT[:, 0, tt], start=True, stop=True)
                done(mm, uses, "KQ")
                filler(2)

                pe.wait_ge(eye_ready, i * 8 + 8)

                def make_x(n):
                    l, g = divmod(n, 4)
                    d = g // 2
                    if l == 0:
                        pe.wait_ge(at_ready, i * 4 + g + 1)
                    else:
                        pe.wait_ge(upd_ready, i * 28 + n - 4 + 1)
                    bank = begin(uses, f"X{l}{g}", i)
                    for tt in range(TT):
                        mm = pe.matmul(bank[:, tt * 64:(tt + 1) * 64], A[:, g, tt], level(T[:, g, tt], d, l), start=True, stop=True)
                    done(mm, uses, f"X{l}{g}")

                def make_u(n):
                    l, g = divmod(n, 4)
                    d = g // 2
                    pe.wait_ge(xm_ready, i * 28 + n + 1)
                    bank = begin(uses, f"U{l}{g}", i)
                    for tt in range(TT):
                        if 0 < l < LEVELS - 1:
                            pe.matmul(bank[:, tt * 64:(tt + 1) * 64], U[:, g, tt], level(X[:, l, g % 2, tt], d, l), start=True, stop=True)
                        mm = pe.matmul(bank[:, 256 + tt * 64:256 + (tt + 1) * 64], X[:, l, g % 2, tt], level(U[:, g, tt], d, l, 1), start=True, stop=True)
                    done(mm, uses, f"U{l}{g}")

                for n in range(LEVELS * 4 + 2):
                    if n < LEVELS * 4:
                        make_x(n)
                    if n >= 2:
                        make_u(n - 2)
                    if n in (1, 4, 6, 8, 10, 11, 13, 15, 17):
                        filler(1)
                filler(99)

                pe.wait_ge(z_in, (i + 1) * 16)

                def make_z(tt):
                    name = f"z{tt // 2}"
                    if tt % 2 == 0:
                        begin(uses, name, i)
                    bank = ps[uses.at[name][0]]
                    for k in range(KD):
                        mm = pe.matmul(bank[:, (tt % 2) * 256:(tt % 2) * 256 + 256], xT[:, k, tt * P:(tt + 1) * P], wz[:, k], start=k == 0, stop=k == KD - 1)
                    if tt % 2:
                        done(mm, uses, name)

                for step in range(4):
                    for d in range(2):
                        tt = 3 - step if d else step
                        if step:
                            pe.wait_ge(S_ready, i * 6 + (step - 1) * 2 + d + 1)
                            bank = begin(uses, f"kq{step}{d}", i)
                            S2 = St[:, d].rearrange("p h n -> p (h n)")
                            pe.matmul(bank[:, 0:256], kqT[:, 1, tt], S2, start=True, stop=True)
                            mm = pe.matmul(bank[:, 256:512], kqT[:, 0, tt], S2, start=True, stop=True)
                            done(mm, uses, f"kq{step}{d}")
                    for k in range(0, 1):
                        make_z(step)
                    for d in range(2):
                        tt = 3 - step if d else step
                        if step:
                            pe.wait_ge(r_ready, i * 6 + (step - 1) * 2 + d + 1)
                        else:
                            pe.wait_ge(upd_ready, i * 28 + 28)
                            pe.wait_ge(v_ready, i * 2 + 2)
                        bank = begin(uses, f"w{step}{d}", i)
                        for h in range(2):
                            mm = pe.matmul(bank[:, h * P:(h + 1) * P], U[:, d * 2 + h, tt], r[:, d, h] if step else v[:, h, tt], start=True, stop=True)
                        done(mm, uses, f"w{step}{d}")
                    for d in range(2):
                        tt = 3 - step if d else step
                        bank = begin(uses, f"os{step}{d}", i)
                        if step < 3:
                            pe.wait_ge(vs_ready, i * 6 + step * 2 + d + 1)
                            pe.matmul(bank[:, 256:512], kq[:, 1, tt], vs[:, d].rearrange("p h n -> p (h n)"), start=True, stop=True)
                        pe.wait_ge(vn_ready, i * 8 + step * 2 + d + 1)
                        pe.wait_ge(qkd_ready, i * 4 + 4)
                        for h in range(2):
                            mm = pe.matmul(bank[:, h * P:(h + 1) * P], dec[:, d * 2 + h, tt], vn[:, d, h], start=True, stop=True)
                        done(mm, uses, f"os{step}{d}")

                for h in range(2):
                    pe.wait_ge(og_ready, i + 1)
                    bank = begin(uses, f"oT{h}", i)
                    for tt in range(TT):
                        mm = pe.transpose(bank[:, tt * P:(tt + 1) * P], o[:, tt, h], ident)
                    done(mm, uses, f"oT{h}")
                pe.wait_ge(o_in, (i + 1) * 16)
                pe.wait_ge(oT_ready, 1 + i * 2 + 2)
                for n in range(8):
                    tt, half = n // 2, n % 2
                    bank = begin(uses, f"y{n}", i)
                    for h in range(2):
                        mm = pe.matmul(bank[:], oT[:, h, tt], wo[:, h, half * 512:(half + 1) * 512], start=h == 0, stop=h == 1)
                    done(mm, uses, f"y{n}")

            pe.wait_ge(taps_ready, 1)
            pe.wait_ge(conv_ready, 4)
            pe.wait_ge(dve_sums, 1)
            with pe.Fori(0, NK - 1) as i:
                body(i, MAIN, True)
            body(NK - 1, LAST, False)

        @block.scalar
        def _(act):
            def got(uses, name, i):
                b, n = nth(uses, name, i)
                act.wait_ge(full[b], n + 1)
                return ps[b]

            act.sem_inc(oT_ready, 1)
            for n in range(8):
                b = 4 + n % 2
                act.wait_ge(full[b], n // 2 + 1)
                tt, half = n // 2, n % 2
                act.copy(xT[:, half * 4:half * 4 + 4, tt * P:(tt + 1) * P], ps[b][:].rearrange("p (k n) -> p k n", k=4)).then_inc(xT_ready, 1)

            act.wait_ge(full[2], 1)
            act.copy(ba[:].rearrange("p t g -> p (t g)"), ps[2][:, 0:256]).then_inc(ba_ready, 1)
            act.wait_ge(ba_ready, 1)
            act.activation(tmp[:, 0], ba[:, :, 0:32], ACT.Exp, scale=-1.0).then_inc(beta_ready, 1)
            act.activation(bvec[:, 0], bvec[:, 0], ACT.Exp).then_inc(beta_ready, 1)
            act.wait_ge(gates_ready, 1)
            act.activation(tmp[:, 2], tmp[:, 2], ACT.Exp).then_inc(alink, 1)
            act.wait_ge(alink, 1)
            act.activation(tmp[:, 2], tmp[:, 2], ACT.Ln, bias=1.0).then_inc(beta_ready, 1)
            act.wait_ge(gates_ready, 2)
            act.activation(gt[:, EG], tmp[:, 0], ACT.Exp).then_inc(sums_ready, 1)
            act.activation(gt[:, EGL], tmp[:, 3], ACT.Exp).then_inc(sums_ready, 1)
            act.activation(tmp[:, 1], tmp[:, 1], ACT.Exp).then_inc(sums_ready, 1)

            def act_silu(n, ct):
                act.wait_ge(conv_ready, n * 4 + ct + 1)
                if not (isinstance(n, int) and n == 0 and ct < 2):
                    act.wait_ge(silu_ready, n * 4 + ct - 1)
                act.activation(th[:, ct % 2], conv[:, ct], ACT.Tanh, scale=0.5).then_inc(th_ready, 1)

            for ct in range(4):
                act_silu(0, ct)

            def body(i, uses, with_next):
                if not isinstance(i, int):
                    act.wait_ge(o_step, 1 + i * 8)
                else:
                    act.wait_ge(o_step, 1 + i * 8)
                act.wait_ge(gates_ready, 3)
                src = gt[:].rearrange("p f t (d h) -> p (f t) d h", d=2)[:, :, :, bass.ds(2 * i, 2)] if not isinstance(i, int) \
                    else gt[:].rearrange("p f t (d h) -> p (f t) d h", d=2)[:, :, :, 2 * i:2 * i + 2]
                act.copy(gb[:], src).then_inc(gb_ready, 1)

                def decay(g):
                    bank = got(uses, f"D{g}", i)
                    act.wait_ge(o_step, 1 + i * 8)
                    act.activation(dec[:, g].rearrange("p t n -> p (t n)"), bank[:], ACT.Exp).then_inc(dec_ready, 1)

                decay(0)
                decay(1)
                for g in range(4):
                    eye = ident.rearrange("p (a n) -> p a n", a=1).to_broadcast([P, TT, P])
                    act.copy(T[:, g], eye).then_inc(eye_ready, 1)
                    act.copy(U[:, g], eye).then_inc(eye_ready, 1)
                for ct in range(2):
                    bank = got(uses, f"tr{ct}", i)
                    act.wait_ge(oss_ready, 1 + i)
                    act.activation(sq[:, ct], bank[:], ACT.Square).then_inc(sq_ready, 1)
                for h in range(2):
                    bank = got(uses, f"tr{2 + h}", i)
                    act.mul(v[:, h].rearrange("p t n -> p (t n)"), bank[:], 0.5).then_inc(v_ready, 1)
                decay(2)
                decay(3)
                for n in (1, 0):
                    name = "kT" if n else "qT"
                    bank = got(uses, name, i)
                    act.copy(kqT[:, n].rearrange("p t n -> p (t n)"), bank[:]).then_inc(kqT_ready, 1)
                if with_next:
                    for ct in range(4):
                        act_silu(i + 1, ct)

                def z_tanh(n):
                    bank = got(uses, f"z{n}", i)
                    act.wait_ge(oss_ready, 1 + i)
                    act.wait_ge(ss_ready, i + 1)
                    act.activation(sq[:, n], bank[:], ACT.Tanh, scale=0.5).then_inc(zt_ready, 1)

                for step in range(4):
                    for d in range(2):
                        tt = 3 - step if d else step
                        bank = got(uses, f"w{step}{d}", i)
                        if step < 3:
                            for h in range(2):
                                ins = act.mul(vs[:, d, h], bank[:, h * P:(h + 1) * P], gb[:, COEF * TT + tt, d, h:h + 1])
                            ins.then_inc(vs_ready, 1)
                        for h in range(2):
                            ins = act.mul(vn[:, d, h], bank[:, h * P:(h + 1) * P], gb[:, BETA * TT + tt, d, h:h + 1])
                        ins.then_inc(vn_ready, 1)
                    if step == 1:
                        z_tanh(0)
                    if step == 3:
                        z_tanh(1)

                act.wait_ge(o_step, 1 + i * 8 + 8)
                act.wait_ge(zs_ready, i * 2 + 2)
                act.activation(sq[:].rearrange("p a n -> p (a n)"), o[:].rearrange("p t h n -> p (t h n)"), ACT.Square).then_inc(osq_ready, 1)
                for h in range(2):
                    bank = got(uses, f"oT{h}", i)
                    act.wait_ge(y_ready, 1 + i * 8)
                    act.mul(oT[:, h].rearrange("p t n -> p (t n)"), bank[:], nw[:, 0:1]).then_inc(oT_ready, 1)

            with act.Fori(0, NK - 1) as i:
                body(i, MAIN, True)
            body(NK - 1, LAST, False)

        @block.gpsimd
        def _(pool):
            nc.gpsimd.memset(X[:], 0.0).then_inc(x_zero, 1)

            def body(i, uses):
                for g in range(4):
                    d, h = divmod(g, 2)
                    if g == 0:
                        pool.wait_ge(gb_ready, i + 1)
                    if g >= 2:
                        b, n = nth(uses, f"D{g - 2}", i)
                        pool.wait_ge(full[b], n + 1)
                    raw = gb[:, GRAW * TT:(GRAW + 1) * TT, d, h:h + 1].to_broadcast([P, TT, P])
                    nc.gpsimd.tensor_tensor(triG[:, g % 2], tri[d].rearrange("p (a n) -> p a n", a=1).to_broadcast([P, TT, P]), raw, ALU.mult).then_inc(triG_ready, 1)
                for g in range(4):
                    pool.wait_ge(at_ready, i * 4 + g + 1)
                    pool.wait_ge(mask_ready, i * 4 + 4)
                    nc.gpsimd.tensor_tensor(dec[:, g], dec[:, g], kqm[:, g // 2], ALU.mult).then_inc(qkd_ready, 1)

            with pool.Fori(0, NK - 1) as i:
                body(i, MAIN)
            body(NK - 1, LAST)

        @block.vector
        def _(dve):
            links = {"base": 0, "i": 0, "per": 0, "k": 0}

            def step(ins):
                links["k"] += 1
                ins.then_inc(link, 1)
                dve.wait_ge(link, links["base"] + links["i"] * links["per"] + links["k"])

            def got(uses, name, i):
                b, n = nth(uses, name, i)
                dve.wait_ge(full[b], n + 1)
                return ps[b]

            for signal in (y_ready, o_step, oss_ready):
                dve.sem_inc(signal, 1)
            def grid(a):
                return a.rearrange("p (a n) -> p a n", a=1).to_broadcast([P, TT, 2 * NV])

            dve.wait_ge(small_in, 64)
            dve.wait_ge(ba_ready, 1)
            step(nc.vector.tensor_tensor(tmp[:, 1], ba[:, :, 32:64], grid(bvec[:, 1]), ALU.add))
            step(nc.vector.scalar_tensor_tensor(out=tmp[:, 2].rearrange("p t g -> p (t g)"), in0=tmp[:, 1].rearrange("p t g -> p (t g)"), scalar=-1.0,
                                                in1=tmp[:, 1].rearrange("p t g -> p (t g)"), op0=ALU.mult, op1=ALU.min))
            nc.vector.tensor_scalar(tmp[:, 3], tmp[:, 1], 0.0, None, ALU.max).then_inc(gates_ready, 1)
            dve.wait_ge(beta_ready, 1)
            step(nc.vector.tensor_scalar(tmp[:, 0], tmp[:, 0], 1.0, None, ALU.add))
            step(nc.vector.reciprocal(gt[:, BETA], tmp[:, 0]))
            dve.wait_ge(beta_ready, 3)
            dve.wait_ge(gates_ready, 1)
            step(nc.vector.tensor_tensor(tmp[:, 2], tmp[:, 2], tmp[:, 3], ALU.add))
            nc.vector.scalar_tensor_tensor(out=gt[:, GRAW], in0=tmp[:, 2], scalar=-1.0, in1=grid(bvec[:, 0]), op0=ALU.mult, op1=ALU.mult).then_inc(raw_ready, 1)
            dve.wait_ge(full[3], 1)
            step(nc.vector.tensor_copy(tmp[:, 0].rearrange("p t g -> p (t g)"), ps[3][:, 0:P]))
            nc.vector.tensor_copy(tmp[:, 3].rearrange("p t g -> p (t g)"), ps[3][:, P:2 * P]).then_inc(dve_sums, 1)
            dve.wait_ge(dve_sums, 1)
            nc.vector.tensor_tensor(tmp[:, 1], tmp[:, 3], tmp[:, 0], ALU.subtract).then_inc(gates_ready, 1)
            dve.wait_ge(sums_ready, 3)
            nc.vector.tensor_scalar(gt[:, NEG_EG], gt[:, EG], -1.0, None, ALU.mult)
            nc.vector.tensor_tensor(gt[:, COEF], gt[:, BETA], tmp[:, 1], ALU.mult).then_inc(gates_ready, 1)
            for tt in range(TT):
                dve.wait_ge(xT_ready, 2 * tt + 2)
                step(nc.vector.tensor_scalar(res[:, tt], res[:, tt], ALPHA, None, ALU.mult))

            def convolve(uses, i, n, ct, first=False, taps_of=(2, 0, 1, 3, 4)):
                if 2 not in taps_of:
                    bank = ps[ct % 2]
                elif first:
                    b, k = F.at[f"proj{ct}"]
                    dve.wait_ge(full[b], k + 1)
                    bank = ps[b]
                else:
                    bank = got(uses, f"proj{ct}", i)
                    got(uses, f"tr{ct}", i)
                w = taps[:, ct]
                if 2 in taps_of:
                    dve.wait_ge(taps_ready, n + 1)
                    step(nc.vector.tensor_scalar(conv[:, ct], bank[:], w[:, 2:3], None, ALU.mult))
                for j in taps_of:
                    if j == 2:
                        continue
                    d = j - 2
                    lo, hi = max(0, -d), SEQ - max(0, d)
                    ins = nc.vector.scalar_tensor_tensor(out=conv[:, ct, lo:hi], in0=bank[:, lo + d:hi + d], scalar=w[:, j:j + 1], in1=conv[:, ct, lo:hi], op0=ALU.mult, op1=ALU.add)
                    if j == 4:
                        ins.then_inc(conv_ready, 1)
                    else:
                        step(ins)

            def silu(n, ct):
                dve.wait_ge(th_ready, n * 4 + ct + 1)
                nc.vector.scalar_tensor_tensor(out=conv[:, ct], in0=th[:, ct % 2], scalar=1.0, in1=conv[:, ct], op0=ALU.add, op1=ALU.mult).then_inc(silu_ready, 1)

            def tap_columns(bank):
                nc.vector.tensor_copy(taps[:].rearrange("p a b -> p (a b)"), bank[:, 0:4 * TAPS]).then_inc(taps_ready, 1)

            dve.wait_ge(full[2], 2)
            tap_columns(ps[2])
            for ct in range(4):
                convolve(None, 0, 0, ct, first=True)
                if ct:
                    silu(0, ct - 1)
            silu(0, 3)
            dve.wait_ge(x_zero, 1)

            def body(i, uses, with_next, per):
                links.update(i=i, per=per, k=0)
                if with_next:
                    tap_columns(got(uses, "taps", i))
                dve.wait_ge(sq_ready, i * 2 + 2)
                nc.vector.tensor_reduce(ss[:], sq[:].rearrange("p a (t n) -> p (a t) n", t=TT), AX.X, ALU.add).then_inc(ss_ready, 1)
                dve.wait_ge(ss_ready, i + 1)
                step(nc.vector.tensor_scalar(ss[:], ss[:], 4.0 * RMS_EPS, None, ALU.add))
                rsqrt(nc, step, rs[:], ss[:], nt[:])
                step(nc.vector.tensor_scalar(rs[:, 0:TT], rs[:, 0:TT], DH ** -0.5, None, ALU.mult))
                for n, ct in enumerate((1, 0)):
                    b = uses.at[f"tr{ct}"][0]
                    rb = rs[:, ct * TT:(ct + 1) * TT].rearrange("p (t a) -> p t a", a=1).to_broadcast([P, TT, P])
                    bank = ps[b][:].rearrange("p (t n) -> p t n", t=TT)
                    nc.vector.tensor_tensor(kq[:, ct], bank, rb, ALU.mult).then_inc(kq_ready, 1)
                jobs = []
                if with_next:
                    for ct in range(4):
                        for j in (2, 0, 1, 3, 4):
                            jobs.append(lambda ct=ct, j=j: convolve(uses, i, i + 1, ct, taps_of=(j,)))
                            if j == 2 and ct:
                                jobs.append(lambda ct=ct: silu(i + 1, ct - 1))
                    jobs.append(lambda: silu(i + 1, 3))

                bank = got(uses, "KK", i)
                for d in range(2):
                    m = before[d].rearrange("p (a n) -> p a n", a=1).to_broadcast([P, TT, P])
                    ins = nc.vector.tensor_tensor(kkm[:, d], bank[:].rearrange("p (t n) -> p t n", t=TT), m, ALU.mult)
                    ins.then_inc(mask_ready, 1)
                bank = got(uses, "KQ", i)
                for d in range(2):
                    m = tri[d].rearrange("p (a n) -> p a n", a=1).to_broadcast([P, TT, P])
                    ins = nc.vector.tensor_tensor(kqm[:, d], bank[:].rearrange("p (t n) -> p t n", t=TT), m, ALU.mult)
                    ins.then_inc(mask_ready, 1)
                dve.wait_ge(mask_ready, i * 4 + 2)
                for g in range(4):
                    d, h = divmod(g, 2)
                    dve.wait_ge(dec_ready, i * 4 + g + 1)
                    step(nc.vector.tensor_tensor(A[:, g], dec[:, g], kkm[:, d], ALU.mult))
                    beta = gb[:, BETA * TT:(BETA + 1) * TT, d, h:h + 1].to_broadcast([P, TT, P])
                    nc.vector.tensor_tensor(A[:, g], A[:, g], beta, ALU.mult).then_inc(at_ready, 1)

                dve.wait_ge(eye_ready, i * 8 + 8)

                def mask_x(n):
                    l, g = divmod(n, 4)
                    d = g // 2
                    b = 1 << l
                    bank = got(uses, f"X{l}{g}", i)
                    at = C_LEV + (d * LEVELS + l) * 64
                    m = c[:, at:at + 64].rearrange("p (o a) -> p o a", o=1).to_broadcast([P, TT, 64]).rearrange("p t (a b) -> p t a b", b=b)
                    xv = X[:, l, g % 2].rearrange("p t (a h b) -> p t a h b", h=2, b=b)[:, :, :, d, :]
                    nc.vector.tensor_tensor(xv, bank[:, 0:256].rearrange("p (t a b) -> p t a b", t=TT, b=b), m, ALU.mult).then_inc(xm_ready, 1)

                def update(n):
                    l, g = divmod(n, 4)
                    d = g // 2
                    b = 1 << l
                    bank = got(uses, f"U{l}{g}", i)
                    if l < LEVELS - 1:
                        Te = level(T[:, g].rearrange("p t n -> p (t n)"), d, l)
                        if l == 0:
                            x = level(X[:, l, g % 2].rearrange("p t n -> p (t n)"), d, l)
                        else:
                            x = bank[:, 0:256].rearrange("p (a b) -> p a b", b=b)
                        nc.vector.tensor_tensor(Te, Te, x, ALU.subtract).then_inc(link, 1)
                        links["k"] += 1
                    Uo = level(U[:, g].rearrange("p t n -> p (t n)"), d, l, 1)
                    nc.vector.tensor_tensor(Uo, Uo, bank[:, 256:512].rearrange("p (a b) -> p a b", b=b), ALU.subtract).then_inc(upd_ready, 1)

                for n in range(LEVELS * 4 + 2):
                    if n >= 2:
                        update(n - 2)
                    if n < LEVELS * 4:
                        mask_x(n)
                    if jobs:
                        jobs.pop(0)()
                while jobs:
                    jobs.pop(0)()

                def z_silu(n):
                    dve.wait_ge(zt_ready, i * 2 + n + 1)
                    b = uses.at[f"z{n}"][0]
                    flat = zs[:, 2 * n:2 * n + 2].rearrange("p t h n -> p (t h n)")
                    nc.vector.scalar_tensor_tensor(out=flat, in0=sq[:, n], scalar=1.0, in1=ps[b][:], op0=ALU.add, op1=ALU.mult).then_inc(zs_ready, 1)

                for st in range(4):
                    for d in range(2):
                        tt = 3 - st if d else st
                        if st:
                            bank = got(uses, f"kq{st}{d}", i)
                            for h in range(2):
                                ins = nc.vector.scalar_tensor_tensor(out=r[:, d, h], in0=bank[:, h * P:(h + 1) * P], scalar=gb[:, NEG_EG * TT + tt, d, h:h + 1],
                                                                     in1=v[:, h, tt], op0=ALU.mult, op1=ALU.add)
                            ins.then_inc(r_ready, 1)
                            if st >= 2:
                                dve.wait_ge(o_step, 1 + i * 8 + st * 2)
                            for h in range(2):
                                q = bank[:, 256 + h * P:256 + (h + 1) * P]
                                e = gb[:, EG * TT + tt, d, h:h + 1]
                                if st < 2:
                                    ins = nc.vector.tensor_scalar(o[:, tt, h], q, e, None, ALU.mult)
                                else:
                                    ins = nc.vector.scalar_tensor_tensor(out=o[:, tt, h], in0=q, scalar=e, in1=o[:, tt, h], op0=ALU.mult, op1=ALU.add)
                            ins.then_inc(oq_ready, 1)
                    for d in range(2):
                        tt = 3 - st if d else st
                        bank = got(uses, f"os{st}{d}", i)
                        if 0 < st < 3:
                            dve.wait_ge(S_ready, i * 6 + (st - 1) * 2 + d + 1)
                        if st < 3:
                            for h in range(2):
                                if st == 0:
                                    ins = nc.vector.tensor_copy(St[:, d, h], bank[:, 256 + h * P:256 + (h + 1) * P])
                                else:
                                    ins = nc.vector.scalar_tensor_tensor(out=St[:, d, h], in0=St[:, d, h], scalar=gb[:, EGL * TT + tt, d, h:h + 1],
                                                                         in1=bank[:, 256 + h * P:256 + (h + 1) * P], op0=ALU.mult, op1=ALU.add)
                            ins.then_inc(S_ready, 1)
                        flat = o[:, tt].rearrange("p h n -> p (h n)")
                        if st:
                            dve.wait_ge(oq_ready, i * 6 + (st - 1) * 2 + d + 1)
                        if st == 0:
                            ins = nc.vector.tensor_copy(flat, bank[:, 0:256])
                        else:
                            ins = nc.vector.tensor_tensor(flat, flat, bank[:, 0:256], ALU.add)
                        ins.then_inc(o_step, 1)
                    if st == 1:
                        z_silu(0)
                z_silu(1)

                dve.wait_ge(osq_ready, i + 1)
                nc.vector.tensor_reduce(ss[:], sq[:].rearrange("p a (t n) -> p (a t) n", n=P), AX.X, ALU.add).then_inc(oss_ready, 1)
                dve.wait_ge(oss_ready, 1 + i + 1)
                step(nc.vector.tensor_scalar(ss[:], ss[:], 4.0 / DH, 4.0 * RMS_EPS, ALU.mult, ALU.add))
                rsqrt(nc, step, rs[:], ss[:], nt[:])
                rb = rs[:].rearrange("p (t a) -> p t a", a=1).to_broadcast([P, 8, P])
                o8 = o[:].rearrange("p t h n -> p (t h) n")
                step(nc.vector.tensor_tensor(o8, o8, rb, ALU.mult))
                nc.vector.tensor_tensor(o8, o8, zs[:].rearrange("p t h n -> p (t h) n"), ALU.mult).then_inc(og_ready, 1)
                for n in range(8):
                    tt, half = n // 2, n % 2
                    bank = got(uses, f"y{n}", i)
                    y = res[:, tt, half * 512:(half + 1) * 512]
                    nc.vector.tensor_tensor(y, y, bank[:], ALU.add).then_inc(y_ready, 1)
                if with_next:
                    assert links["k"] == per, links["k"]

            links["base"] = links["k"]
            per = DN_DVE_STEPS
            with dve.Fori(0, NK - 1) as i:
                body(i, MAIN, True, per)
            body(NK - 1, LAST, False, per)


DN_DVE_STEPS = 4 * 4 + 1 + 4 + 24 + 1 + 2 + 2 * RSQRT_STEPS


class Steps:

    def __init__(self, dve, link):
        self.dve, self.link, self.k = dve, link, 0

    def __call__(self, ins):
        self.k += 1
        ins.then_inc(self.link, 1)
        self.dve.wait_ge(self.link, self.k)


def norm(nc, t, dram, gname, bname, layer, name, routed=True, out=None):
    c, ps, res, xT = t["const"], t["ps"], t["res"], t["xT"]
    ident = c[:, C_ID:C_ID + P]
    with ExitStack() as ctx:
        def sb(n, shape):
            return ctx.enter_context(nc.sbuf_tensor(f"{name}_{n}", shape, F32))

        sem = phase(nc, ctx, name + "_")

        g, b = sb("g", [P, D]), sb("b", [P, D])
        stats, mv = sb("stats", [P, TT, 2, 6]), sb("mv", [P, TT, 2])
        var, rstd, shift, nt = (sb(n, [P, TT]) for n in ("var", "rstd", "shift", "nt"))
        rows_in, stats_ready, scale_ready, scaled, normed, turned, xT_ready, stored, link = (
            sem(n) for n in ("rows_in", "stats_ready", "scale_ready", "scaled", "normed", "turned", "xT_ready", "stored", "link"))
        if routed:
            rw, rb = sb("rw", [P, KD, 16]), sb("rb", [P, 16])
            s, sel, e, w, chosen = (sb(n, [P, TT, 16]) for n in ("s", "sel", "e", "w", "chosen"))
            beat, tie = sb("beat", [P, 16, 4, 4]), sb("tie", [P, 16, 4, 4])
            cnt = sb("cnt", [P, 64])
            gs, gcnt, total = sb("gs", [P, TT, 4]), sb("gcnt", [P, 16]), sb("total", [P, TT])
            router_in, logits, e_ready = sem("router_in"), sem("logits"), sem("e_ready")
        block = ctx.enter_context(nc.Block())

        @block.sync
        def _(sp):
            sp.dma_start(g[:], dram[gname][layer].partition_broadcast(P)).then_inc(rows_in, 16)
            sp.dma_start(b[:], dram[bname][layer].partition_broadcast(P)).then_inc(rows_in, 16)
            if routed:
                sp.dma_start(rw[:], dram["router_w"].rearrange("(k p) e -> p k e", p=P)).then_inc(router_in, 16)
                sp.dma_start(rb[:], dram["router_bias"].partition_broadcast(P)).then_inc(router_in, 16)
            if out is not None:
                for tt in range(TT):
                    sp.wait_ge(normed, tt + 1)
                    sp.dma_start(out[0, tt * P:(tt + 1) * P], res[:, tt]).then_inc(stored, 16)
                sp.wait_ge(stored, 16 * TT)

        @block.scalar
        def _(act):
            for tt in range(TT):
                act.wait_ge(scale_ready, 1)
                act.activation(res[:, tt], res[:, tt], ACT.Identity, scale=rstd[:, tt:tt + 1], bias=shift[:, tt:tt + 1]).then_inc(scaled, 1)
            if out is None:
                for n in range(8):
                    tt, half = n // 2, n % 2
                    act.wait_ge(turned, n + 1)
                    act.copy(xT[:, half * 4:half * 4 + 4, tt * P:(tt + 1) * P], ps[n % 4][:].rearrange("p (k n) -> p k n", k=4)).then_inc(xT_ready, 1)
            if routed:
                act.wait_ge(logits, 1)
                act.activation(e[:].rearrange("p t e -> p (t e)"), ps[4][:, 0:64], ACT.Exp, scale=-1.0).then_inc(e_ready, 1)

        if out is None:
            @block.tensor
            def _(pe):
                for n in range(8):
                    tt, half = n // 2, n % 2
                    pe.wait_ge(normed, tt + 1)
                    if n >= 4:
                        pe.wait_ge(xT_ready, n - 3)
                    for k in range(4):
                        mm = pe.transpose(ps[n % 4][:, k * P:(k + 1) * P], res[:, tt, (half * 4 + k) * P:(half * 4 + k + 1) * P], ident)
                    mm.then_inc(turned, 1)
                if not routed:
                    return
                pe.wait_ge(router_in, 32)
                for tt in range(TT):
                    pe.wait_ge(xT_ready, 2 * tt + 2)
                    for k in range(KD):
                        mm = pe.matmul(ps[4][:, tt * 16:(tt + 1) * 16], xT[:, k, tt * P:(tt + 1) * P], rw[:, k], start=k == 0, stop=k == KD - 1)
                mm.then_inc(logits, 1)

        @block.vector
        def _(dve):
            step = Steps(dve, link)
            for tt in range(TT):
                for h in range(2):
                    ins = nc.vector.bn_stats(stats[:, tt, h], res[:, tt, h * 512:(h + 1) * 512])
                step(ins)
                ins = nc.vector.bn_aggr(mv[:, tt], stats[:, tt].rearrange("p h s -> p (h s)"))
            step(ins)
            step(nc.vector.tensor_scalar(var[:], mv[:, :, 1], LN_EPS, None, ALU.add))
            rsqrt(nc, step, rstd[:], var[:], nt[:])
            nc.vector.scalar_tensor_tensor(out=shift[:], in0=mv[:, :, 0], scalar=-1.0, in1=rstd[:], op0=ALU.mult, op1=ALU.mult).then_inc(scale_ready, 1)
            dve.wait_ge(rows_in, 32)
            for tt in range(TT):
                dve.wait_ge(scaled, tt + 1)
                step(nc.vector.tensor_tensor(res[:, tt], res[:, tt], g[:], ALU.mult))
                nc.vector.tensor_tensor(res[:, tt], res[:, tt], b[:], ALU.add).then_inc(normed, 1)
            if out is not None:
                return
            for tt in range(TT):
                dve.wait_ge(turned, 2 * tt + 2)
                dve.wait_ge(normed, tt + 1)
                step(nc.vector.tensor_scalar(res[:, tt], res[:, tt], ALPHA, None, ALU.mult))
            if not routed:
                return
            dve.wait_ge(e_ready, 1)
            dve.wait_ge(router_in, 32)
            step(nc.vector.tensor_scalar(e[:], e[:], 1.0, None, ALU.add))
            step(nc.vector.reciprocal(s[:], e[:]))
            step(nc.vector.tensor_tensor(sel[:], s[:], rb[:].rearrange("p (a e) -> p a e", a=1).to_broadcast([P, TT, 16]), ALU.add))

            def losses(values, n, count):
                one = values.rearrange("p (g a j) -> p g a j", a=1, j=4).to_broadcast([P, n, 4, 4])
                other = values.rearrange("p (g i a) -> p g i a", i=4, a=1).to_broadcast([P, n, 4, 4])
                flat = lambda a: a[:, 0:n].rearrange("p g i j -> p (g i) j")
                step(nc.vector.tensor_tensor(beat[:, 0:n], one, other, ALU.is_gt))
                step(nc.vector.tensor_tensor(tie[:, 0:n], one, other, ALU.is_equal))
                lower = c[:, C_JLT:C_JLT + 16].rearrange("p (a i) -> p a i", a=1).to_broadcast([P, n, 16])
                tied = tie[:, 0:n].rearrange("p g i j -> p g (i j)")
                step(nc.vector.tensor_tensor(tied, tied, lower, ALU.mult))
                step(nc.vector.tensor_tensor(beat[:, 0:n], beat[:, 0:n], tie[:, 0:n], ALU.add))
                step(nc.vector.tensor_reduce(count, flat(beat), AX.X, ALU.add))

            ch = chosen[:].rearrange("p t e -> p (t e)")
            losses(sel[:].rearrange("p t e -> p (t e)"), 16, cnt[:])
            step(nc.vector.tensor_scalar(ch, cnt[:], 2.0, None, ALU.is_lt))
            step(nc.vector.tensor_tensor(w[:], chosen[:], sel[:], ALU.mult))
            step(nc.vector.tensor_reduce(gs[:].rearrange("p t g -> p (t g)"), w[:].rearrange("p t (g e) -> p (t g) e", e=4), AX.X, ALU.add))
            losses(gs[:].rearrange("p t g -> p (t g)"), 4, gcnt[:])
            step(nc.vector.tensor_scalar(gcnt[:], gcnt[:], 1.0, None, ALU.is_lt))
            step(nc.vector.tensor_tensor(chosen[:].rearrange("p t (g e) -> p (t g) e", e=4), chosen[:].rearrange("p t (g e) -> p (t g) e", e=4),
                                         gcnt[:].rearrange("p (g a) -> p g a", a=1).to_broadcast([P, 16, 4]), ALU.mult))
            step(nc.vector.tensor_tensor(w[:], chosen[:], s[:], ALU.mult))
            step(nc.vector.tensor_reduce(total[:], w[:], AX.X, ALU.add))
            step(nc.vector.reciprocal(total[:], total[:]))
            step(nc.vector.tensor_tensor(t["gates"][:], w[:], total[:].rearrange("p (t a) -> p t a", a=1).to_broadcast([P, TT, 16]), ALU.mult))


NE, FF = 16, 256


def experts(nc, t, dram, layer, name):
    ps, res, xT, gates = t["ps"], t["res"], t["xT"], t["gates"]
    with ExitStack() as ctx:
        def sb(n, shape):
            return ctx.enter_context(nc.sbuf_tensor(f"{name}_{n}", shape, F32))

        sem = phase(nc, ctx, name + "_")

        wg, wu, wd = sb("wg", [P, 2, KD, FF]), sb("wu", [P, 2, KD, FF]), sb("wd", [P, 2, 2, D])
        silu, hid = sb("silu", [P, 2, SEQ]), sb("hid", [P, 2, SEQ])
        gu_in, d_in = [sem("gu_in0"), sem("gu_in1")], [sem("d_in0"), sem("d_in1")]
        gate_full, up_full, silu_ready, hid_ready, down_full, y_ready = (sem(n) for n in ("gate_full", "up_full", "silu_ready", "hid_ready", "down_full", "y_ready"))
        block = ctx.enter_context(nc.Block())
        g_dram, u_dram, d_dram = (dram[n][layer] for n in ("moe_w_gate", "moe_w_up", "moe_w_down"))
        g_dram = g_dram.rearrange("e (k p) f -> p e k f", p=P)
        u_dram = u_dram.rearrange("e (k p) f -> p e k f", p=P)
        d_dram = d_dram.rearrange("e (k p) n -> p e k n", p=P)

        def pick(a, e):
            return a[:, e] if isinstance(e, int) else a[:, bass.ds(e, 1)].rearrange("p a k f -> p (a k) f")

        @block.sync
        def _(sp):
            def load(e, slot, used):
                if used:
                    sp.wait_ge(hid_ready, 1 + 2 * e - 2)
                sp.dma_start(wg[:, slot], pick(g_dram, e)).then_inc(gu_in[slot], 16)
                sp.dma_start(wu[:, slot], pick(u_dram, e)).then_inc(gu_in[slot], 16)
                if used:
                    sp.wait_ge(y_ready, 1 + 8 * e - 8)
                sp.dma_start(wd[:, slot], pick(d_dram, e)).then_inc(d_in[slot], 16)
            load(0, 0, False)
            load(1, 1, False)
            with sp.Fori(1, NE // 2) as pair:
                for slot in range(2):
                    load(2 * pair + slot, slot, True)

        @block.tensor
        def _(pe):
            with pe.Fori(0, NE // 2) as pair:
                for slot in range(2):
                    e = 2 * pair + slot
                    pe.wait_ge(gu_in[slot], (pair + 1) * 32)
                    for f in range(2):
                        pe.wait_ge(hid_ready, 1 + 2 * e)
                        for w, bank, signal in ((wg, ps[f], gate_full), (wu, ps[2 + f], up_full)):
                            for k in range(KD):
                                mm = pe.matmul(bank[:], w[:, slot, k, f * P:(f + 1) * P], xT[:, k], start=k == 0, stop=k == KD - 1)
                            mm.then_inc(signal, 1)
                    pe.wait_ge(d_in[slot], (pair + 1) * 16)
                    pe.wait_ge(hid_ready, 1 + 2 * e + 2)
                    for n in range(8):
                        tt, half = n // 2, n % 2
                        if n >= 4:
                            pe.wait_ge(y_ready, 1 + 8 * e + n - 3)
                        else:
                            pe.wait_ge(y_ready, 1 + 8 * e)
                        for f in range(2):
                            mm = pe.matmul(ps[4 + n % 4][:], hid[:, f, tt * P:(tt + 1) * P], wd[:, slot, f, half * 512:(half + 1) * 512], start=f == 0, stop=f == 1)
                        mm.then_inc(down_full, 1)

        @block.scalar
        def _(act):
            with act.Fori(0, NE) as e:
                for f in range(2):
                    act.wait_ge(gate_full, 2 * e + f + 1)
                    act.activation(silu[:, f], ps[f][:], ACT.Silu).then_inc(silu_ready, 1)

        @block.vector
        def _(dve):
            for signal in (hid_ready, y_ready):
                dve.sem_inc(signal, 1)
            with dve.Fori(0, NE) as e:
                for f in range(2):
                    dve.wait_ge(silu_ready, 2 * e + f + 1)
                    dve.wait_ge(up_full, 2 * e + f + 1)
                    nc.vector.tensor_tensor(hid[:, f], silu[:, f], ps[2 + f][:], ALU.mult).then_inc(hid_ready, 1)
                for n in range(8):
                    tt, half = n // 2, n % 2
                    dve.wait_ge(down_full, 8 * e + n + 1)
                    y = res[:, tt, half * 512:(half + 1) * 512]
                    gate = gates[:, tt, bass.ds(e, 1)]
                    nc.vector.scalar_tensor_tensor(out=y, in0=ps[4 + n % 4][:], scalar=gate, in1=y, op0=ALU.mult, op1=ALU.add).then_inc(y_ready, 1)


NH, NOPE, ROPE, QR, KVR = 8, 128, 64, 384, 256
KQ_, KKV = QR // P, KVR // P


def mla_uses(first):
    names = [("qr", 0), ("qn", 1), ("kn", 2), ("v", 3), ("qrT", 0)] + [(f"S{n}", 4 + n) for n in range(4)]
    if not first:
        names += [(f"y{n}", n % 4) for n in range(8)]
    return Uses(names + [(f"T{n}", n) for n in range(4)] + [("pv", 4)])


def latent_attention(nc, t, dram):
    c, ps, res, xT = t["const"], t["ps"], t["res"], t["xT"]
    ident = c[:, C_ID:C_ID + P]
    FIRST, MAIN = mla_uses(True), mla_uses(False)
    scale = (NOPE + ROPE) ** -0.5
    with ExitStack() as ctx:
        def sb(n, shape, dt=F32):
            return ctx.enter_context(nc.sbuf_tensor(f"mla_{n}", shape, dt))

        sem = phase(nc, ctx, "mla_")

        W = QR + KVR + ROPE
        w_in, h = sb("win", [P, KD, W]), sb("h", [P, TT, W])
        junk = sb("junk", [P, QR])
        pos_i, pos = sb("pos_i", [P, TT], mybir.dt.int32), sb("pos", [P, TT])
        ang, turns, sin, cos = (sb(n, [P, TT, 32]) for n in ("ang", "turns", "sin", "cos"))
        ss, rs, nt = (sb(n, [P, 2 * TT]) for n in ("ss", "rs", "nt"))
        qw, kvw = sb("qw", [P, KQ_]), sb("kvw", [P, KKV])
        cqT, ckvT, krT = sb("cqT", [P, KQ_, SEQ]), sb("ckvT", [P, KKV, SEQ]), sb("krT", [P, SEQ])
        kr = sb("kr", [P, TT, 2, ROPE])
        rt = sb("rt", [P, 4, TT, 32])
        wq, wkv, wo = sb("wq", [P, KQ_, NOPE + ROPE]), sb("wkv", [P, KKV, 2 * P]), sb("wo", [P, D])
        qnT, knT, v = sb("qnT", [P, SEQ]), sb("knT", [P, SEQ]), sb("v", [P, TT, P])
        qr, qrT = sb("qr", [P, TT, ROPE]), sb("qrT", [P, 2, P])
        mx, nb, sums, inv = (sb(n, [P, TT]) for n in ("mx", "nb", "sums", "inv"))
        p, pT, oT = sb("p", [P, TT, SEQ]), sb("pT", [P, TT, SEQ]), sb("oT", [P, SEQ])

        full = [sem(f"full{b}") for b in range(8)]
        w_loaded, small_in = sem("w_loaded"), sem("small_in")
        wq_in, wkv_in, wo_in = sem("wq_in"), sem("wkv_in"), sem("wo_in")
        h_full, h_ready, sq_ready, norm_ready, kr_ready, cT_full, cT_ready, krT_ready = (
            sem(n) for n in ("h_full", "h_ready", "sq_ready", "norm_ready", "kr_ready", "cT_full", "cT_ready", "krT_ready"))
        ang_ready, trig_ready, link = sem("ang_ready"), sem("trig_ready"), sem("link")
        rope_read, qr_ready, qrT_ready, kv_ready, nb_ready, p_ready, pn_ready, oT_ready, y_ready = (
            sem(n) for n in ("rope_read", "qr_ready", "qrT_ready", "kv_ready", "nb_ready", "p_ready", "pn_ready", "oT_ready", "y_ready"))
        pT_ready = [sem("pT_ready_act"), sem("pT_ready_dve")]
        block = ctx.enter_context(nc.Block())

        base = {b: FIRST.per[b] - MAIN.per[b] for b in range(8)}

        def nth(uses, name, i):
            b, k = uses.at[name]
            return b, (k if isinstance(i, int) and i == 0 else base[b] + i * MAIN.per[b] + k)

        def read_of(name, i):
            n = int(name[-1]) if name[-1].isdigit() else 0
            if name[0] == "S":
                return p_ready, 4 * i + n + 1
            if name[0] == "T":
                return pT_ready[n % 2], 2 * i + n // 2 + 1
            if name[0] == "y":
                return y_ready, 1 + 8 * (i - 1) + n + 1
            return {"qr": (rope_read, i + 1), "qn": (kv_ready, 3 * i + 1), "kn": (kv_ready, 3 * i + 2), "v": (kv_ready, 3 * i + 3),
                    "qrT": (qrT_ready, i + 1), "pv": (oT_ready, i + 1)}[name]

        last_read = {b: (pT_ready[b % 2], 2) for b in range(4)} | {4: (oT_ready, 1)} | {b: (p_ready, 4) for b in (5, 6, 7)}

        def rotate(step, out, x, last):
            a, b = x[:, :, 0:32], x[:, :, 32:64]
            step(nc.vector.tensor_tensor(rt[:, 0], a, cos[:], ALU.mult))
            step(nc.vector.tensor_tensor(rt[:, 1], b, sin[:], ALU.mult))
            step(nc.vector.tensor_tensor(rt[:, 2], b, cos[:], ALU.mult))
            last(nc.vector.tensor_tensor(rt[:, 3], a, sin[:], ALU.mult))
            step(nc.vector.tensor_tensor(out[:, :, 0:32], rt[:, 0], rt[:, 1], ALU.subtract))
            return nc.vector.tensor_tensor(out[:, :, 32:64], rt[:, 2], rt[:, 3], ALU.add)

        @block.sync
        def _(sp):
            src = dram["mla_w_in"][0].rearrange("(k p) n -> p k n", p=P)
            sp.dma_start(w_in[:], src).then_inc(w_loaded, 16)
            sp.dma_start(pos_i[:], dram["positions"][0].rearrange("(t p) -> p t", p=P), allow_slow_non_contiguous=True).then_inc(small_in, 16)
            sp.dma_start(qw[:], dram["mla_q_norm"][0].rearrange("(k p) -> p k", p=P), allow_slow_non_contiguous=True).then_inc(small_in, 16)
            sp.dma_start(kvw[:], dram["mla_kv_norm"][0].rearrange("(k p) -> p k", p=P), allow_slow_non_contiguous=True).then_inc(small_in, 16)
            q_dram = dram["mla_w_qb"][0].rearrange("(k p) n -> p k n", p=P)
            kv_dram = dram["mla_w_kvb"][0].rearrange("(k p) n -> p k n", p=P)
            o_dram = dram["mla_w_out"][0]

            def load(i):
                if isinstance(i, int):
                    q, kv, o = q_dram[:, :, 0:192], kv_dram[:, :, 0:256], o_dram[0:P]
                else:
                    q, kv, o = q_dram[:, :, bass.ds(i * 192, 192)], kv_dram[:, :, bass.ds(i * 256, 256)], o_dram[bass.ds(i * P, P)]
                    sp.wait_ge(kv_ready, 3 * i)
                    sp.wait_ge(qrT_ready, i)
                sp.dma_start(wq[:], q).then_inc(wq_in, 16)
                sp.dma_start(wkv[:], kv).then_inc(wkv_in, 16)
                if not isinstance(i, int):
                    sp.wait_ge(y_ready, 1 + 8 * i)
                sp.dma_start(wo[:], o).then_inc(wo_in, 16)

            load(0)
            with sp.Fori(1, NH) as i:
                load(i)

        @block.tensor
        def _(pe):
            pe.wait_ge(w_loaded, 16)
            for tt in range(TT):
                for half in range(2):
                    for k in range(KD):
                        mm = pe.matmul(ps[2 * tt + half][:, 0:352], xT[:, k, tt * P:(tt + 1) * P], w_in[:, k, half * 352:(half + 1) * 352], start=k == 0, stop=k == KD - 1)
                mm.then_inc(h_full, 1)
            pe.wait_ge(h_ready, TT)
            for tt in range(TT):
                pe.wait_ge(norm_ready, tt + 1)
                if tt:
                    pe.wait_ge(cT_ready, 2 * tt)
                for k in range(KQ_):
                    mm = pe.transpose(ps[0][:, k * P:(k + 1) * P], h[:, tt, k * P:(k + 1) * P], ident)
                mm.then_inc(cT_full, 1)
                for k in range(KKV):
                    mm = pe.transpose(ps[1][:, k * P:(k + 1) * P], h[:, tt, QR + k * P:QR + (k + 1) * P], ident)
                mm.then_inc(cT_full, 1)
            pe.wait_ge(kr_ready, 1)
            for tt in range(TT):
                mm = pe.transpose(ps[2][:, tt * P:(tt + 1) * P], kr[:, tt].rearrange("p a n -> p (a n)"), ident)
            mm.then_inc(cT_full, 1)
            pe.wait_ge(cT_ready, 2 * TT)
            pe.wait_ge(krT_ready, 1)

            def body(i, uses, first):
                def begin(name):
                    b, k = uses.at[name]
                    if k:
                        pe.wait_ge(*read_of(uses.before[name], i))
                    elif not first:
                        signal, per = last_read[b]
                        pe.wait_ge(signal, i * per)
                    return ps[b]

                def done(mm, name):
                    mm.then_inc(full[uses.at[name][0]], 1)

                pe.wait_ge(wq_in, (i + 1) * 16)
                bank = begin("qr")
                for tt in range(TT):
                    for k in range(KQ_):
                        mm = pe.matmul(bank[:, tt * 64:(tt + 1) * 64], cqT[:, k, tt * P:(tt + 1) * P], wq[:, k, NOPE:NOPE + ROPE], start=k == 0, stop=k == KQ_ - 1)
                done(mm, "qr")
                bank = begin("qn")
                for k in range(KQ_):
                    mm = pe.matmul(bank[:], wq[:, k, 0:NOPE], cqT[:, k], start=k == 0, stop=k == KQ_ - 1)
                done(mm, "qn")
                pe.wait_ge(wkv_in, (i + 1) * 16)
                bank = begin("kn")
                for k in range(KKV):
                    mm = pe.matmul(bank[:], wkv[:, k, 0:P], ckvT[:, k], start=k == 0, stop=k == KKV - 1)
                done(mm, "kn")
                bank = begin("v")
                for tt in range(TT):
                    for k in range(KKV):
                        mm = pe.matmul(bank[:, tt * P:(tt + 1) * P], ckvT[:, k, tt * P:(tt + 1) * P], wkv[:, k, P:2 * P], start=k == 0, stop=k == KKV - 1)
                done(mm, "v")
                pe.wait_ge(qr_ready, i + 1)
                bank = begin("qrT")
                for n in range(2):
                    mm = pe.transpose(bank[:, n * P:(n + 1) * P], qr[:, 2 * n:2 * n + 2].rearrange("p a n -> p (a n)"), ident)
                done(mm, "qrT")
                pe.wait_ge(kv_ready, 3 * i + 2)
                pe.wait_ge(qrT_ready, i + 1)
                for n in range(TT):
                    bank = begin(f"S{n}")
                    pe.matmul(bank[:], qnT[:, n * P:(n + 1) * P], knT[:], start=True, stop=False)
                    half = slice(ROPE * (n % 2), ROPE * (n % 2) + ROPE)
                    done(pe.matmul(bank[:], qrT[half, n // 2], krT[half], start=False, stop=True), f"S{n}")
                if not first:
                    pe.wait_ge(wo_in, i * 16)
                    output(begin, done, i)
                for n in range(TT):
                    pe.wait_ge(pn_ready, 4 * i + n + 1)
                    bank = begin(f"T{n}")
                    for k in range(TT):
                        mm = pe.transpose(bank[:, k * P:(k + 1) * P], p[:, n, k * P:(k + 1) * P], ident)
                    done(mm, f"T{n}")
                for n in range(2):
                    pe.wait_ge(pT_ready[n], 2 * i + 2)
                pe.wait_ge(kv_ready, 3 * i + 3)
                bank = begin("pv")
                for k in range(TT):
                    mm = pe.matmul(bank[:], v[:, k], pT[:, k], start=k == 0, stop=k == TT - 1)
                done(mm, "pv")

            def output(begin, done, i):
                pe.wait_ge(oT_ready, i)
                for n in range(8):
                    tt, half = n // 2, n % 2
                    done(pe.matmul(begin(f"y{n}")[:], oT[:, tt * P:(tt + 1) * P], wo[:, half * 512:(half + 1) * 512], start=True, stop=True), f"y{n}")

            body(0, FIRST, True)
            with pe.Fori(1, NH) as i:
                body(i, MAIN, False)
            pe.wait_ge(wo_in, NH * 16)
            pe.wait_ge(oT_ready, NH)
            for n in range(8):
                tt, half = n // 2, n % 2
                if n >= 4:
                    pe.wait_ge(y_ready, 1 + 8 * (NH - 1) + n - 3)
                else:
                    pe.wait_ge(pT_ready[n % 2], 2 * NH)
                pe.matmul(ps[n % 4][:], oT[:, tt * P:(tt + 1) * P], wo[:, half * 512:(half + 1) * 512], start=True, stop=True).then_inc(full[n % 4], 1)

        @block.scalar
        def _(act):
            act.wait_ge(ang_ready, 1)
            act.activation(sin[:], ang[:], ACT.Sin).then_inc(trig_ready, 1)
            act.activation(cos[:], turns[:], ACT.Sin).then_inc(trig_ready, 1)
            for tt in range(TT):
                act.wait_ge(h_full, tt + 1)
                for half in range(2):
                    ins = act.copy(h[:, tt, half * 352:(half + 1) * 352], ps[2 * tt + half][:, 0:352])
                ins.then_inc(h_ready, 1)
                act.wait_ge(h_ready, tt + 1)
                act.activation(junk[:], h[:, tt, 0:QR], ACT.Square, accum_out=ss[:, tt:tt + 1]).then_inc(sq_ready, 1)
                act.wait_ge(sq_ready, 2 * tt + 1)
                act.activation(junk[:, 0:KVR], h[:, tt, QR:QR + KVR], ACT.Square, accum_out=ss[:, TT + tt:TT + tt + 1]).then_inc(sq_ready, 1)
                act.wait_ge(sq_ready, 2 * tt + 2)
            act.wait_ge(small_in, 48)
            for tt in range(TT):
                act.wait_ge(cT_full, 2 * tt + 1)
                for k in range(KQ_):
                    ins = act.mul(cqT[:, k, tt * P:(tt + 1) * P], ps[0][:, k * P:(k + 1) * P], qw[:, k:k + 1])
                ins.then_inc(cT_ready, 1)
                act.wait_ge(cT_full, 2 * tt + 2)
                for k in range(KKV):
                    ins = act.mul(ckvT[:, k, tt * P:(tt + 1) * P], ps[1][:, k * P:(k + 1) * P], kvw[:, k:k + 1])
                ins.then_inc(cT_ready, 1)
            act.wait_ge(cT_full, 2 * TT + 1)
            act.copy(krT[:], ps[2][:]).then_inc(krT_ready, 1)

            pre = {0: 0}

            def body(i, uses):
                def got(name):
                    b, n = nth(uses, name, i)
                    act.wait_ge(full[b], n + 1)
                    return ps[b]

                act.copy(qnT[:], got("qn")[:]).then_inc(kv_ready, 1)
                act.copy(knT[:], got("kn")[:]).then_inc(kv_ready, 1)
                act.copy(v[:].rearrange("p t n -> p (t n)"), got("v")[:]).then_inc(kv_ready, 1)
                for n in range(TT):
                    act.wait_ge(nb_ready, 4 * i + n + 1)
                    bank = ps[4 + n]
                    act.activation(p[:, n], bank[:], ACT.Exp, scale=scale, bias=nb[:, n:n + 1], accum_out=sums[:, n:n + 1]).then_inc(p_ready, 1)
                for n in (0, 2):
                    bank = got(f"T{n}")
                    act.copy(pT[:, :, n * P:(n + 1) * P], bank[:].rearrange("p (k n) -> p k n", k=TT)).then_inc(pT_ready[0], 1)
                act.copy(oT[:], got("pv")[:]).then_inc(oT_ready, 1)

            body(0, FIRST)
            with act.Fori(1, NH) as i:
                body(i, MAIN)

        @block.vector
        def _(dve):
            state = {"base": 0, "i": 0, "per": 0, "k": 0}

            def step(ins):
                state["k"] += 1
                ins.then_inc(link, 1)
                dve.wait_ge(link, state["base"] + state["i"] * state["per"] + state["k"])

            dve.sem_inc(y_ready, 1)
            dve.wait_ge(small_in, 48)
            step(nc.vector.tensor_copy(pos[:], pos_i[:]))
            step(nc.vector.tensor_tensor(ang[:], pos[:].rearrange("p (t a) -> p t a", a=1).to_broadcast([P, TT, 32]),
                                         c[:, C_FREQ:C_FREQ + 32].rearrange("p (a f) -> p a f", a=1).to_broadcast([P, TT, 32]), ALU.mult))
            big = 12582912.0
            step(nc.vector.tensor_scalar(turns[:], ang[:], float(1 / (2 * np.pi)), big, ALU.mult, ALU.add))
            step(nc.vector.tensor_scalar(turns[:], turns[:], big, None, ALU.subtract))
            for part in TWO_PI:
                step(nc.vector.scalar_tensor_tensor(out=ang[:], in0=turns[:], scalar=-part, in1=ang[:], op0=ALU.mult, op1=ALU.add))
            pi = float(np.nextafter(np.float32(np.pi), np.float32(0)))
            step(nc.vector.tensor_scalar(turns[:], ang[:], float(np.pi / 2), None, ALU.add))
            step(nc.vector.tensor_scalar(rt[:, 0], turns[:], pi, None, ALU.is_gt))
            step(nc.vector.scalar_tensor_tensor(out=turns[:], in0=rt[:, 0], scalar=float(-2 * np.pi), in1=turns[:], op0=ALU.mult, op1=ALU.add))
            step(nc.vector.tensor_scalar(turns[:], turns[:], pi, -pi, ALU.min, ALU.max))
            nc.vector.tensor_scalar(ang[:], ang[:], pi, -pi, ALU.min, ALU.max).then_inc(ang_ready, 1)
            dve.wait_ge(trig_ready, 2)
            dve.wait_ge(h_ready, TT)
            step(rotate(step, kr[:, :, 0], h[:, :, QR + KVR:], step))
            nc.vector.tensor_copy(kr[:, :, 1], kr[:, :, 0]).then_inc(kr_ready, 1)
            dve.wait_ge(sq_ready, 2 * TT)
            step(nc.vector.tensor_scalar(ss[:, 0:TT], ss[:, 0:TT], 1.0 / QR, RMS_EPS, ALU.mult, ALU.add))
            step(nc.vector.tensor_scalar(ss[:, TT:], ss[:, TT:], 1.0 / KVR, RMS_EPS, ALU.mult, ALU.add))
            rsqrt(nc, step, rs[:], ss[:], nt[:])
            for tt in range(TT):
                nc.vector.tensor_scalar(h[:, tt, 0:QR], h[:, tt, 0:QR], rs[:, tt:tt + 1], None, ALU.mult)
                nc.vector.tensor_scalar(h[:, tt, QR:QR + KVR], h[:, tt, QR:QR + KVR], rs[:, TT + tt:TT + tt + 1], None, ALU.mult).then_inc(norm_ready, 1)

            def add_output(i, n, b):
                y = res[:, n // 2, (n % 2) * 512:(n % 2 + 1) * 512]
                nc.vector.tensor_tensor(y, y, ps[b][:], ALU.add).then_inc(y_ready, 1)

            def body(i, uses, first):
                def got(name):
                    b, n = nth(uses, name, i)
                    dve.wait_ge(full[b], n + 1)
                    return ps[b]

                def read(ins):
                    ins.then_inc(rope_read, 1)
                    dve.wait_ge(rope_read, i + 1)

                bank = got("qr")
                rotate(step, qr, bank[:, 0:TT * ROPE].rearrange("p (t n) -> p t n", t=TT), read).then_inc(qr_ready, 1)
                nc.vector.tensor_copy(qrT[:].rearrange("p a n -> p (a n)"), got("qrT")[:, 0:2 * P]).then_inc(qrT_ready, 1)
                for n in range(TT):
                    bank = got(f"S{n}")
                    step(nc.vector.tensor_reduce(mx[:, n:n + 1], bank[:], AX.X, ALU.max))
                    nc.vector.tensor_scalar(nb[:, n:n + 1], mx[:, n:n + 1], -scale, None, ALU.mult).then_inc(nb_ready, 1)
                if not first:
                    for n in range(8):
                        got(f"y{n}")
                        if n == 0:
                            dve.wait_ge(y_ready, 1 + 8 * (i - 1))
                        add_output(i - 1, n, n % 4)
                for n in range(TT):
                    dve.wait_ge(p_ready, 4 * i + n + 1)
                    step(nc.vector.reciprocal(inv[:, n:n + 1], sums[:, n:n + 1]))
                    nc.vector.tensor_scalar(p[:, n], p[:, n], inv[:, n:n + 1], None, ALU.mult).then_inc(pn_ready, 1)
                for n in (1, 3):
                    bank = got(f"T{n}")
                    nc.vector.tensor_copy(pT[:, :, n * P:(n + 1) * P], bank[:].rearrange("p (k n) -> p k n", k=TT)).then_inc(pT_ready[1], 1)
                assert first or state["k"] == state["per"]

            state["base"] += state["k"]
            state["k"] = 0
            body(0, FIRST, True)
            per = state["k"]
            state.update(per=per)

            def round_(i):
                state.update(i=i, k=0)
                body(i, MAIN, False)
            with dve.Fori(1, NH) as i:
                round_(i)
            for n in range(8):
                dve.wait_ge(full[n % 4], nth(MAIN, f"T{n % 4}", NH - 1)[1] + 2 + n // 4)
                dve.wait_ge(y_ready, 1 + 8 * (NH - 1))
                add_output(NH - 1, n, n % 4)


TWO_PI = (6.28125, 0.0019340515136718750, float(2 * np.pi - 6.28125 - 0.0019340515136718750))


def program(nc, dram, out):
    with ExitStack() as ctx:
        t = {
            "const": ctx.enter_context(nc.sbuf_tensor("masks", [P, C_ALL], F32)),
            "res": ctx.enter_context(nc.sbuf_tensor("res", [P, TT, D], F32)),
            "xT": ctx.enter_context(nc.sbuf_tensor("xT", [P, KD, SEQ], F32)),
            "gates": ctx.enter_context(nc.sbuf_tensor("gates", [P, TT, NE], F32)),
            "ps": [ctx.enter_context(nc.psum_tensor(f"bank{b}", [P, 512], F32)) for b in range(8)],
            "x_in": [ctx.enter_context(nc.semaphore(f"x_in_{n}")) for n in range(TT)],
        }
        delta_net(nc, t, None, dram)
        norm(nc, t, dram, "ln1_g", "ln1_b", 0, "norm0")
        experts(nc, t, dram, 0, "moe0")
        norm(nc, t, dram, "ln2_g", "ln2_b", 0, "norm1", routed=False)
        latent_attention(nc, t, dram)
        norm(nc, t, dram, "ln1_g", "ln1_b", 1, "norm2")
        experts(nc, t, dram, 1, "moe1")
        norm(nc, t, dram, "ln2_g", "ln2_b", 1, "norm3", routed=False, out=out)


_INS = ["x", "positions", "dn_w_in", "dn_conv_w", "dn_a_log", "dn_dt_bias", "dn_norm_w", "dn_w_out",
        "mla_w_in", "mla_q_norm", "mla_w_qb", "mla_kv_norm", "mla_w_kvb", "mla_w_out",
        "ln1_g", "ln1_b", "ln2_g", "ln2_b", "router_w", "router_bias", "moe_w_gate", "moe_w_up", "moe_w_down"]


def kernel(**inputs):
    import concourse.bacc as _bacc
    from concourse.bass_utils import run_bass_kernel_spmd as _run

    nc = _bacc.Bacc("TRN2", target_bir_lowering=False, num_devices=1)
    arrays = {name: np.ascontiguousarray(inputs[name]) for name in _INS}
    arrays["const"] = constants()
    dram = {name: nc.dram_tensor(name, a.shape, mybir.dt.from_np(a.dtype), kind="ExternalInput").ap() for name, a in arrays.items()}
    out = nc.dram_tensor("out", (1, SEQ, D), F32, kind="ExternalOutput").ap()
    program(nc, dram, out)
    return _run(nc, [arrays], core_ids=[0]).results[0]["out"]
```

```python
from contextlib import ExitStack

import numpy as np

import concourse.bass as bass
from concourse import mybir

ALU = mybir.AluOpType
ACT = mybir.ActivationFunctionType
AX = mybir.AxisListType
F32 = mybir.dt.float32

P = 128
D = 1024
SEQ = 512
TT = SEQ // P
KD = D // P
ALPHA = 4.0 ** 0.25
LN_EPS = 1e-5
RMS_EPS = 1e-6

NK, NV, DH = 8, 16, 128
K_OFF, V_OFF, Z_OFF, BA_OFF = NK * DH, 2 * NK * DH, 2 * NK * DH + NV * DH, 2 * NK * DH + 2 * NV * DH
TAPS = 5
LEVELS = 7
GRAW, NEG_EG, EG, BETA, COEF, EGL = range(6)

C_ID, C_ONE, C_TF, C_TB, C_SF, C_SB = (P * n for n in range(6))
C_LEV = 6 * P
C_JLT = C_LEV + 2 * LEVELS * 64
C_FREQ = C_JLT + 16
C_BELOW = C_FREQ + 32
C_NUM = C_BELOW + 256
C_ALL = C_NUM + 16


def constants():
    c = np.zeros((P, C_ALL), np.float32)
    r, q = np.arange(P)[:, None], np.arange(P)[None, :]
    c[:, C_ID:C_ID + P] = r == q
    c[:, C_ONE:C_ONE + P] = 1.0
    c[:, C_TF:C_TF + P] = r <= q
    c[:, C_TB:C_TB + P] = r >= q
    c[:, C_SF:C_SF + P] = r > q
    c[:, C_SB:C_SB + P] = r < q
    for d in range(2):
        for l in range(LEVELS):
            b = 1 << l
            m = (r // (2 * b) == q // (2 * b)) & ((r // b) % 2 == 1 - d) & ((q // b) % 2 == d)
            cols = [x for x in range(P) if (x // b) % 2 == d]
            at = C_LEV + (d * LEVELS + l) * 64
            c[:, at:at + 64] = m[:, cols]
    i, j = np.arange(4)[:, None], np.arange(4)[None, :]
    c[:, C_JLT:C_JLT + 16] = (j < i).reshape(1, 16)
    c[:, C_BELOW:C_BELOW + 256] = (np.arange(16)[None, :] < np.arange(16)[:, None]).reshape(1, 256)
    c[:, C_NUM:C_NUM + 16] = np.arange(16)[None]
    inv = (1.0 / (10000.0 ** (np.arange(0, 64, 2, dtype=np.float32) / np.float32(64)))).astype(np.float32)
    c[:, C_FREQ:C_FREQ + 32] = inv[None]
    return c




class Uses:

    def __init__(self, names):
        self.at, self.per, self.before, last = {}, {}, {}, {}
        for name, bank in names:
            self.before[name] = last.get(bank)
            last[bank] = name
            self.at[name] = (bank, self.per.get(bank, 0))
            self.per[bank] = self.per.get(bank, 0) + 1


PROJECT = [("proj0", 0), ("proj1", 1), ("proj2", 0), ("proj3", 1)]
def phase(nc, ctx, prefix=""):
    made = []

    def end():
        nc.clear_and_free_semaphores(made)
        nc.all_engine_barrier()

    def sem(name):
        made.append(nc.alloc_semaphore(name=prefix + name))
        return made[-1]

    ctx.callback(end)
    return sem


def dn_uses(with_next):
    names = [("taps", 2)] if with_next else []
    names += [("D0", 2), ("D1", 3)] + [(f"tr{c}", 2 + c % 2) for c in range(4)]
    names += [("D2", 2), ("D3", 3), ("kT", 2), ("qT", 3), ("KK", 2), ("KQ", 3)]
    if with_next:
        names += PROJECT
    for l in range(LEVELS):
        for g in range(4):
            names += [(f"X{l}{g}", 4 + g % 2), (f"U{l}{g}", 6 + g % 2)]
    names += [("z0", 0), ("z1", 1)]
    for s in range(4):
        for d in range(2):
            if s:
                names.append((f"kq{s}{d}", 4 + d))
            names += [(f"w{s}{d}", 2 + d), (f"os{s}{d}", 6 + d)]
    names += [("oT0", 2), ("oT1", 3)] + [(f"y{n}", n % 2) for n in range(8)]
    return Uses(names)


RSQRT_STEPS = 11


def rsqrt(nc, step, out, x, tmp):
    i32 = mybir.dt.int32
    step(nc.vector.tensor_scalar(out.bitcast(i32), x.bitcast(i32), 1, None, ALU.logical_shift_right))
    step(nc.vector.tensor_scalar(out.bitcast(i32), out.bitcast(i32), -1.0, float(0x5F3759DF), ALU.mult, ALU.add))
    for _ in range(3):
        step(nc.vector.tensor_tensor(tmp, out, out, ALU.mult))
        step(nc.vector.scalar_tensor_tensor(out=tmp, in0=tmp, scalar=-0.5, in1=x, op0=ALU.mult, op1=ALU.mult))
        step(nc.vector.scalar_tensor_tensor(out=out, in0=tmp, scalar=1.5, in1=out, op0=ALU.add, op1=ALU.mult))


def delta_net(nc, t, s, dram):
    F = Uses(PROJECT + [("taps", 2)])
    MAIN, LAST = dn_uses(True), dn_uses(False)
    c, ps, res, xT = t["const"], t["ps"], t["res"], t["xT"]
    ident, ones = c[:, C_ID:C_ID + P], c[:, C_ONE:C_ONE + P]
    tri = [c[:, C_TF:C_TF + P], c[:, C_TB:C_TB + P]]
    after = [c[:, C_SF:C_SF + P], c[:, C_SB:C_SB + P]]
    before = [after[1], after[0]]

    with ExitStack() as ctx:
        def sb(name, shape):
            return ctx.enter_context(nc.sbuf_tensor(name, shape, F32))

        sem = phase(nc, ctx)

        wqkv = sb("wqkv", [P, 4, KD, P])
        wz = sb("wz", [P, KD, 2 * P])
        wo = sb("wo", [P, 2, D])
        tapr = sb("tapr", [TAPS, 4, P])
        taps = sb("taps", [P, 4, TAPS])
        conv = sb("conv", [P, 4, SEQ])
        th = sb("th", [P, 2, SEQ])
        sq = sb("sq", [P, 2, SEQ])
        kq = sb("kq", [P, 2, TT, P])
        kqT = sb("kqT", [P, 2, TT, P])
        v = sb("v", [P, 2, TT, P])
        zs = sb("zs", [P, TT, 2, P])
        ss = sb("ss", [P, 8])
        rs = sb("rs", [P, 8])
        nt = sb("nt", [P, 8])
        triG = sb("triG", [P, 2, TT, P])
        dec = sb("dec", [P, 4, TT, P])
        kkm = sb("kkm", [P, 2, TT, P])
        kqm = sb("kqm", [P, 2, TT, P])
        A = sb("A", [P, 4, TT, P])
        T = sb("T", [P, 4, TT, P])
        U = sb("U", [P, 4, TT, P])
        X = sb("X", [P, LEVELS, 2, TT, P])
        St = sb("St", [P, 2, 2, P])
        r = sb("r", [P, 2, 2, P])
        vn = sb("vn", [P, 2, 2, P])
        vs = sb("vs", [P, 2, 2, P])
        o = sb("o", [P, TT, 2, P])
        oT = sb("oT", [P, 2, TT, P])
        gt = sb("gt", [P, 6, TT, 2 * NV])
        gb = sb("gb", [P, 6 * TT, 2, 2])
        nw = sb("nw", [P, 1])
        bvec = sb("bvec", [P, 2, 2 * NV])
        wba = sb("wba", [P, KD, 4 * NV])
        ba = sb("ba", [P, TT, 4 * NV])
        tmp = sb("tmp", [P, 4, TT, 2 * NV])

        full = [sem(f"dn_full{b}") for b in range(8)]
        x_in, small_in, ba_in = sem("x_in"), sem("small_in"), sem("ba_in")
        w_in = [sem(f"w_in{n}") for n in range(4)]
        z_in, o_in, taps_in = sem("z_in"), sem("o_in"), sem("taps_in")
        link, alink, plink = sem("dve_link"), sem("act_link"), sem("pool_link")
        x_turned = sem("x_turned")
        xT_ready = sem("xT_ready")
        gates_ready, raw_ready, beta_ready = sem("gates_ready"), sem("raw_ready"), sem("beta_ready")
        sums_ready = sem("sums_ready")
        gb_ready, triG_ready, dec_ready, at_ready, qkd_ready = (sem(n) for n in ("gb_ready", "triG_ready", "dec_ready", "at_ready", "qkd_ready"))
        eye_ready = sem("eye_ready")
        taps_ready, conv_ready, th_ready, silu_ready = (sem(n) for n in ("taps_ready", "conv_ready", "th_ready", "silu_ready"))
        sq_ready, ss_ready, rs_ready, kq_ready, kqT_ready, v_ready = (sem(n) for n in ("sq_ready", "ss_ready", "rs_ready", "kq_ready", "kqT_ready", "v_ready"))
        mask_ready = sem("mask_ready")
        xm_ready, upd_ready = sem("xm_ready"), sem("upd_ready")
        zt_ready, zs_ready = sem("zt_ready"), sem("zs_ready")
        r_ready, vs_ready, vn_ready, S_ready, o_step = (sem(n) for n in ("r_ready", "vs_ready", "vn_ready", "S_ready", "o_step"))
        oq_ready, ba_ready, dve_sums = sem("oq_ready"), sem("ba_ready"), sem("dve_sums")
        osq_ready, oss_ready, ors_ready, on_ready, og_ready, oT_ready, y_ready = (sem(n) for n in ("osq_ready", "oss_ready", "ors_ready", "on_ready", "og_ready", "oT_ready", "y_ready"))
        x_zero, zeroed, zero_filled = sem("x_zero"), sem("zeroed"), sem("zero_filled")
        zeros = sb("zeros", [CAP, D])

        base = {0: 2, 1: 2, 2: 2, 3: 1, 4: 4, 5: 4, 6: 0, 7: 0}

        def read_of(name, i):
            if name[:-1] in ("D", "tr", "proj", "z", "y", "oT"):
                n = int(name[-1])
                if name[:-1] == "tr":
                    return (v_ready, i * 2 + n - 1) if n >= 2 else (kq_ready, i * 2 + 2 - n)
                return {"D": (dec_ready, i * 4 + n + 1), "proj": (conv_ready, (i + 1) * 4 + n + 1), "z": (zs_ready, i * 2 + n + 1),
                        "y": (y_ready, 1 + i * 8 + n + 1), "oT": (oT_ready, 1 + i * 2 + n + 1)}[name[:-1]]
            if name in ("kT", "qT"):
                return kqT_ready, i * 2 + (1 if name == "kT" else 2)
            if name in ("KK", "KQ"):
                return mask_ready, i * 4 + (2 if name == "KK" else 4)
            if name == "taps":
                return taps_ready, i + 2
            a, b = int(name[-2]), int(name[-1])
            if name[0] in "XU":
                return (xm_ready if name[0] == "X" else upd_ready), i * 28 + a * 4 + b + 1
            if name[:2] == "kq":
                return oq_ready, i * 6 + (a - 1) * 2 + b + 1
            if name[0] == "w":
                return vn_ready, i * 8 + a * 2 + b + 1
            return o_step, 1 + i * 8 + a * 2 + b + 1

        last_read = {0: (y_ready, 8), 1: (y_ready, 8), 2: (oT_ready, 2), 3: (oT_ready, 2), 4: (o_step, 8), 5: (o_step, 8), 6: (o_step, 8), 7: (o_step, 8)}

        def nth(uses, name, i):
            b, k = uses.at[name]
            return b, base[b] + i * MAIN.per[b] + k

        def level(a, d, l, other=0):
            b = 1 << l
            return a.rearrange("p (a h b) -> p a h b", h=2, b=b)[:, :, (d + other) % 2, :]

        w_dram = dram["dn_w_in"][0].rearrange("(k p) n -> p k n", p=P)
        wo_dram = dram["dn_w_out"][0].rearrange("(h p) n -> p h n", p=P)
        cw_dram = dram["dn_conv_w"][0]

        block = ctx.enter_context(nc.Block())

        @block.sync
        def _(sp):
            x_dram = dram["x"][0].rearrange("(t p) n -> p t n", p=P)
            sp.dma_start(c[:], dram["const"]).then_inc(small_in, 16)
            for tt in range(TT):
                sp.dma_start(res[:, tt], x_dram[:, tt]).then_inc(t["x_in"][tt], 16)
            sp.dma_start(wba[:], w_dram[:, :, BA_OFF:BA_OFF + 4 * NV]).then_inc(ba_in, 16)
            sp.dma_start(bvec[:, 0], dram["dn_a_log"][0].rearrange("d h -> (d h)").partition_broadcast(P)).then_inc(small_in, 16)
            sp.dma_start(bvec[:, 1], dram["dn_dt_bias"][0].rearrange("d h -> (d h)").partition_broadcast(P)).then_inc(small_in, 16)
            sp.dma_start(nw[:], dram["dn_norm_w"].rearrange("a p -> p a")).then_inc(small_in, 16)

            def load_w(n, dynamic):
                at = (lambda off, w: bass.ds(off, w)) if dynamic else (lambda off, w: slice(off, off + w))
                for ct in range(4):
                    off = [n * P, K_OFF + n * P, V_OFF + n * 2 * P, V_OFF + n * 2 * P + P][ct]
                    if dynamic or n:
                        b, k = (F.at[f"proj{ct}"])
                        if dynamic:
                            sp.wait_ge(conv_ready, (n - 1) * 4 + ct + 1)
                    sp.dma_start(wqkv[:, ct], w_dram[:, :, at(off, P)]).then_inc(w_in[ct], 16)
                if dynamic:
                    sp.wait_ge(taps_ready, n)
                for a, (off, w) in enumerate([(n * P, P), (K_OFF + n * P, P), (V_OFF + n * 2 * P, 2 * P)]):
                    sp.dma_start(tapr[:, a:a + w // P].rearrange("p a b -> p (a b)"), cw_dram[:, at(off, w)]).then_inc(taps_in, 16)

            def load_late(n, dynamic):
                at = (lambda off, w: bass.ds(off, w)) if dynamic else (lambda off, w: slice(off, off + w))
                if dynamic:
                    sp.wait_ge(zs_ready, n * 2)
                sp.dma_start(wz[:], w_dram[:, :, at(Z_OFF + n * 2 * P, 2 * P)]).then_inc(z_in, 16)
                if dynamic:
                    sp.wait_ge(y_ready, 1 + n * 8)
                src = wo_dram[:, at(n * 2, 2), :]
                sp.dma_start(wo[:], src).then_inc(o_in, 16)

            load_w(0, False)
            load_late(0, False)
            sp.wait_ge(zeroed, 1)
            for slots in (t["slots_x"], t["slots_y"]):
                blocks = slots.rearrange("(b p) n -> p b n", p=CAP)
                sp.dma_start(blocks, zeros[:].rearrange("p (a n) -> p a n", a=1).to_broadcast([CAP, BLOCKS, D])).then_inc(zero_filled, 16)
            with sp.Fori(1, NK) as n:
                load_w(n, True)
                load_late(n, True)
            sp.wait_ge(zero_filled, 32)

        @block.tensor
        def _(pe):
            def begin(uses, name, i):
                b, k = uses.at[name]
                if k == 0:
                    signal, per = last_read[b]
                    pe.wait_ge(signal, 1 + i * per)
                else:
                    pe.wait_ge(*read_of(uses.before[name], i))
                return ps[b]

            def done(mm, uses, name):
                mm.then_inc(full[uses.at[name][0]], 1)

            pe.wait_ge(small_in, 64)
            for n in range(8):
                tt, half = n // 2, n % 2
                if half == 0:
                    pe.wait_ge(t["x_in"][tt], 16)
                b = 4 + n % 2
                if n >= 2:
                    pe.wait_ge(xT_ready, n - 1)
                for k in range(4):
                    mm = pe.transpose(ps[b][:, k * P:(k + 1) * P], res[:, tt, (half * 4 + k) * P:(half * 4 + k + 1) * P], ident)
                mm.then_inc(full[b], 1)
            pe.wait_ge(ba_in, 16)
            pe.wait_ge(xT_ready, 8)
            for tt in range(TT):
                for k in range(KD):
                    mm = pe.matmul(ps[2][:, tt * 64:(tt + 1) * 64], xT[:, k, tt * P:(tt + 1) * P], wba[:, k], start=k == 0, stop=k == KD - 1)
            mm.then_inc(full[2], 1)

            def project(uses, i, n, ct, part=(0, KD)):
                if part[0] == 0:
                    pe.wait_ge(w_in[ct], (n + 1) * 16)
                    begin(uses, f"proj{ct}", i)
                bank = ps[uses.at[f"proj{ct}"][0]]
                for k in range(*part):
                    mm = pe.matmul(bank[:], wqkv[:, ct, k], xT[:, k], start=k == 0, stop=k == KD - 1)
                if part[1] == KD:
                    done(mm, uses, f"proj{ct}")

            def tap_rows(uses, i, n):
                pe.wait_ge(taps_in, (n + 1) * 48)
                bank = begin(uses, "taps", i)
                for ct in range(4):
                    mm = pe.matmul(bank[:, ct * TAPS:(ct + 1) * TAPS], tapr[:, ct], ident[0:TAPS, 0:TAPS], start=True, stop=True)
                done(mm, uses, "taps")

            pe.wait_ge(raw_ready, 1)
            for d in range(2):
                pe.matmul(ps[3][:, 0:P].rearrange("p (t g) -> p t g", t=TT)[:, :, d * NV:(d + 1) * NV], tri[d], gt[:, GRAW, :, d * NV:(d + 1) * NV], start=True, stop=True)
            mm = pe.matmul(ps[3][:, P:2 * P], ones, gt[:, GRAW].rearrange("p t g -> p (t g)"), start=True, stop=True)
            mm.then_inc(full[3], 1)

            pe.wait_ge(taps_in, 48)
            pe.wait_ge(ba_ready, 1)
            for ct in range(4):
                mm = pe.transpose(ps[2][:, ct * TAPS:(ct + 1) * TAPS], tapr[:, ct], ident[0:TAPS, 0:TAPS])
            mm.then_inc(full[2], 1)
            for ct in range(4):
                pe.wait_ge(w_in[ct], 16)
                b = ct % 2
                if ct >= 2:
                    pe.wait_ge(conv_ready, ct - 1)
                for kk in range(KD):
                    mm = pe.matmul(ps[b][:], wqkv[:, ct, kk], xT[:, kk], start=kk == 0, stop=kk == KD - 1)
                mm.then_inc(full[b], 1)

            def body(i, uses, with_next):
                fill = []
                if with_next:
                    for ct in range(4):
                        for a in range(0, KD, 2):
                            fill.append((project, (uses, i, i + 1, ct, (a, a + 2))))
                    tap_rows(uses, i, i + 1)

                def filler(n=1):
                    for _ in range(n):
                        if fill:
                            f, a = fill.pop(0)
                            f(*a)

                def decay(g):
                    pe.wait_ge(triG_ready, i * 4 + g + 1)
                    bank = begin(uses, f"D{g}", i)
                    done(pe.matmul(bank[:], after[g // 2], triG[:, g % 2].rearrange("p t n -> p (t n)"), start=True, stop=True), uses, f"D{g}")

                decay(0)
                decay(1)
                for ct in range(4):
                    pe.wait_ge(silu_ready, i * 4 + ct + 1)
                    bank = begin(uses, f"tr{ct}", i)
                    for tt in range(TT):
                        mm = pe.transpose(bank[:, tt * P:(tt + 1) * P], conv[:, ct, tt * P:(tt + 1) * P], ident)
                    done(mm, uses, f"tr{ct}")
                filler(2)
                decay(2)
                decay(3)
                filler(2)
                for n, ct in ((1, 1), (0, 0)):
                    name = "kT" if n else "qT"
                    pe.wait_ge(kq_ready, i * 2 + (1 if ct else 2))
                    bank = begin(uses, name, i)
                    for tt in range(TT):
                        mm = pe.transpose(bank[:, tt * P:(tt + 1) * P], kq[:, ct, tt], ident)
                    done(mm, uses, name)
                filler(1)
                pe.wait_ge(kqT_ready, i * 2 + 1)
                bank = begin(uses, "KK", i)
                for tt in range(TT):
                    mm = pe.matmul(bank[:, tt * P:(tt + 1) * P], kqT[:, 1, tt], kqT[:, 1, tt], start=True, stop=True)
                done(mm, uses, "KK")
                pe.wait_ge(kqT_ready, i * 2 + 2)
                bank = begin(uses, "KQ", i)
                for tt in range(TT):
                    mm = pe.matmul(bank[:, tt * P:(tt + 1) * P], kqT[:, 1, tt], kqT[:, 0, tt], start=True, stop=True)
                done(mm, uses, "KQ")
                filler(2)

                pe.wait_ge(eye_ready, i * 8 + 8)

                def make_x(n):
                    l, g = divmod(n, 4)
                    d = g // 2
                    if l == 0:
                        pe.wait_ge(at_ready, i * 4 + g + 1)
                    else:
                        pe.wait_ge(upd_ready, i * 28 + n - 4 + 1)
                    bank = begin(uses, f"X{l}{g}", i)
                    for tt in range(TT):
                        mm = pe.matmul(bank[:, tt * 64:(tt + 1) * 64], A[:, g, tt], level(T[:, g, tt], d, l), start=True, stop=True)
                    done(mm, uses, f"X{l}{g}")

                def make_u(n):
                    l, g = divmod(n, 4)
                    d = g // 2
                    pe.wait_ge(xm_ready, i * 28 + n + 1)
                    bank = begin(uses, f"U{l}{g}", i)
                    for tt in range(TT):
                        if 0 < l < LEVELS - 1:
                            pe.matmul(bank[:, tt * 64:(tt + 1) * 64], U[:, g, tt], level(X[:, l, g % 2, tt], d, l), start=True, stop=True)
                        mm = pe.matmul(bank[:, 256 + tt * 64:256 + (tt + 1) * 64], X[:, l, g % 2, tt], level(U[:, g, tt], d, l, 1), start=True, stop=True)
                    done(mm, uses, f"U{l}{g}")

                for n in range(LEVELS * 4 + 2):
                    if n < LEVELS * 4:
                        make_x(n)
                    if n >= 2:
                        make_u(n - 2)
                    if n in (1, 4, 6, 8, 10, 11, 13, 15, 17):
                        filler(1)
                filler(99)

                pe.wait_ge(z_in, (i + 1) * 16)

                def make_z(tt):
                    name = f"z{tt // 2}"
                    if tt % 2 == 0:
                        begin(uses, name, i)
                    bank = ps[uses.at[name][0]]
                    for k in range(KD):
                        mm = pe.matmul(bank[:, (tt % 2) * 256:(tt % 2) * 256 + 256], xT[:, k, tt * P:(tt + 1) * P], wz[:, k], start=k == 0, stop=k == KD - 1)
                    if tt % 2:
                        done(mm, uses, name)

                for step in range(4):
                    for d in range(2):
                        tt = 3 - step if d else step
                        if step:
                            pe.wait_ge(S_ready, i * 6 + (step - 1) * 2 + d + 1)
                            bank = begin(uses, f"kq{step}{d}", i)
                            S2 = St[:, d].rearrange("p h n -> p (h n)")
                            pe.matmul(bank[:, 0:256], kqT[:, 1, tt], S2, start=True, stop=True)
                            mm = pe.matmul(bank[:, 256:512], kqT[:, 0, tt], S2, start=True, stop=True)
                            done(mm, uses, f"kq{step}{d}")
                    for k in range(0, 1):
                        make_z(step)
                    for d in range(2):
                        tt = 3 - step if d else step
                        if step:
                            pe.wait_ge(r_ready, i * 6 + (step - 1) * 2 + d + 1)
                        else:
                            pe.wait_ge(upd_ready, i * 28 + 28)
                            pe.wait_ge(v_ready, i * 2 + 2)
                        bank = begin(uses, f"w{step}{d}", i)
                        for h in range(2):
                            mm = pe.matmul(bank[:, h * P:(h + 1) * P], U[:, d * 2 + h, tt], r[:, d, h] if step else v[:, h, tt], start=True, stop=True)
                        done(mm, uses, f"w{step}{d}")
                    for d in range(2):
                        tt = 3 - step if d else step
                        bank = begin(uses, f"os{step}{d}", i)
                        if step < 3:
                            pe.wait_ge(vs_ready, i * 6 + step * 2 + d + 1)
                            pe.matmul(bank[:, 256:512], kq[:, 1, tt], vs[:, d].rearrange("p h n -> p (h n)"), start=True, stop=True)
                        pe.wait_ge(vn_ready, i * 8 + step * 2 + d + 1)
                        pe.wait_ge(qkd_ready, i * 4 + 4)
                        for h in range(2):
                            mm = pe.matmul(bank[:, h * P:(h + 1) * P], dec[:, d * 2 + h, tt], vn[:, d, h], start=True, stop=True)
                        done(mm, uses, f"os{step}{d}")

                for h in range(2):
                    pe.wait_ge(og_ready, i + 1)
                    bank = begin(uses, f"oT{h}", i)
                    for tt in range(TT):
                        mm = pe.transpose(bank[:, tt * P:(tt + 1) * P], o[:, tt, h], ident)
                    done(mm, uses, f"oT{h}")
                pe.wait_ge(o_in, (i + 1) * 16)
                pe.wait_ge(oT_ready, 1 + i * 2 + 2)
                for n in range(8):
                    tt, half = n // 2, n % 2
                    bank = begin(uses, f"y{n}", i)
                    for h in range(2):
                        mm = pe.matmul(bank[:], oT[:, h, tt], wo[:, h, half * 512:(half + 1) * 512], start=h == 0, stop=h == 1)
                    done(mm, uses, f"y{n}")

            pe.wait_ge(taps_ready, 1)
            pe.wait_ge(conv_ready, 4)
            pe.wait_ge(dve_sums, 1)
            with pe.Fori(0, NK - 1) as i:
                body(i, MAIN, True)
            body(NK - 1, LAST, False)

        @block.scalar
        def _(act):
            def got(uses, name, i):
                b, n = nth(uses, name, i)
                act.wait_ge(full[b], n + 1)
                return ps[b]

            act.sem_inc(oT_ready, 1)
            for n in range(8):
                b = 4 + n % 2
                act.wait_ge(full[b], n // 2 + 1)
                tt, half = n // 2, n % 2
                act.copy(xT[:, half * 4:half * 4 + 4, tt * P:(tt + 1) * P], ps[b][:].rearrange("p (k n) -> p k n", k=4)).then_inc(xT_ready, 1)

            act.wait_ge(full[2], 1)
            act.copy(ba[:].rearrange("p t g -> p (t g)"), ps[2][:, 0:256]).then_inc(ba_ready, 1)
            act.wait_ge(ba_ready, 1)
            act.activation(tmp[:, 0], ba[:, :, 0:32], ACT.Exp, scale=-1.0).then_inc(beta_ready, 1)
            act.activation(bvec[:, 0], bvec[:, 0], ACT.Exp).then_inc(beta_ready, 1)
            act.wait_ge(gates_ready, 1)
            act.activation(tmp[:, 2], tmp[:, 2], ACT.Exp).then_inc(alink, 1)
            act.wait_ge(alink, 1)
            act.activation(tmp[:, 2], tmp[:, 2], ACT.Ln, bias=1.0).then_inc(beta_ready, 1)
            act.wait_ge(gates_ready, 2)
            act.activation(gt[:, EG], tmp[:, 0], ACT.Exp).then_inc(sums_ready, 1)
            act.activation(gt[:, EGL], tmp[:, 3], ACT.Exp).then_inc(sums_ready, 1)
            act.activation(tmp[:, 1], tmp[:, 1], ACT.Exp).then_inc(sums_ready, 1)

            def act_silu(n, ct):
                act.wait_ge(conv_ready, n * 4 + ct + 1)
                if not (isinstance(n, int) and n == 0 and ct < 2):
                    act.wait_ge(silu_ready, n * 4 + ct - 1)
                act.activation(th[:, ct % 2], conv[:, ct], ACT.Tanh, scale=0.5).then_inc(th_ready, 1)

            for ct in range(4):
                act_silu(0, ct)

            def body(i, uses, with_next):
                if not isinstance(i, int):
                    act.wait_ge(o_step, 1 + i * 8)
                else:
                    act.wait_ge(o_step, 1 + i * 8)
                act.wait_ge(gates_ready, 3)
                src = gt[:].rearrange("p f t (d h) -> p (f t) d h", d=2)[:, :, :, bass.ds(2 * i, 2)] if not isinstance(i, int) \
                    else gt[:].rearrange("p f t (d h) -> p (f t) d h", d=2)[:, :, :, 2 * i:2 * i + 2]
                act.copy(gb[:], src).then_inc(gb_ready, 1)

                def decay(g):
                    bank = got(uses, f"D{g}", i)
                    act.wait_ge(o_step, 1 + i * 8)
                    act.activation(dec[:, g].rearrange("p t n -> p (t n)"), bank[:], ACT.Exp).then_inc(dec_ready, 1)

                decay(0)
                decay(1)
                for g in range(4):
                    eye = ident.rearrange("p (a n) -> p a n", a=1).to_broadcast([P, TT, P])
                    act.copy(T[:, g], eye).then_inc(eye_ready, 1)
                    act.copy(U[:, g], eye).then_inc(eye_ready, 1)
                for ct in range(2):
                    bank = got(uses, f"tr{ct}", i)
                    act.wait_ge(oss_ready, 1 + i)
                    act.activation(sq[:, ct], bank[:], ACT.Square).then_inc(sq_ready, 1)
                for h in range(2):
                    bank = got(uses, f"tr{2 + h}", i)
                    act.mul(v[:, h].rearrange("p t n -> p (t n)"), bank[:], 0.5).then_inc(v_ready, 1)
                decay(2)
                decay(3)
                for n in (1, 0):
                    name = "kT" if n else "qT"
                    bank = got(uses, name, i)
                    act.copy(kqT[:, n].rearrange("p t n -> p (t n)"), bank[:]).then_inc(kqT_ready, 1)
                if with_next:
                    for ct in range(4):
                        act_silu(i + 1, ct)

                def z_tanh(n):
                    bank = got(uses, f"z{n}", i)
                    act.wait_ge(oss_ready, 1 + i)
                    act.wait_ge(ss_ready, i + 1)
                    act.activation(sq[:, n], bank[:], ACT.Tanh, scale=0.5).then_inc(zt_ready, 1)

                for step in range(4):
                    for d in range(2):
                        tt = 3 - step if d else step
                        bank = got(uses, f"w{step}{d}", i)
                        if step < 3:
                            for h in range(2):
                                ins = act.mul(vs[:, d, h], bank[:, h * P:(h + 1) * P], gb[:, COEF * TT + tt, d, h:h + 1])
                            ins.then_inc(vs_ready, 1)
                        for h in range(2):
                            ins = act.mul(vn[:, d, h], bank[:, h * P:(h + 1) * P], gb[:, BETA * TT + tt, d, h:h + 1])
                        ins.then_inc(vn_ready, 1)
                    if step == 1:
                        z_tanh(0)
                    if step == 3:
                        z_tanh(1)

                act.wait_ge(o_step, 1 + i * 8 + 8)
                act.wait_ge(zs_ready, i * 2 + 2)
                act.activation(sq[:].rearrange("p a n -> p (a n)"), o[:].rearrange("p t h n -> p (t h n)"), ACT.Square).then_inc(osq_ready, 1)
                for h in range(2):
                    bank = got(uses, f"oT{h}", i)
                    act.wait_ge(y_ready, 1 + i * 8)
                    act.mul(oT[:, h].rearrange("p t n -> p (t n)"), bank[:], nw[:, 0:1]).then_inc(oT_ready, 1)

            with act.Fori(0, NK - 1) as i:
                body(i, MAIN, True)
            body(NK - 1, LAST, False)

        @block.gpsimd
        def _(pool):
            nc.gpsimd.memset(zeros[:], 0.0).then_inc(zeroed, 1)
            nc.gpsimd.memset(X[:], 0.0).then_inc(x_zero, 1)

            def body(i, uses):
                for g in range(4):
                    d, h = divmod(g, 2)
                    if g == 0:
                        pool.wait_ge(gb_ready, i + 1)
                    if g >= 2:
                        b, n = nth(uses, f"D{g - 2}", i)
                        pool.wait_ge(full[b], n + 1)
                    raw = gb[:, GRAW * TT:(GRAW + 1) * TT, d, h:h + 1].to_broadcast([P, TT, P])
                    nc.gpsimd.tensor_tensor(triG[:, g % 2], tri[d].rearrange("p (a n) -> p a n", a=1).to_broadcast([P, TT, P]), raw, ALU.mult).then_inc(triG_ready, 1)
                for g in range(4):
                    pool.wait_ge(at_ready, i * 4 + g + 1)
                    pool.wait_ge(mask_ready, i * 4 + 4)
                    nc.gpsimd.tensor_tensor(dec[:, g], dec[:, g], kqm[:, g // 2], ALU.mult).then_inc(qkd_ready, 1)

            with pool.Fori(0, NK - 1) as i:
                body(i, MAIN)
            body(NK - 1, LAST)

        @block.vector
        def _(dve):
            links = {"base": 0, "i": 0, "per": 0, "k": 0}

            def step(ins):
                links["k"] += 1
                ins.then_inc(link, 1)
                dve.wait_ge(link, links["base"] + links["i"] * links["per"] + links["k"])

            def got(uses, name, i):
                b, n = nth(uses, name, i)
                dve.wait_ge(full[b], n + 1)
                return ps[b]

            for signal in (y_ready, o_step, oss_ready):
                dve.sem_inc(signal, 1)
            def grid(a):
                return a.rearrange("p (a n) -> p a n", a=1).to_broadcast([P, TT, 2 * NV])

            dve.wait_ge(small_in, 64)
            dve.wait_ge(ba_ready, 1)
            step(nc.vector.tensor_tensor(tmp[:, 1], ba[:, :, 32:64], grid(bvec[:, 1]), ALU.add))
            step(nc.vector.scalar_tensor_tensor(out=tmp[:, 2].rearrange("p t g -> p (t g)"), in0=tmp[:, 1].rearrange("p t g -> p (t g)"), scalar=-1.0,
                                                in1=tmp[:, 1].rearrange("p t g -> p (t g)"), op0=ALU.mult, op1=ALU.min))
            nc.vector.tensor_scalar(tmp[:, 3], tmp[:, 1], 0.0, None, ALU.max).then_inc(gates_ready, 1)
            dve.wait_ge(beta_ready, 1)
            step(nc.vector.tensor_scalar(tmp[:, 0], tmp[:, 0], 1.0, None, ALU.add))
            step(nc.vector.reciprocal(gt[:, BETA], tmp[:, 0]))
            dve.wait_ge(beta_ready, 3)
            dve.wait_ge(gates_ready, 1)
            step(nc.vector.tensor_tensor(tmp[:, 2], tmp[:, 2], tmp[:, 3], ALU.add))
            nc.vector.scalar_tensor_tensor(out=gt[:, GRAW], in0=tmp[:, 2], scalar=-1.0, in1=grid(bvec[:, 0]), op0=ALU.mult, op1=ALU.mult).then_inc(raw_ready, 1)
            dve.wait_ge(full[3], 1)
            step(nc.vector.tensor_copy(tmp[:, 0].rearrange("p t g -> p (t g)"), ps[3][:, 0:P]))
            nc.vector.tensor_copy(tmp[:, 3].rearrange("p t g -> p (t g)"), ps[3][:, P:2 * P]).then_inc(dve_sums, 1)
            dve.wait_ge(dve_sums, 1)
            nc.vector.tensor_tensor(tmp[:, 1], tmp[:, 3], tmp[:, 0], ALU.subtract).then_inc(gates_ready, 1)
            dve.wait_ge(sums_ready, 3)
            nc.vector.tensor_scalar(gt[:, NEG_EG], gt[:, EG], -1.0, None, ALU.mult)
            nc.vector.tensor_tensor(gt[:, COEF], gt[:, BETA], tmp[:, 1], ALU.mult).then_inc(gates_ready, 1)
            for tt in range(TT):
                dve.wait_ge(xT_ready, 2 * tt + 2)
                step(nc.vector.tensor_scalar(res[:, tt], res[:, tt], ALPHA, None, ALU.mult))

            def convolve(uses, i, n, ct, first=False, taps_of=(2, 0, 1, 3, 4)):
                if 2 not in taps_of:
                    bank = ps[ct % 2]
                elif first:
                    b, k = F.at[f"proj{ct}"]
                    dve.wait_ge(full[b], k + 1)
                    bank = ps[b]
                else:
                    bank = got(uses, f"proj{ct}", i)
                    got(uses, f"tr{ct}", i)
                w = taps[:, ct]
                if 2 in taps_of:
                    dve.wait_ge(taps_ready, n + 1)
                    step(nc.vector.tensor_scalar(conv[:, ct], bank[:], w[:, 2:3], None, ALU.mult))
                for j in taps_of:
                    if j == 2:
                        continue
                    d = j - 2
                    lo, hi = max(0, -d), SEQ - max(0, d)
                    ins = nc.vector.scalar_tensor_tensor(out=conv[:, ct, lo:hi], in0=bank[:, lo + d:hi + d], scalar=w[:, j:j + 1], in1=conv[:, ct, lo:hi], op0=ALU.mult, op1=ALU.add)
                    if j == 4:
                        ins.then_inc(conv_ready, 1)
                    else:
                        step(ins)

            def silu(n, ct):
                dve.wait_ge(th_ready, n * 4 + ct + 1)
                nc.vector.scalar_tensor_tensor(out=conv[:, ct], in0=th[:, ct % 2], scalar=1.0, in1=conv[:, ct], op0=ALU.add, op1=ALU.mult).then_inc(silu_ready, 1)

            def tap_columns(bank):
                nc.vector.tensor_copy(taps[:].rearrange("p a b -> p (a b)"), bank[:, 0:4 * TAPS]).then_inc(taps_ready, 1)

            dve.wait_ge(full[2], 2)
            tap_columns(ps[2])
            for ct in range(4):
                convolve(None, 0, 0, ct, first=True)
                if ct:
                    silu(0, ct - 1)
            silu(0, 3)
            dve.wait_ge(x_zero, 1)

            def body(i, uses, with_next, per):
                links.update(i=i, per=per, k=0)
                if with_next:
                    tap_columns(got(uses, "taps", i))
                dve.wait_ge(sq_ready, i * 2 + 2)
                nc.vector.tensor_reduce(ss[:], sq[:].rearrange("p a (t n) -> p (a t) n", t=TT), AX.X, ALU.add).then_inc(ss_ready, 1)
                dve.wait_ge(ss_ready, i + 1)
                step(nc.vector.tensor_scalar(ss[:], ss[:], 4.0 * RMS_EPS, None, ALU.add))
                rsqrt(nc, step, rs[:], ss[:], nt[:])
                step(nc.vector.tensor_scalar(rs[:, 0:TT], rs[:, 0:TT], DH ** -0.5, None, ALU.mult))
                for n, ct in enumerate((1, 0)):
                    b = uses.at[f"tr{ct}"][0]
                    rb = rs[:, ct * TT:(ct + 1) * TT].rearrange("p (t a) -> p t a", a=1).to_broadcast([P, TT, P])
                    bank = ps[b][:].rearrange("p (t n) -> p t n", t=TT)
                    nc.vector.tensor_tensor(kq[:, ct], bank, rb, ALU.mult).then_inc(kq_ready, 1)
                jobs = []
                if with_next:
                    for ct in range(4):
                        for j in (2, 0, 1, 3, 4):
                            jobs.append(lambda ct=ct, j=j: convolve(uses, i, i + 1, ct, taps_of=(j,)))
                            if j == 2 and ct:
                                jobs.append(lambda ct=ct: silu(i + 1, ct - 1))
                    jobs.append(lambda: silu(i + 1, 3))

                bank = got(uses, "KK", i)
                for d in range(2):
                    m = before[d].rearrange("p (a n) -> p a n", a=1).to_broadcast([P, TT, P])
                    ins = nc.vector.tensor_tensor(kkm[:, d], bank[:].rearrange("p (t n) -> p t n", t=TT), m, ALU.mult)
                    ins.then_inc(mask_ready, 1)
                bank = got(uses, "KQ", i)
                for d in range(2):
                    m = tri[d].rearrange("p (a n) -> p a n", a=1).to_broadcast([P, TT, P])
                    ins = nc.vector.tensor_tensor(kqm[:, d], bank[:].rearrange("p (t n) -> p t n", t=TT), m, ALU.mult)
                    ins.then_inc(mask_ready, 1)
                dve.wait_ge(mask_ready, i * 4 + 2)
                for g in range(4):
                    d, h = divmod(g, 2)
                    dve.wait_ge(dec_ready, i * 4 + g + 1)
                    step(nc.vector.tensor_tensor(A[:, g], dec[:, g], kkm[:, d], ALU.mult))
                    beta = gb[:, BETA * TT:(BETA + 1) * TT, d, h:h + 1].to_broadcast([P, TT, P])
                    nc.vector.tensor_tensor(A[:, g], A[:, g], beta, ALU.mult).then_inc(at_ready, 1)

                dve.wait_ge(eye_ready, i * 8 + 8)

                def mask_x(n):
                    l, g = divmod(n, 4)
                    d = g // 2
                    b = 1 << l
                    bank = got(uses, f"X{l}{g}", i)
                    at = C_LEV + (d * LEVELS + l) * 64
                    m = c[:, at:at + 64].rearrange("p (o a) -> p o a", o=1).to_broadcast([P, TT, 64]).rearrange("p t (a b) -> p t a b", b=b)
                    xv = X[:, l, g % 2].rearrange("p t (a h b) -> p t a h b", h=2, b=b)[:, :, :, d, :]
                    nc.vector.tensor_tensor(xv, bank[:, 0:256].rearrange("p (t a b) -> p t a b", t=TT, b=b), m, ALU.mult).then_inc(xm_ready, 1)

                def update(n):
                    l, g = divmod(n, 4)
                    d = g // 2
                    b = 1 << l
                    bank = got(uses, f"U{l}{g}", i)
                    if l < LEVELS - 1:
                        Te = level(T[:, g].rearrange("p t n -> p (t n)"), d, l)
                        if l == 0:
                            x = level(X[:, l, g % 2].rearrange("p t n -> p (t n)"), d, l)
                        else:
                            x = bank[:, 0:256].rearrange("p (a b) -> p a b", b=b)
                        nc.vector.tensor_tensor(Te, Te, x, ALU.subtract).then_inc(link, 1)
                        links["k"] += 1
                    Uo = level(U[:, g].rearrange("p t n -> p (t n)"), d, l, 1)
                    nc.vector.tensor_tensor(Uo, Uo, bank[:, 256:512].rearrange("p (a b) -> p a b", b=b), ALU.subtract).then_inc(upd_ready, 1)

                for n in range(LEVELS * 4 + 2):
                    if n >= 2:
                        update(n - 2)
                    if n < LEVELS * 4:
                        mask_x(n)
                    if jobs:
                        jobs.pop(0)()
                while jobs:
                    jobs.pop(0)()

                def z_silu(n):
                    dve.wait_ge(zt_ready, i * 2 + n + 1)
                    b = uses.at[f"z{n}"][0]
                    flat = zs[:, 2 * n:2 * n + 2].rearrange("p t h n -> p (t h n)")
                    nc.vector.scalar_tensor_tensor(out=flat, in0=sq[:, n], scalar=1.0, in1=ps[b][:], op0=ALU.add, op1=ALU.mult).then_inc(zs_ready, 1)

                for st in range(4):
                    for d in range(2):
                        tt = 3 - st if d else st
                        if st:
                            bank = got(uses, f"kq{st}{d}", i)
                            for h in range(2):
                                ins = nc.vector.scalar_tensor_tensor(out=r[:, d, h], in0=bank[:, h * P:(h + 1) * P], scalar=gb[:, NEG_EG * TT + tt, d, h:h + 1],
                                                                     in1=v[:, h, tt], op0=ALU.mult, op1=ALU.add)
                            ins.then_inc(r_ready, 1)
                            if st >= 2:
                                dve.wait_ge(o_step, 1 + i * 8 + st * 2)
                            for h in range(2):
                                q = bank[:, 256 + h * P:256 + (h + 1) * P]
                                e = gb[:, EG * TT + tt, d, h:h + 1]
                                if st < 2:
                                    ins = nc.vector.tensor_scalar(o[:, tt, h], q, e, None, ALU.mult)
                                else:
                                    ins = nc.vector.scalar_tensor_tensor(out=o[:, tt, h], in0=q, scalar=e, in1=o[:, tt, h], op0=ALU.mult, op1=ALU.add)
                            ins.then_inc(oq_ready, 1)
                    for d in range(2):
                        tt = 3 - st if d else st
                        bank = got(uses, f"os{st}{d}", i)
                        if 0 < st < 3:
                            dve.wait_ge(S_ready, i * 6 + (st - 1) * 2 + d + 1)
                        if st < 3:
                            for h in range(2):
                                if st == 0:
                                    ins = nc.vector.tensor_copy(St[:, d, h], bank[:, 256 + h * P:256 + (h + 1) * P])
                                else:
                                    ins = nc.vector.scalar_tensor_tensor(out=St[:, d, h], in0=St[:, d, h], scalar=gb[:, EGL * TT + tt, d, h:h + 1],
                                                                         in1=bank[:, 256 + h * P:256 + (h + 1) * P], op0=ALU.mult, op1=ALU.add)
                            ins.then_inc(S_ready, 1)
                        flat = o[:, tt].rearrange("p h n -> p (h n)")
                        if st:
                            dve.wait_ge(oq_ready, i * 6 + (st - 1) * 2 + d + 1)
                        if st == 0:
                            ins = nc.vector.tensor_copy(flat, bank[:, 0:256])
                        else:
                            ins = nc.vector.tensor_tensor(flat, flat, bank[:, 0:256], ALU.add)
                        ins.then_inc(o_step, 1)
                    if st == 1:
                        z_silu(0)
                z_silu(1)

                dve.wait_ge(osq_ready, i + 1)
                nc.vector.tensor_reduce(ss[:], sq[:].rearrange("p a (t n) -> p (a t) n", n=P), AX.X, ALU.add).then_inc(oss_ready, 1)
                dve.wait_ge(oss_ready, 1 + i + 1)
                step(nc.vector.tensor_scalar(ss[:], ss[:], 4.0 / DH, 4.0 * RMS_EPS, ALU.mult, ALU.add))
                rsqrt(nc, step, rs[:], ss[:], nt[:])
                rb = rs[:].rearrange("p (t a) -> p t a", a=1).to_broadcast([P, 8, P])
                o8 = o[:].rearrange("p t h n -> p (t h) n")
                step(nc.vector.tensor_tensor(o8, o8, rb, ALU.mult))
                nc.vector.tensor_tensor(o8, o8, zs[:].rearrange("p t h n -> p (t h) n"), ALU.mult).then_inc(og_ready, 1)
                for n in range(8):
                    tt, half = n // 2, n % 2
                    bank = got(uses, f"y{n}", i)
                    y = res[:, tt, half * 512:(half + 1) * 512]
                    nc.vector.tensor_tensor(y, y, bank[:], ALU.add).then_inc(y_ready, 1)
                if with_next:
                    assert links["k"] == per, links["k"]

            links["base"] = links["k"]
            per = DN_DVE_STEPS
            with dve.Fori(0, NK - 1) as i:
                body(i, MAIN, True, per)
            body(NK - 1, LAST, False, per)


DN_DVE_STEPS = 4 * 4 + 1 + 4 + 24 + 1 + 2 + 2 * RSQRT_STEPS


class Steps:

    def __init__(self, dve, link):
        self.dve, self.link, self.k = dve, link, 0

    def __call__(self, ins):
        self.k += 1
        ins.then_inc(self.link, 1)
        self.dve.wait_ge(self.link, self.k)


def norm(nc, t, dram, gname, bname, layer, name, routed=True, out=None):
    c, ps, res, xT = t["const"], t["ps"], t["res"], t["xT"]
    ident = c[:, C_ID:C_ID + P]
    with ExitStack() as ctx:
        def sb(n, shape):
            return ctx.enter_context(nc.sbuf_tensor(f"{name}_{n}", shape, F32))

        sem = phase(nc, ctx, name + "_")

        g, b = sb("g", [P, D]), sb("b", [P, D])
        stats, mv = sb("stats", [P, TT, 2, 6]), sb("mv", [P, TT, 2])
        var, rstd, shift, nt = (sb(n, [P, TT]) for n in ("var", "rstd", "shift", "nt"))
        rows_in, stats_ready, scale_ready, scaled, normed, turned, xT_ready, stored, link = (
            sem(n) for n in ("rows_in", "stats_ready", "scale_ready", "scaled", "normed", "turned", "xT_ready", "stored", "link"))
        if routed:
            rw, rb = sb("rw", [P, KD, 16]), sb("rb", [P, 16])
            s, sel, e, w, chosen = (sb(n, [P, TT, 16]) for n in ("s", "sel", "e", "w", "chosen"))
            beat, tie = sb("beat", [P, 16, 4, 4]), sb("tie", [P, 16, 4, 4])
            cnt = sb("cnt", [P, 64])
            gs, gcnt, total = sb("gs", [P, TT, 4]), sb("gcnt", [P, 16]), sb("total", [P, TT])
            router_in, logits, e_ready = sem("router_in"), sem("logits"), sem("e_ready")
        block = ctx.enter_context(nc.Block())

        @block.sync
        def _(sp):
            sp.dma_start(g[:], dram[gname][layer].partition_broadcast(P)).then_inc(rows_in, 16)
            sp.dma_start(b[:], dram[bname][layer].partition_broadcast(P)).then_inc(rows_in, 16)
            if routed:
                sp.dma_start(rw[:], dram["router_w"].rearrange("(k p) e -> p k e", p=P)).then_inc(router_in, 16)
                sp.dma_start(rb[:], dram["router_bias"].partition_broadcast(P)).then_inc(router_in, 16)
            if out is not None:
                for tt in range(TT):
                    sp.wait_ge(normed, tt + 1)
                    sp.dma_start(out[0, tt * P:(tt + 1) * P], res[:, tt]).then_inc(stored, 16)
                sp.wait_ge(stored, 16 * TT)

        @block.scalar
        def _(act):
            for tt in range(TT):
                act.wait_ge(scale_ready, 1)
                act.activation(res[:, tt], res[:, tt], ACT.Identity, scale=rstd[:, tt:tt + 1], bias=shift[:, tt:tt + 1]).then_inc(scaled, 1)
            if out is None:
                for n in range(8):
                    tt, half = n // 2, n % 2
                    act.wait_ge(turned, n + 1)
                    act.copy(xT[:, half * 4:half * 4 + 4, tt * P:(tt + 1) * P], ps[n % 4][:].rearrange("p (k n) -> p k n", k=4)).then_inc(xT_ready, 1)
            if routed:
                act.wait_ge(logits, 1)
                act.activation(e[:].rearrange("p t e -> p (t e)"), ps[4][:, 0:64], ACT.Exp, scale=-1.0).then_inc(e_ready, 1)

        if out is None:
            @block.tensor
            def _(pe):
                for n in range(8):
                    tt, half = n // 2, n % 2
                    pe.wait_ge(normed, tt + 1)
                    if n >= 4:
                        pe.wait_ge(xT_ready, n - 3)
                    for k in range(4):
                        mm = pe.transpose(ps[n % 4][:, k * P:(k + 1) * P], res[:, tt, (half * 4 + k) * P:(half * 4 + k + 1) * P], ident)
                    mm.then_inc(turned, 1)
                if not routed:
                    return
                pe.wait_ge(router_in, 32)
                for tt in range(TT):
                    pe.wait_ge(xT_ready, 2 * tt + 2)
                    for k in range(KD):
                        mm = pe.matmul(ps[4][:, tt * 16:(tt + 1) * 16], xT[:, k, tt * P:(tt + 1) * P], rw[:, k], start=k == 0, stop=k == KD - 1)
                mm.then_inc(logits, 1)

        @block.vector
        def _(dve):
            step = Steps(dve, link)
            for tt in range(TT):
                for h in range(2):
                    ins = nc.vector.bn_stats(stats[:, tt, h], res[:, tt, h * 512:(h + 1) * 512])
                step(ins)
                ins = nc.vector.bn_aggr(mv[:, tt], stats[:, tt].rearrange("p h s -> p (h s)"))
            step(ins)
            step(nc.vector.tensor_scalar(var[:], mv[:, :, 1], LN_EPS, None, ALU.add))
            rsqrt(nc, step, rstd[:], var[:], nt[:])
            nc.vector.scalar_tensor_tensor(out=shift[:], in0=mv[:, :, 0], scalar=-1.0, in1=rstd[:], op0=ALU.mult, op1=ALU.mult).then_inc(scale_ready, 1)
            dve.wait_ge(rows_in, 32)
            for tt in range(TT):
                dve.wait_ge(scaled, tt + 1)
                step(nc.vector.tensor_tensor(res[:, tt], res[:, tt], g[:], ALU.mult))
                nc.vector.tensor_tensor(res[:, tt], res[:, tt], b[:], ALU.add).then_inc(normed, 1)
            if out is not None:
                return
            for tt in range(TT):
                dve.wait_ge(turned, 2 * tt + 2)
                dve.wait_ge(normed, tt + 1)
                step(nc.vector.tensor_scalar(res[:, tt], res[:, tt], ALPHA, None, ALU.mult))
            if not routed:
                return
            dve.wait_ge(e_ready, 1)
            dve.wait_ge(router_in, 32)
            step(nc.vector.tensor_scalar(e[:], e[:], 1.0, None, ALU.add))
            step(nc.vector.reciprocal(s[:], e[:]))
            step(nc.vector.tensor_tensor(sel[:], s[:], rb[:].rearrange("p (a e) -> p a e", a=1).to_broadcast([P, TT, 16]), ALU.add))

            def losses(values, n, count):
                one = values.rearrange("p (g a j) -> p g a j", a=1, j=4).to_broadcast([P, n, 4, 4])
                other = values.rearrange("p (g i a) -> p g i a", i=4, a=1).to_broadcast([P, n, 4, 4])
                flat = lambda a: a[:, 0:n].rearrange("p g i j -> p (g i) j")
                step(nc.vector.tensor_tensor(beat[:, 0:n], one, other, ALU.is_gt))
                step(nc.vector.tensor_tensor(tie[:, 0:n], one, other, ALU.is_equal))
                lower = c[:, C_JLT:C_JLT + 16].rearrange("p (a i) -> p a i", a=1).to_broadcast([P, n, 16])
                tied = tie[:, 0:n].rearrange("p g i j -> p g (i j)")
                step(nc.vector.tensor_tensor(tied, tied, lower, ALU.mult))
                step(nc.vector.tensor_tensor(beat[:, 0:n], beat[:, 0:n], tie[:, 0:n], ALU.add))
                step(nc.vector.tensor_reduce(count, flat(beat), AX.X, ALU.add))

            ch = chosen[:].rearrange("p t e -> p (t e)")
            losses(sel[:].rearrange("p t e -> p (t e)"), 16, cnt[:])
            step(nc.vector.tensor_scalar(ch, cnt[:], 2.0, None, ALU.is_lt))
            step(nc.vector.tensor_tensor(w[:], chosen[:], sel[:], ALU.mult))
            step(nc.vector.tensor_reduce(gs[:].rearrange("p t g -> p (t g)"), w[:].rearrange("p t (g e) -> p (t g) e", e=4), AX.X, ALU.add))
            losses(gs[:].rearrange("p t g -> p (t g)"), 4, gcnt[:])
            step(nc.vector.tensor_scalar(gcnt[:], gcnt[:], 1.0, None, ALU.is_lt))
            step(nc.vector.tensor_tensor(chosen[:].rearrange("p t (g e) -> p (t g) e", e=4), chosen[:].rearrange("p t (g e) -> p (t g) e", e=4),
                                         gcnt[:].rearrange("p (g a) -> p g a", a=1).to_broadcast([P, 16, 4]), ALU.mult))
            step(nc.vector.tensor_tensor(w[:], chosen[:], s[:], ALU.mult))
            step(nc.vector.tensor_reduce(total[:], w[:], AX.X, ALU.add))
            step(nc.vector.reciprocal(total[:], total[:]))
            step(nc.vector.tensor_tensor(t["gates"][:], w[:], total[:].rearrange("p (t a) -> p t a", a=1).to_broadcast([P, TT, 16]), ALU.mult))


NE, FF = 16, 256
CAP = 96
EXTRA = 2 * SEQ // (CAP + 1)
BLOCKS = NE + EXTRA
PIECES = (SEQ - 1) // CAP
RING = 3


def expert_rows(dram, layer):
    return (dram["moe_w_gate"][layer].rearrange("e (k p) f -> p e k f", p=P), dram["moe_w_up"][layer].rearrange("e (k p) f -> p e k f", p=P),
            dram["moe_w_down"][layer].rearrange("e (k p) n -> p e k n", p=P))


def mixture(nc, t, dram, gname, bname, layer, name):
    c, ps, res, xT = t["const"], t["ps"], t["res"], t["xT"]
    ident = c[:, C_ID:C_ID + P]
    with ExitStack() as ctx:
        def sb(n, shape, dt=F32):
            return ctx.enter_context(nc.sbuf_tensor(f"{name}_{n}", shape, dt))

        wgu, wd = sb("wgu", [P, RING, KD, 2, FF]), sb("wd", [P, RING, 2, D])
        x_rows, y_rows = sb("x_rows", [CAP, 3, D]), sb("y_rows", [CAP, 3, D])
        xgT = sb("xgT", [P, 3, KD, CAP])
        silu, hid, hidT = sb("silu", [CAP, FF]), sb("hid", [CAP, FF]), sb("hidT", [P, 2, CAP])
        counts = sb("counts", [1, 1], mybir.dt.uint32)
        owner = sb("owner", [1, EXTRA], mybir.dt.uint32)
        place, gate2 = sb("place", [P, 2, TT], mybir.dt.uint32), sb("gate2", [P, 2, TT])
        route_and_run(nc, t, dram, gname, bname, layer, name, locals())
        extra_blocks(nc, t, dram, layer, name, locals())
        combine(nc, t, name, locals())


def route_and_run(nc, t, dram, gname, bname, layer, name, m):
    c, ps, res, xT = t["const"], t["ps"], t["res"], t["xT"]
    ident, ones, before = c[:, C_ID:C_ID + P], c[:, C_ONE:C_ONE + P], c[:, C_SB:C_SB + P]
    wgu, wd, x_rows, y_rows, xgT, silu, hid, hidT = (m[n] for n in ("wgu", "wd", "x_rows", "y_rows", "xgT", "silu", "hid", "hidT"))
    place, gate2, counts, owner = m["place"], m["gate2"], m["counts"], m["owner"]
    slots_x, slots_y = t["slots_x"], t["slots_y"]
    g_dram, u_dram, d_dram = expert_rows(dram, layer)

    with ExitStack() as ctx:
        def sb(n, shape, dt=F32):
            return ctx.enter_context(nc.sbuf_tensor(f"{name}_{n}", shape, dt))

        sem = phase(nc, ctx, name + "_")
        g, b = sb("g", [P, D]), sb("b", [P, D])
        stats, mv = sb("stats", [P, TT, 2, 6]), sb("mv", [P, TT, 2])
        var, rstd, shift, nt = (sb(n, [P, TT]) for n in ("var", "rstd", "shift", "nt"))
        rw, rb = sb("rw", [P, KD, NE]), sb("rb", [P, NE])
        s, sel, decay, w, chosen = (sb(n, [P, TT, NE]) for n in ("s", "sel", "decay", "w", "chosen"))
        beat, tie = sb("beat", [P, 16, 4, 4]), sb("tie", [P, 16, 4, 4])
        cnt = sb("cnt", [P, 64])
        gs, gcnt, total = sb("gs", [P, TT, 4]), sb("gcnt", [P, 16]), sb("total", [P, TT])
        rank, piece, slot, moved = (sb(n, [P, TT, NE]) for n in ("rank", "piece", "slot", "moved"))
        load, extra, base, ends = (sb(n, [P, NE]) for n in ("load", "extra", "base", "ends"))
        below = sb("below", [P, NE, NE])
        slot2 = sb("slot2", [P, 2, TT])
        owner_f = sb("owner_f", [P, EXTRA])

        rows_in, router_in, stats_ready, scale_ready, scaled, normed, turned, xT_ready, logits, e_ready, link = (
            sem(n) for n in ("rows_in", "router_in", "stats_ready", "scale_ready", "scaled", "normed", "turned", "xT_ready", "logits", "e_ready", "link"))
        chosen_ready, ranked, place_ready, scattered = (sem(n) for n in ("chosen_ready", "ranked", "place_ready", "scattered"))
        gu_in, d_in = [sem(f"gu_in{n}") for n in range(RING)], [sem(f"d_in{n}") for n in range(RING)]
        rows_loaded, stored = [sem(f"rows_loaded{n}") for n in range(3)], [sem(f"stored{n}") for n in range(3)]
        rowsT_full, rowsT_ready = sem("rowsT_full"), [sem("rowsT_act"), sem("rowsT_dve")]
        gu_full, silu_ready, hid_ready, hidT_full, hidT_ready = (sem(n) for n in ("gu_full", "silu_ready", "hid_ready", "hidT_full", "hidT_ready"))
        down_full, y_ready = sem("down_full"), [sem("y_act"), sem("y_dve")]
        block = ctx.enter_context(nc.Block())

        def pick(a, e):
            return a[:, e] if isinstance(e, int) else a[:, bass.ds(e, 1)].rearrange("p a k f -> p (a k) f")

        def rows_of(a, e):
            return a[e * CAP:(e + 1) * CAP] if isinstance(e, int) else a[bass.ds(e * CAP, CAP)]

        @block.sync
        def _(sp):
            sp.dma_start(g[:], dram[gname][layer].partition_broadcast(P)).then_inc(rows_in, 16)
            sp.dma_start(b[:], dram[bname][layer].partition_broadcast(P)).then_inc(rows_in, 16)
            sp.dma_start(rw[:], dram["router_w"].rearrange("(k p) e -> p k e", p=P)).then_inc(router_in, 16)
            sp.dma_start(rb[:], dram["router_bias"].partition_broadcast(P)).then_inc(router_in, 16)

            def load_weights(e, r):
                late = not isinstance(e, int)
                if late:
                    sp.wait_ge(gu_full, e - RING + 1)
                sp.dma_start(wgu[:, r, :, 0], pick(g_dram, e)).then_inc(gu_in[r], 16)
                sp.dma_start(wgu[:, r, :, 1], pick(u_dram, e)).then_inc(gu_in[r], 16)
                if late:
                    sp.wait_ge(down_full, e - RING + 1)
                sp.dma_start(wd[:, r], pick(d_dram, e)).then_inc(d_in[r], 16)

            for e in range(RING):
                load_weights(e, e)
            with sp.Fori(1, NE // RING) as q:
                for r in range(RING):
                    load_weights(q * RING + r, r)
            for e in range(NE // RING * RING, NE):
                r = e % RING
                sp.wait_ge(gu_full, e - RING + 1)
                sp.dma_start(wgu[:, r, :, 0], pick(g_dram, e)).then_inc(gu_in[r], 16)
                sp.dma_start(wgu[:, r, :, 1], pick(u_dram, e)).then_inc(gu_in[r], 16)
                sp.wait_ge(down_full, e - RING + 1)
                sp.dma_start(wd[:, r], pick(d_dram, e)).then_inc(d_in[r], 16)

        @block.gpsimd
        def _(pool):
            pool.wait_ge(place_ready, 1)
            for k in range(2):
                for tt in range(TT):
                    nc.gpsimd.indirect_dma_start(slots_x, bass.IndirectOffsetOnAxis(place[:, k, tt:tt + 1], 0), res[:, tt], None,
                                                 bounds_check=BLOCKS * CAP - 1).then_inc(scattered, 16)

        @block.tensor
        def _(pe):
            for n in range(8):
                tt, half = n // 2, n % 2
                pe.wait_ge(normed, tt + 1)
                if n >= 4:
                    pe.wait_ge(xT_ready, n - 3)
                for k in range(4):
                    mm = pe.transpose(ps[n % 4][:, k * P:(k + 1) * P], res[:, tt, (half * 4 + k) * P:(half * 4 + k + 1) * P], ident)
                mm.then_inc(turned, 1)
            pe.wait_ge(router_in, 32)
            for tt in range(TT):
                pe.wait_ge(xT_ready, 2 * tt + 2)
                for k in range(KD):
                    mm = pe.matmul(ps[4][:, tt * NE:(tt + 1) * NE], xT[:, k, tt * P:(tt + 1) * P], rw[:, k], start=k == 0, stop=k == KD - 1)
            mm.then_inc(logits, 1)
            pe.wait_ge(chosen_ready, 1)
            for tt in range(TT):
                for other in range(tt):
                    pe.matmul(ps[5][:, tt * NE:(tt + 1) * NE], ones, chosen[:, other], start=other == 0, stop=False)
                pe.matmul(ps[5][:, tt * NE:(tt + 1) * NE], before, chosen[:, tt], start=tt == 0, stop=True)
            for tt in range(TT):
                mm = pe.matmul(ps[5][:, 64:64 + NE], ones, chosen[:, tt], start=tt == 0, stop=tt == TT - 1)
            mm.then_inc(ranked, 1)

            def turn_rows(e, r, n):
                pe.wait_ge(rows_loaded[r], (n + 1) * 16)
                if not (isinstance(e, int) and e == 0):
                    for half in range(2):
                        pe.wait_ge(rowsT_ready[half], e)
                for k in range(KD):
                    mm = pe.transpose(ps[k // 4][:, k % 4 * CAP:(k % 4 + 1) * CAP], x_rows[:, r, k * P:(k + 1) * P], ident[0:CAP, 0:CAP])
                    if k % 4 == 3:
                        mm.then_inc(rowsT_full, 1)

            def gate_up(e, r, n):
                pe.wait_ge(gu_in[r], (n + 1) * 32)
                for half in range(2):
                    pe.wait_ge(rowsT_ready[half], e + 1)
                for k in range(KD):
                    mm = pe.matmul(ps[2][0:CAP], xgT[:, r, k], wgu[:, r, k].rearrange("p a f -> p (a f)"), start=k == 0, stop=k == KD - 1)
                mm.then_inc(gu_full, 1)

            def turn_hidden(e):
                pe.wait_ge(hid_ready, e + 1)
                for f in range(2):
                    mm = pe.transpose(ps[3][:, f * CAP:(f + 1) * CAP], hid[:, f * P:(f + 1) * P], ident[0:CAP, 0:CAP])
                mm.then_inc(hidT_full, 1)

            def down(e, r, n, first=False):
                pe.wait_ge(d_in[r], (n + 1) * 16)
                pe.wait_ge(hidT_ready, e + 1)
                if not first:
                    pe.wait_ge(y_ready[0], e)
                    pe.wait_ge(y_ready[1], e)
                for half in range(2):
                    for f in range(2):
                        mm = pe.matmul(ps[4 + half][0:CAP], hidT[:, f], wd[:, r, f, half * 512:(half + 1) * 512], start=f == 0, stop=f == 1)
                mm.then_inc(down_full, 1)

            turn_rows(0, 0, 0)
            gate_up(0, 0, 0)
            turn_rows(1, 1, 0)
            def round_(q, first):
                for r in range(RING):
                    e = q * RING + r
                    turn_hidden(e)
                    gate_up(e + 1, (r + 1) % RING, q + (r + 1) // RING)
                    turn_rows(e + 2, (r + 2) % RING, q + (r + 2) // RING)
                    down(e, r, q, first and r == 0)
            round_(0, True)
            with pe.Fori(1, NE // RING) as q:
                round_(q, False)
            turn_hidden(NE - 1)
            down(NE - 1, (NE - 1) % RING, (NE - 1) // RING)

        @block.scalar
        def _(act):
            for tt in range(TT):
                act.wait_ge(scale_ready, 1)
                act.activation(res[:, tt], res[:, tt], ACT.Identity, scale=rstd[:, tt:tt + 1], bias=shift[:, tt:tt + 1]).then_inc(scaled, 1)
            for n in range(8):
                tt, half = n // 2, n % 2
                act.wait_ge(turned, n + 1)
                act.copy(xT[:, half * 4:half * 4 + 4, tt * P:(tt + 1) * P], ps[n % 4][:].rearrange("p (k n) -> p k n", k=4)).then_inc(xT_ready, 1)
            act.wait_ge(logits, 1)
            act.activation(decay[:].rearrange("p t e -> p (t e)"), ps[4][:, 0:64], ACT.Exp, scale=-1.0).then_inc(e_ready, 1)
            act.wait_ge(scattered, 16 * 2 * TT)

            def load_rows(e, r):
                act.dma_start(x_rows[:, r], rows_of(slots_x, e)).then_inc(rows_loaded[r], 16)

            def rowsT(e, r):
                act.wait_ge(rowsT_full, 2 * e + 1)
                act.copy(xgT[:, r, 0:4].rearrange("p k n -> p (k n)"), ps[0][:, 0:4 * CAP]).then_inc(rowsT_ready[0], 1)

            def activate(e):
                act.wait_ge(gu_full, e + 1)
                if not (isinstance(e, int) and e == 0):
                    act.wait_ge(hid_ready, e)
                act.activation(silu[:], ps[2][0:CAP, 0:FF], ACT.Silu).then_inc(silu_ready, 1)

            def results(e, r, n, first):
                act.wait_ge(down_full, e + 1)
                if not first:
                    act.wait_ge(stored[r], n * 16)
                act.copy(y_rows[:, r, 0:512], ps[4][0:CAP]).then_inc(y_ready[0], 1)
                act.wait_ge(y_ready[0], e + 1)
                act.wait_ge(y_ready[1], e + 1)
                act.dma_start(rows_of(slots_y, e), y_rows[:, r]).then_inc(stored[r], 16)

            for e in range(3):
                load_rows(e, e)
            rowsT(0, 0)
            rowsT(1, 1)
            activate(0)

            def round_(q, first):
                for r in range(RING):
                    e = q * RING + r
                    if not (isinstance(e, int) and e + 3 > NE):
                        if first or r < 2:
                            load_rows(e + 3, r)
                    rowsT(e + 2, (r + 2) % RING)
                    activate(e + 1)
                    results(e, r, q, first)
            round_(0, True)
            with act.Fori(1, NE // RING - 1) as q:
                for r in range(RING):
                    e = q * RING + r
                    load_rows(e + 3, r)
                    rowsT(e + 2, (r + 2) % RING)
                    activate(e + 1)
                    results(e, r, q, False)
            q = NE // RING - 1
            for r in range(RING):
                e = q * RING + r
                if e + 3 <= NE:
                    load_rows(e + 3, r)
                rowsT(e + 2, (r + 2) % RING)
                activate(e + 1)
                results(e, r, q, False)
            results(NE - 1, (NE - 1) % RING, (NE - 1) // RING, False)
            for r in range(RING):
                act.wait_ge(stored[r], 16 * len(range(r, NE, RING)))

        @block.vector
        def _(dve):
            step = Steps(dve, link)
            for tt in range(TT):
                for h in range(2):
                    ins = nc.vector.bn_stats(stats[:, tt, h], res[:, tt, h * 512:(h + 1) * 512])
                step(ins)
                ins = nc.vector.bn_aggr(mv[:, tt], stats[:, tt].rearrange("p h s -> p (h s)"))
            step(ins)
            step(nc.vector.tensor_scalar(var[:], mv[:, :, 1], LN_EPS, None, ALU.add))
            rsqrt(nc, step, rstd[:], var[:], nt[:])
            nc.vector.scalar_tensor_tensor(out=shift[:], in0=mv[:, :, 0], scalar=-1.0, in1=rstd[:], op0=ALU.mult, op1=ALU.mult).then_inc(scale_ready, 1)
            dve.wait_ge(rows_in, 32)
            for tt in range(TT):
                dve.wait_ge(scaled, tt + 1)
                step(nc.vector.tensor_tensor(res[:, tt], res[:, tt], g[:], ALU.mult))
                nc.vector.tensor_tensor(res[:, tt], res[:, tt], b[:], ALU.add).then_inc(normed, 1)
            dve.wait_ge(normed, TT)
            dve.wait_ge(e_ready, 1)
            dve.wait_ge(router_in, 32)
            step(nc.vector.tensor_scalar(decay[:], decay[:], 1.0, None, ALU.add))
            step(nc.vector.reciprocal(s[:], decay[:]))
            step(nc.vector.tensor_tensor(sel[:], s[:], rb[:].rearrange("p (a e) -> p a e", a=1).to_broadcast([P, TT, NE]), ALU.add))

            def losses(values, n, count):
                one = values.rearrange("p (g a j) -> p g a j", a=1, j=4).to_broadcast([P, n, 4, 4])
                other = values.rearrange("p (g i a) -> p g i a", i=4, a=1).to_broadcast([P, n, 4, 4])
                nc.vector.tensor_tensor(beat[:, 0:n], one, other, ALU.is_gt)
                step(nc.vector.tensor_tensor(tie[:, 0:n], one, other, ALU.is_equal))
                lower = c[:, C_JLT:C_JLT + 16].rearrange("p (a i) -> p a i", a=1).to_broadcast([P, n, 16])
                tied = tie[:, 0:n].rearrange("p g i j -> p g (i j)")
                step(nc.vector.tensor_tensor(tied, tied, lower, ALU.mult))
                step(nc.vector.tensor_tensor(beat[:, 0:n], beat[:, 0:n], tie[:, 0:n], ALU.add))
                step(nc.vector.tensor_reduce(count, beat[:, 0:n].rearrange("p g i j -> p (g i) j"), AX.X, ALU.add))

            ch = chosen[:].rearrange("p t e -> p (t e)")
            losses(sel[:].rearrange("p t e -> p (t e)"), 16, cnt[:])
            step(nc.vector.tensor_scalar(ch, cnt[:], 2.0, None, ALU.is_lt))
            step(nc.vector.tensor_tensor(w[:], chosen[:], sel[:], ALU.mult))
            step(nc.vector.tensor_reduce(gs[:].rearrange("p t g -> p (t g)"), w[:].rearrange("p t (g e) -> p (t g) e", e=4), AX.X, ALU.add))
            losses(gs[:].rearrange("p t g -> p (t g)"), 4, gcnt[:])
            step(nc.vector.tensor_scalar(gcnt[:], gcnt[:], 1.0, None, ALU.is_lt))
            in_group = chosen[:].rearrange("p t (g e) -> p (t g) e", e=4)
            nc.vector.tensor_tensor(in_group, in_group, gcnt[:].rearrange("p (g a) -> p g a", a=1).to_broadcast([P, 16, 4]), ALU.mult).then_inc(chosen_ready, 1)
            dve.wait_ge(chosen_ready, 1)
            step(nc.vector.tensor_tensor(w[:], chosen[:], s[:], ALU.mult))
            step(nc.vector.tensor_reduce(total[:], w[:], AX.X, ALU.add))
            step(nc.vector.reciprocal(total[:], total[:]))
            step(nc.vector.tensor_tensor(w[:], w[:], total[:].rearrange("p (t a) -> p t a", a=1).to_broadcast([P, TT, NE]), ALU.mult))

            dve.wait_ge(ranked, 1)
            nc.vector.tensor_copy(rank[:].rearrange("p t e -> p (t e)"), ps[5][:, 0:64])
            step(nc.vector.tensor_copy(load[:], ps[5][:, 64:64 + NE]))
            nc.vector.tensor_scalar(extra[:], load[:], float(CAP), None, ALU.is_gt)
            step(nc.vector.tensor_scalar(piece[:], rank[:], float(CAP), None, ALU.is_ge))
            for n in range(2, PIECES + 1):
                nc.vector.scalar_tensor_tensor(out=extra[:], in0=load[:], scalar=float(n * CAP), in1=extra[:], op0=ALU.is_gt, op1=ALU.add)
                flat = lambda a: a[:].rearrange("p t e -> p (t e)")
                step(nc.vector.scalar_tensor_tensor(out=flat(piece), in0=flat(rank), scalar=float(n * CAP), in1=flat(piece), op0=ALU.is_ge, op1=ALU.add))
            earlier = c[:, C_BELOW:C_BELOW + NE * NE].rearrange("p (a b) -> p a b", a=NE)
            step(nc.vector.tensor_tensor(below[:], earlier, extra[:].rearrange("p (a b) -> p a b", a=1).to_broadcast([P, NE, NE]), ALU.mult))
            step(nc.vector.tensor_reduce(base[:], below[:], AX.X, ALU.add))
            step(nc.vector.tensor_tensor(ends[:], base[:], extra[:], ALU.add))

            def over_tiles(a):
                return a.rearrange("p (a e) -> p a e", a=1).to_broadcast([P, TT, NE])

            number = c[:, C_NUM:C_NUM + NE]
            step(nc.vector.tensor_tensor(base[:], base[:], number, ALU.subtract))
            step(nc.vector.tensor_tensor(moved[:], piece[:], over_tiles(base[:]), ALU.add))
            step(nc.vector.tensor_scalar(moved[:], moved[:], float(NE - 1), None, ALU.add))
            step(nc.vector.tensor_scalar(slot[:], piece[:], 1.0, None, ALU.is_ge))
            step(nc.vector.tensor_tensor(slot[:], slot[:], moved[:], ALU.mult))
            step(nc.vector.tensor_tensor(slot[:], slot[:], over_tiles(number), ALU.add))
            step(nc.vector.tensor_tensor(slot[:], slot[:], piece[:], ALU.subtract))
            step(nc.vector.scalar_tensor_tensor(out=flat(slot), in0=flat(slot), scalar=float(CAP), in1=flat(rank), op0=ALU.mult, op1=ALU.add))
            big = float(BLOCKS * CAP)
            step(nc.vector.scalar_tensor_tensor(out=flat(moved), in0=flat(slot), scalar=1.0, in1=flat(chosen), op0=ALU.add, op1=ALU.mult))
            nc.vector.tensor_reduce(slot2[:, 0], moved[:], AX.X, ALU.max)
            step(nc.vector.tensor_scalar(rank[:], slot[:], -1.0, big, ALU.mult, ALU.add))
            step(nc.vector.tensor_tensor(rank[:], rank[:], chosen[:], ALU.mult))
            step(nc.vector.tensor_reduce(slot2[:, 1], rank[:], AX.X, ALU.max))
            nc.vector.tensor_scalar(slot2[:, 0], slot2[:, 0], -1.0, None, ALU.add)
            step(nc.vector.tensor_scalar(slot2[:, 1], slot2[:, 1], -1.0, big, ALU.mult, ALU.add))
            nc.vector.tensor_copy(place[:], slot2[:]).then_inc(place_ready, 1)
            for k in range(2):
                at = slot2[:, k].rearrange("p (t a) -> p t a", a=1).to_broadcast([P, TT, NE])
                step(nc.vector.tensor_tensor(moved[:], slot[:], at, ALU.is_equal))
                step(nc.vector.tensor_tensor(moved[:], moved[:], w[:], ALU.mult))
                step(nc.vector.tensor_reduce(gate2[:, k], moved[:], AX.X, ALU.add))
            for n in range(EXTRA):
                ins = nc.vector.tensor_scalar(below[:, n], ends[:], float(n), None, ALU.is_le)
            step(ins)
            step(nc.vector.tensor_reduce(owner_f[:], below[:, 0:EXTRA], AX.X, ALU.add))
            step(nc.vector.tensor_scalar(owner_f[:], owner_f[:], float(NE - 1), None, ALU.min))
            nc.vector.tensor_copy(owner[:], owner_f[0:1])
            nc.vector.tensor_copy(counts[:], ends[0:1, NE - 1:NE])
            dve.wait_ge(scattered, 16 * 2 * TT)
            dve.wait_ge(turned, 8)
            for tt in range(TT):
                nc.vector.tensor_scalar(res[:, tt], res[:, tt], ALPHA, None, ALU.mult)

            def rowsT(e, r):
                dve.wait_ge(rowsT_full, 2 * e + 2)
                nc.vector.tensor_copy(xgT[:, r, 4:8].rearrange("p k n -> p (k n)"), ps[1][:, 0:4 * CAP]).then_inc(rowsT_ready[1], 1)

            def hidden(e):
                dve.wait_ge(silu_ready, e + 1)
                nc.vector.tensor_tensor(hid[:], silu[:], ps[2][0:CAP, FF:2 * FF], ALU.mult).then_inc(hid_ready, 1)

            def hiddenT(e):
                dve.wait_ge(hidT_full, e + 1)
                nc.vector.tensor_copy(hidT[:].rearrange("p f n -> p (f n)"), ps[3][:, 0:2 * CAP]).then_inc(hidT_ready, 1)

            def results(e, r, n, first):
                dve.wait_ge(down_full, e + 1)
                if not first:
                    dve.wait_ge(stored[r], n * 16)
                nc.vector.tensor_copy(y_rows[:, r, 512:1024], ps[5][0:CAP]).then_inc(y_ready[1], 1)

            rowsT(0, 0)
            rowsT(1, 1)
            hidden(0)

            def round_(q, first):
                for r in range(RING):
                    e = q * RING + r
                    hiddenT(e)
                    rowsT(e + 2, (r + 2) % RING)
                    hidden(e + 1)
                    results(e, r, q, first)
            round_(0, True)
            with dve.Fori(1, NE // RING) as q:
                round_(q, False)
            hiddenT(NE - 1)
            results(NE - 1, (NE - 1) % RING, (NE - 1) // RING, False)


def extra_blocks(nc, t, dram, layer, name, m):
    c, ps = t["const"], t["ps"]
    ident = c[:, C_ID:C_ID + P]
    wgu, wd, x_rows, y_rows, xgT, silu, hid, hidT, owner, counts = (m[n] for n in ("wgu", "wd", "x_rows", "y_rows", "xgT", "silu", "hid", "hidT", "owner", "counts"))
    g_dram, u_dram, d_dram = expert_rows(dram, layer)
    with ExitStack() as ctx:
        sem = phase(nc, ctx, name + "_x_")
        block_in, stored, rowsT_full, rowsT_ready, gu_full, silu_ready, hid_ready, hidT_full, hidT_ready, down_full, y_ready = (
            sem(n) for n in ("block_in", "stored", "rowsT_full", "rowsT_ready", "gu_full", "silu_ready", "hid_ready", "hidT_full", "hidT_ready", "down_full", "y_ready"))
        block = ctx.enter_context(nc.Block())

        def crowded(engine):
            return engine.value_load(counts[0:1, 0:1], min_val=0, max_val=EXTRA) > 0

        @block.sync
        def _(sp):
            with sp.If(crowded(sp)):
                sp.sem_inc(stored, 1)
                with sp.Fori(0, EXTRA) as n:
                    sp.wait_ge(stored, 1 + n * 16)
                    e = sp.value_load(owner[0:1, bass.ds(n, 1)], min_val=0, max_val=NE - 1)
                    pick = lambda a: a[:, bass.ds(e, 1)].rearrange("p a k f -> p (a k) f")
                    sp.dma_start(wgu[:, 0, :, 0], pick(g_dram)).then_inc(block_in, 16)
                    sp.dma_start(wgu[:, 0, :, 1], pick(u_dram)).then_inc(block_in, 16)
                    sp.dma_start(wd[:, 0], pick(d_dram)).then_inc(block_in, 16)
                    sp.dma_start(x_rows[:, 0], t["slots_x"][bass.ds((n + NE) * CAP, CAP)]).then_inc(block_in, 16)
                    sp.wait_ge(y_ready, n + 1)
                    sp.dma_start(t["slots_y"][bass.ds((n + NE) * CAP, CAP)], y_rows[:, 0]).then_inc(stored, 16)
                sp.wait_ge(stored, 1 + EXTRA * 16)

        @block.tensor
        def _(pe):
            with pe.If(crowded(pe)):
                with pe.Fori(0, EXTRA) as n:
                    pe.wait_ge(block_in, (n + 1) * 64)
                    for k in range(KD):
                        mm = pe.transpose(ps[k // 4][:, k % 4 * CAP:(k % 4 + 1) * CAP], x_rows[:, 0, k * P:(k + 1) * P], ident[0:CAP, 0:CAP])
                    mm.then_inc(rowsT_full, 1)
                    pe.wait_ge(rowsT_ready, n + 1)
                    for k in range(KD):
                        mm = pe.matmul(ps[2][0:CAP], xgT[:, 0, k], wgu[:, 0, k].rearrange("p a f -> p (a f)"), start=k == 0, stop=k == KD - 1)
                    mm.then_inc(gu_full, 1)
                    pe.wait_ge(hid_ready, n + 1)
                    for f in range(2):
                        mm = pe.transpose(ps[3][:, f * CAP:(f + 1) * CAP], hid[:, f * P:(f + 1) * P], ident[0:CAP, 0:CAP])
                    mm.then_inc(hidT_full, 1)
                    pe.wait_ge(hidT_ready, n + 1)
                    for half in range(2):
                        for f in range(2):
                            mm = pe.matmul(ps[4 + half][0:CAP], hidT[:, f], wd[:, 0, f, half * 512:(half + 1) * 512], start=f == 0, stop=f == 1)
                    mm.then_inc(down_full, 1)

        @block.scalar
        def _(act):
            with act.If(crowded(act)):
                with act.Fori(0, EXTRA) as n:
                    act.wait_ge(gu_full, n + 1)
                    act.activation(silu[:], ps[2][0:CAP, 0:FF], ACT.Silu).then_inc(silu_ready, 1)

        @block.vector
        def _(dve):
            with dve.If(crowded(dve)):
                with dve.Fori(0, EXTRA) as n:
                    dve.wait_ge(rowsT_full, n + 1)
                    for half in range(2):
                        ins = nc.vector.tensor_copy(xgT[:, 0, half * 4:half * 4 + 4].rearrange("p k n -> p (k n)"), ps[half][:, 0:4 * CAP])
                    ins.then_inc(rowsT_ready, 1)
                    dve.wait_ge(silu_ready, n + 1)
                    nc.vector.tensor_tensor(hid[:], silu[:], ps[2][0:CAP, FF:2 * FF], ALU.mult).then_inc(hid_ready, 1)
                    dve.wait_ge(hidT_full, n + 1)
                    nc.vector.tensor_copy(hidT[:].rearrange("p f n -> p (f n)"), ps[3][:, 0:2 * CAP]).then_inc(hidT_ready, 1)
                    dve.wait_ge(down_full, n + 1)
                    for half in range(2):
                        ins = nc.vector.tensor_copy(y_rows[:, 0, half * 512:(half + 1) * 512], ps[4 + half][0:CAP])
                    ins.then_inc(y_ready, 1)


def combine(nc, t, name, m):
    res, place, gate2 = t["res"], m["place"], m["gate2"]
    with ExitStack() as ctx:
        sem = phase(nc, ctx, name + "_c_")
        fetched_rows = ctx.enter_context(nc.sbuf_tensor(f"{name}_fetched", [P, 2, TT, D], F32))
        fetched = [[sem(f"fetched{k}{n}") for n in range(TT)] for k in range(2)]
        added = sem("added")
        block = ctx.enter_context(nc.Block())

        @block.gpsimd
        def _(pool):
            for tt in range(TT):
                for k in range(2):
                    nc.gpsimd.indirect_dma_start(fetched_rows[:, k, tt], None, t["slots_y"], bass.IndirectOffsetOnAxis(place[:, k, tt:tt + 1], 0),
                                                 bounds_check=BLOCKS * CAP - 1).then_inc(fetched[k][tt], 16)

        @block.vector
        def _(dve):
            for tt in range(TT):
                for k in range(2):
                    dve.wait_ge(fetched[k][tt], 16)
                    if k:
                        dve.wait_ge(added, tt + 1)
                    ins = nc.vector.scalar_tensor_tensor(out=res[:, tt], in0=fetched_rows[:, k, tt], scalar=gate2[:, k, tt:tt + 1], in1=res[:, tt], op0=ALU.mult, op1=ALU.add)
                    if k == 0:
                        ins.then_inc(added, 1)


NH, NOPE, ROPE, QR, KVR = 8, 128, 64, 384, 256
KQ_, KKV = QR // P, KVR // P


def mla_uses(first):
    names = [("qr", 0), ("qn", 1), ("kn", 2), ("v", 3), ("qrT", 0)] + [(f"S{n}", 4 + n) for n in range(4)]
    if not first:
        names += [(f"y{n}", n % 4) for n in range(8)]
    return Uses(names + [(f"T{n}", n) for n in range(4)] + [("pv", 4)])


def latent_attention(nc, t, dram):
    c, ps, res, xT = t["const"], t["ps"], t["res"], t["xT"]
    ident = c[:, C_ID:C_ID + P]
    FIRST, MAIN = mla_uses(True), mla_uses(False)
    scale = (NOPE + ROPE) ** -0.5
    with ExitStack() as ctx:
        def sb(n, shape, dt=F32):
            return ctx.enter_context(nc.sbuf_tensor(f"mla_{n}", shape, dt))

        sem = phase(nc, ctx, "mla_")

        W = QR + KVR + ROPE
        w_in, h = sb("win", [P, KD, W]), sb("h", [P, TT, W])
        junk = sb("junk", [P, QR])
        pos_i, pos = sb("pos_i", [P, TT], mybir.dt.int32), sb("pos", [P, TT])
        ang, turns, sin, cos = (sb(n, [P, TT, 32]) for n in ("ang", "turns", "sin", "cos"))
        ss, rs, nt = (sb(n, [P, 2 * TT]) for n in ("ss", "rs", "nt"))
        qw, kvw = sb("qw", [P, KQ_]), sb("kvw", [P, KKV])
        cqT, ckvT, krT = sb("cqT", [P, KQ_, SEQ]), sb("ckvT", [P, KKV, SEQ]), sb("krT", [P, SEQ])
        kr = sb("kr", [P, TT, 2, ROPE])
        rt = sb("rt", [P, 4, TT, 32])
        wq, wkv, wo = sb("wq", [P, KQ_, NOPE + ROPE]), sb("wkv", [P, KKV, 2 * P]), sb("wo", [P, D])
        qnT, knT, v = sb("qnT", [P, SEQ]), sb("knT", [P, SEQ]), sb("v", [P, TT, P])
        qr, qrT = sb("qr", [P, TT, ROPE]), sb("qrT", [P, 2, P])
        mx, nb, sums, inv = (sb(n, [P, TT]) for n in ("mx", "nb", "sums", "inv"))
        p, pT, oT = sb("p", [P, TT, SEQ]), sb("pT", [P, TT, SEQ]), sb("oT", [P, SEQ])

        full = [sem(f"full{b}") for b in range(8)]
        w_loaded, small_in = sem("w_loaded"), sem("small_in")
        wq_in, wkv_in, wo_in = sem("wq_in"), sem("wkv_in"), sem("wo_in")
        h_full, h_ready, sq_ready, norm_ready, kr_ready, cT_full, cT_ready, krT_ready = (
            sem(n) for n in ("h_full", "h_ready", "sq_ready", "norm_ready", "kr_ready", "cT_full", "cT_ready", "krT_ready"))
        ang_ready, trig_ready, link = sem("ang_ready"), sem("trig_ready"), sem("link")
        rope_read, qr_ready, qrT_ready, kv_ready, nb_ready, p_ready, pn_ready, oT_ready, y_ready = (
            sem(n) for n in ("rope_read", "qr_ready", "qrT_ready", "kv_ready", "nb_ready", "p_ready", "pn_ready", "oT_ready", "y_ready"))
        pT_ready = [sem("pT_ready_act"), sem("pT_ready_dve")]
        block = ctx.enter_context(nc.Block())

        base = {b: FIRST.per[b] - MAIN.per[b] for b in range(8)}

        def nth(uses, name, i):
            b, k = uses.at[name]
            return b, (k if isinstance(i, int) and i == 0 else base[b] + i * MAIN.per[b] + k)

        def read_of(name, i):
            n = int(name[-1]) if name[-1].isdigit() else 0
            if name[0] == "S":
                return p_ready, 4 * i + n + 1
            if name[0] == "T":
                return pT_ready[n % 2], 2 * i + n // 2 + 1
            if name[0] == "y":
                return y_ready, 1 + 8 * (i - 1) + n + 1
            return {"qr": (rope_read, i + 1), "qn": (kv_ready, 3 * i + 1), "kn": (kv_ready, 3 * i + 2), "v": (kv_ready, 3 * i + 3),
                    "qrT": (qrT_ready, i + 1), "pv": (oT_ready, i + 1)}[name]

        last_read = {b: (pT_ready[b % 2], 2) for b in range(4)} | {4: (oT_ready, 1)} | {b: (p_ready, 4) for b in (5, 6, 7)}

        def rotate(step, out, x, last):
            a, b = x[:, :, 0:32], x[:, :, 32:64]
            step(nc.vector.tensor_tensor(rt[:, 0], a, cos[:], ALU.mult))
            step(nc.vector.tensor_tensor(rt[:, 1], b, sin[:], ALU.mult))
            step(nc.vector.tensor_tensor(rt[:, 2], b, cos[:], ALU.mult))
            last(nc.vector.tensor_tensor(rt[:, 3], a, sin[:], ALU.mult))
            step(nc.vector.tensor_tensor(out[:, :, 0:32], rt[:, 0], rt[:, 1], ALU.subtract))
            return nc.vector.tensor_tensor(out[:, :, 32:64], rt[:, 2], rt[:, 3], ALU.add)

        @block.sync
        def _(sp):
            src = dram["mla_w_in"][0].rearrange("(k p) n -> p k n", p=P)
            sp.dma_start(w_in[:], src).then_inc(w_loaded, 16)
            sp.dma_start(pos_i[:], dram["positions"][0].rearrange("(t p) -> p t", p=P), allow_slow_non_contiguous=True).then_inc(small_in, 16)
            sp.dma_start(qw[:], dram["mla_q_norm"][0].rearrange("(k p) -> p k", p=P), allow_slow_non_contiguous=True).then_inc(small_in, 16)
            sp.dma_start(kvw[:], dram["mla_kv_norm"][0].rearrange("(k p) -> p k", p=P), allow_slow_non_contiguous=True).then_inc(small_in, 16)
            q_dram = dram["mla_w_qb"][0].rearrange("(k p) n -> p k n", p=P)
            kv_dram = dram["mla_w_kvb"][0].rearrange("(k p) n -> p k n", p=P)
            o_dram = dram["mla_w_out"][0]

            def load(i):
                if isinstance(i, int):
                    q, kv, o = q_dram[:, :, 0:192], kv_dram[:, :, 0:256], o_dram[0:P]
                else:
                    q, kv, o = q_dram[:, :, bass.ds(i * 192, 192)], kv_dram[:, :, bass.ds(i * 256, 256)], o_dram[bass.ds(i * P, P)]
                    sp.wait_ge(kv_ready, 3 * i)
                    sp.wait_ge(qrT_ready, i)
                sp.dma_start(wq[:], q).then_inc(wq_in, 16)
                sp.dma_start(wkv[:], kv).then_inc(wkv_in, 16)
                if not isinstance(i, int):
                    sp.wait_ge(y_ready, 1 + 8 * i)
                sp.dma_start(wo[:], o).then_inc(wo_in, 16)

            load(0)
            with sp.Fori(1, NH) as i:
                load(i)

        @block.tensor
        def _(pe):
            pe.wait_ge(w_loaded, 16)
            for tt in range(TT):
                for half in range(2):
                    for k in range(KD):
                        mm = pe.matmul(ps[2 * tt + half][:, 0:352], xT[:, k, tt * P:(tt + 1) * P], w_in[:, k, half * 352:(half + 1) * 352], start=k == 0, stop=k == KD - 1)
                mm.then_inc(h_full, 1)
            pe.wait_ge(h_ready, TT)
            for tt in range(TT):
                pe.wait_ge(norm_ready, tt + 1)
                if tt:
                    pe.wait_ge(cT_ready, 2 * tt)
                for k in range(KQ_):
                    mm = pe.transpose(ps[0][:, k * P:(k + 1) * P], h[:, tt, k * P:(k + 1) * P], ident)
                mm.then_inc(cT_full, 1)
                for k in range(KKV):
                    mm = pe.transpose(ps[1][:, k * P:(k + 1) * P], h[:, tt, QR + k * P:QR + (k + 1) * P], ident)
                mm.then_inc(cT_full, 1)
            pe.wait_ge(kr_ready, 1)
            for tt in range(TT):
                mm = pe.transpose(ps[2][:, tt * P:(tt + 1) * P], kr[:, tt].rearrange("p a n -> p (a n)"), ident)
            mm.then_inc(cT_full, 1)
            pe.wait_ge(cT_ready, 2 * TT)
            pe.wait_ge(krT_ready, 1)

            def body(i, uses, first):
                def begin(name):
                    b, k = uses.at[name]
                    if k:
                        pe.wait_ge(*read_of(uses.before[name], i))
                    elif not first:
                        signal, per = last_read[b]
                        pe.wait_ge(signal, i * per)
                    return ps[b]

                def done(mm, name):
                    mm.then_inc(full[uses.at[name][0]], 1)

                pe.wait_ge(wq_in, (i + 1) * 16)
                bank = begin("qr")
                for tt in range(TT):
                    for k in range(KQ_):
                        mm = pe.matmul(bank[:, tt * 64:(tt + 1) * 64], cqT[:, k, tt * P:(tt + 1) * P], wq[:, k, NOPE:NOPE + ROPE], start=k == 0, stop=k == KQ_ - 1)
                done(mm, "qr")
                bank = begin("qn")
                for k in range(KQ_):
                    mm = pe.matmul(bank[:], wq[:, k, 0:NOPE], cqT[:, k], start=k == 0, stop=k == KQ_ - 1)
                done(mm, "qn")
                pe.wait_ge(wkv_in, (i + 1) * 16)
                bank = begin("kn")
                for k in range(KKV):
                    mm = pe.matmul(bank[:], wkv[:, k, 0:P], ckvT[:, k], start=k == 0, stop=k == KKV - 1)
                done(mm, "kn")
                bank = begin("v")
                for tt in range(TT):
                    for k in range(KKV):
                        mm = pe.matmul(bank[:, tt * P:(tt + 1) * P], ckvT[:, k, tt * P:(tt + 1) * P], wkv[:, k, P:2 * P], start=k == 0, stop=k == KKV - 1)
                done(mm, "v")
                pe.wait_ge(qr_ready, i + 1)
                bank = begin("qrT")
                for n in range(2):
                    mm = pe.transpose(bank[:, n * P:(n + 1) * P], qr[:, 2 * n:2 * n + 2].rearrange("p a n -> p (a n)"), ident)
                done(mm, "qrT")
                pe.wait_ge(kv_ready, 3 * i + 2)
                pe.wait_ge(qrT_ready, i + 1)
                for n in range(TT):
                    bank = begin(f"S{n}")
                    pe.matmul(bank[:], qnT[:, n * P:(n + 1) * P], knT[:], start=True, stop=False)
                    half = slice(ROPE * (n % 2), ROPE * (n % 2) + ROPE)
                    done(pe.matmul(bank[:], qrT[half, n // 2], krT[half], start=False, stop=True), f"S{n}")
                if not first:
                    pe.wait_ge(wo_in, i * 16)
                    output(begin, done, i)
                for n in range(TT):
                    pe.wait_ge(pn_ready, 4 * i + n + 1)
                    bank = begin(f"T{n}")
                    for k in range(TT):
                        mm = pe.transpose(bank[:, k * P:(k + 1) * P], p[:, n, k * P:(k + 1) * P], ident)
                    done(mm, f"T{n}")
                for n in range(2):
                    pe.wait_ge(pT_ready[n], 2 * i + 2)
                pe.wait_ge(kv_ready, 3 * i + 3)
                bank = begin("pv")
                for k in range(TT):
                    mm = pe.matmul(bank[:], v[:, k], pT[:, k], start=k == 0, stop=k == TT - 1)
                done(mm, "pv")

            def output(begin, done, i):
                pe.wait_ge(oT_ready, i)
                for n in range(8):
                    tt, half = n // 2, n % 2
                    done(pe.matmul(begin(f"y{n}")[:], oT[:, tt * P:(tt + 1) * P], wo[:, half * 512:(half + 1) * 512], start=True, stop=True), f"y{n}")

            body(0, FIRST, True)
            with pe.Fori(1, NH) as i:
                body(i, MAIN, False)
            pe.wait_ge(wo_in, NH * 16)
            pe.wait_ge(oT_ready, NH)
            for n in range(8):
                tt, half = n // 2, n % 2
                if n >= 4:
                    pe.wait_ge(y_ready, 1 + 8 * (NH - 1) + n - 3)
                else:
                    pe.wait_ge(pT_ready[n % 2], 2 * NH)
                pe.matmul(ps[n % 4][:], oT[:, tt * P:(tt + 1) * P], wo[:, half * 512:(half + 1) * 512], start=True, stop=True).then_inc(full[n % 4], 1)

        @block.scalar
        def _(act):
            act.wait_ge(ang_ready, 1)
            act.activation(sin[:], ang[:], ACT.Sin).then_inc(trig_ready, 1)
            act.activation(cos[:], turns[:], ACT.Sin).then_inc(trig_ready, 1)
            for tt in range(TT):
                act.wait_ge(h_full, tt + 1)
                for half in range(2):
                    ins = act.copy(h[:, tt, half * 352:(half + 1) * 352], ps[2 * tt + half][:, 0:352])
                ins.then_inc(h_ready, 1)
                act.wait_ge(h_ready, tt + 1)
                act.activation(junk[:], h[:, tt, 0:QR], ACT.Square, accum_out=ss[:, tt:tt + 1]).then_inc(sq_ready, 1)
                act.wait_ge(sq_ready, 2 * tt + 1)
                act.activation(junk[:, 0:KVR], h[:, tt, QR:QR + KVR], ACT.Square, accum_out=ss[:, TT + tt:TT + tt + 1]).then_inc(sq_ready, 1)
                act.wait_ge(sq_ready, 2 * tt + 2)
            act.wait_ge(small_in, 48)
            for tt in range(TT):
                act.wait_ge(cT_full, 2 * tt + 1)
                for k in range(KQ_):
                    ins = act.mul(cqT[:, k, tt * P:(tt + 1) * P], ps[0][:, k * P:(k + 1) * P], qw[:, k:k + 1])
                ins.then_inc(cT_ready, 1)
                act.wait_ge(cT_full, 2 * tt + 2)
                for k in range(KKV):
                    ins = act.mul(ckvT[:, k, tt * P:(tt + 1) * P], ps[1][:, k * P:(k + 1) * P], kvw[:, k:k + 1])
                ins.then_inc(cT_ready, 1)
            act.wait_ge(cT_full, 2 * TT + 1)
            act.copy(krT[:], ps[2][:]).then_inc(krT_ready, 1)

            pre = {0: 0}

            def body(i, uses):
                def got(name):
                    b, n = nth(uses, name, i)
                    act.wait_ge(full[b], n + 1)
                    return ps[b]

                act.copy(qnT[:], got("qn")[:]).then_inc(kv_ready, 1)
                act.copy(knT[:], got("kn")[:]).then_inc(kv_ready, 1)
                act.copy(v[:].rearrange("p t n -> p (t n)"), got("v")[:]).then_inc(kv_ready, 1)
                for n in range(TT):
                    act.wait_ge(nb_ready, 4 * i + n + 1)
                    bank = ps[4 + n]
                    act.activation(p[:, n], bank[:], ACT.Exp, scale=scale, bias=nb[:, n:n + 1], accum_out=sums[:, n:n + 1]).then_inc(p_ready, 1)
                for n in (0, 2):
                    bank = got(f"T{n}")
                    act.copy(pT[:, :, n * P:(n + 1) * P], bank[:].rearrange("p (k n) -> p k n", k=TT)).then_inc(pT_ready[0], 1)
                act.copy(oT[:], got("pv")[:]).then_inc(oT_ready, 1)

            body(0, FIRST)
            with act.Fori(1, NH) as i:
                body(i, MAIN)

        @block.vector
        def _(dve):
            state = {"base": 0, "i": 0, "per": 0, "k": 0}

            def step(ins):
                state["k"] += 1
                ins.then_inc(link, 1)
                dve.wait_ge(link, state["base"] + state["i"] * state["per"] + state["k"])

            dve.sem_inc(y_ready, 1)
            dve.wait_ge(small_in, 48)
            step(nc.vector.tensor_copy(pos[:], pos_i[:]))
            step(nc.vector.tensor_tensor(ang[:], pos[:].rearrange("p (t a) -> p t a", a=1).to_broadcast([P, TT, 32]),
                                         c[:, C_FREQ:C_FREQ + 32].rearrange("p (a f) -> p a f", a=1).to_broadcast([P, TT, 32]), ALU.mult))
            big = 12582912.0
            step(nc.vector.tensor_scalar(turns[:], ang[:], float(1 / (2 * np.pi)), big, ALU.mult, ALU.add))
            step(nc.vector.tensor_scalar(turns[:], turns[:], big, None, ALU.subtract))
            for part in TWO_PI:
                step(nc.vector.scalar_tensor_tensor(out=ang[:], in0=turns[:], scalar=-part, in1=ang[:], op0=ALU.mult, op1=ALU.add))
            pi = float(np.nextafter(np.float32(np.pi), np.float32(0)))
            step(nc.vector.tensor_scalar(turns[:], ang[:], float(np.pi / 2), None, ALU.add))
            step(nc.vector.tensor_scalar(rt[:, 0], turns[:], pi, None, ALU.is_gt))
            step(nc.vector.scalar_tensor_tensor(out=turns[:], in0=rt[:, 0], scalar=float(-2 * np.pi), in1=turns[:], op0=ALU.mult, op1=ALU.add))
            step(nc.vector.tensor_scalar(turns[:], turns[:], pi, -pi, ALU.min, ALU.max))
            nc.vector.tensor_scalar(ang[:], ang[:], pi, -pi, ALU.min, ALU.max).then_inc(ang_ready, 1)
            dve.wait_ge(trig_ready, 2)
            dve.wait_ge(h_ready, TT)
            step(rotate(step, kr[:, :, 0], h[:, :, QR + KVR:], step))
            nc.vector.tensor_copy(kr[:, :, 1], kr[:, :, 0]).then_inc(kr_ready, 1)
            dve.wait_ge(sq_ready, 2 * TT)
            step(nc.vector.tensor_scalar(ss[:, 0:TT], ss[:, 0:TT], 1.0 / QR, RMS_EPS, ALU.mult, ALU.add))
            step(nc.vector.tensor_scalar(ss[:, TT:], ss[:, TT:], 1.0 / KVR, RMS_EPS, ALU.mult, ALU.add))
            rsqrt(nc, step, rs[:], ss[:], nt[:])
            for tt in range(TT):
                nc.vector.tensor_scalar(h[:, tt, 0:QR], h[:, tt, 0:QR], rs[:, tt:tt + 1], None, ALU.mult)
                nc.vector.tensor_scalar(h[:, tt, QR:QR + KVR], h[:, tt, QR:QR + KVR], rs[:, TT + tt:TT + tt + 1], None, ALU.mult).then_inc(norm_ready, 1)

            def add_output(i, n, b):
                y = res[:, n // 2, (n % 2) * 512:(n % 2 + 1) * 512]
                nc.vector.tensor_tensor(y, y, ps[b][:], ALU.add).then_inc(y_ready, 1)

            def body(i, uses, first):
                def got(name):
                    b, n = nth(uses, name, i)
                    dve.wait_ge(full[b], n + 1)
                    return ps[b]

                def read(ins):
                    ins.then_inc(rope_read, 1)
                    dve.wait_ge(rope_read, i + 1)

                bank = got("qr")
                rotate(step, qr, bank[:, 0:TT * ROPE].rearrange("p (t n) -> p t n", t=TT), read).then_inc(qr_ready, 1)
                nc.vector.tensor_copy(qrT[:].rearrange("p a n -> p (a n)"), got("qrT")[:, 0:2 * P]).then_inc(qrT_ready, 1)
                for n in range(TT):
                    bank = got(f"S{n}")
                    step(nc.vector.tensor_reduce(mx[:, n:n + 1], bank[:], AX.X, ALU.max))
                    nc.vector.tensor_scalar(nb[:, n:n + 1], mx[:, n:n + 1], -scale, None, ALU.mult).then_inc(nb_ready, 1)
                if not first:
                    for n in range(8):
                        got(f"y{n}")
                        if n == 0:
                            dve.wait_ge(y_ready, 1 + 8 * (i - 1))
                        add_output(i - 1, n, n % 4)
                for n in range(TT):
                    dve.wait_ge(p_ready, 4 * i + n + 1)
                    step(nc.vector.reciprocal(inv[:, n:n + 1], sums[:, n:n + 1]))
                    nc.vector.tensor_scalar(p[:, n], p[:, n], inv[:, n:n + 1], None, ALU.mult).then_inc(pn_ready, 1)
                for n in (1, 3):
                    bank = got(f"T{n}")
                    nc.vector.tensor_copy(pT[:, :, n * P:(n + 1) * P], bank[:].rearrange("p (k n) -> p k n", k=TT)).then_inc(pT_ready[1], 1)
                assert first or state["k"] == state["per"]

            state["base"] += state["k"]
            state["k"] = 0
            body(0, FIRST, True)
            per = state["k"]
            state.update(per=per)

            def round_(i):
                state.update(i=i, k=0)
                body(i, MAIN, False)
            with dve.Fori(1, NH) as i:
                round_(i)
            for n in range(8):
                dve.wait_ge(full[n % 4], nth(MAIN, f"T{n % 4}", NH - 1)[1] + 2 + n // 4)
                dve.wait_ge(y_ready, 1 + 8 * (NH - 1))
                add_output(NH - 1, n, n % 4)


TWO_PI = (6.28125, 0.0019340515136718750, float(2 * np.pi - 6.28125 - 0.0019340515136718750))


def program(nc, dram, out):
    with ExitStack() as ctx:
        t = {
            "const": ctx.enter_context(nc.sbuf_tensor("masks", [P, C_ALL], F32)),
            "res": ctx.enter_context(nc.sbuf_tensor("res", [P, TT, D], F32)),
            "xT": ctx.enter_context(nc.sbuf_tensor("xT", [P, KD, SEQ], F32)),
            "ps": [ctx.enter_context(nc.psum_tensor(f"bank{b}", [P, 512], F32)) for b in range(8)],
            "slots_x": nc.dram_tensor("slots_x", (BLOCKS * CAP, D), F32, kind="Internal").ap(),
            "slots_y": nc.dram_tensor("slots_y", (BLOCKS * CAP, D), F32, kind="Internal").ap(),
            "x_in": [ctx.enter_context(nc.semaphore(f"x_in_{n}")) for n in range(TT)],
        }
        delta_net(nc, t, None, dram)
        mixture(nc, t, dram, "ln1_g", "ln1_b", 0, "moe0")
        norm(nc, t, dram, "ln2_g", "ln2_b", 0, "norm1", routed=False)
        latent_attention(nc, t, dram)
        mixture(nc, t, dram, "ln1_g", "ln1_b", 1, "moe1")
        norm(nc, t, dram, "ln2_g", "ln2_b", 1, "norm3", routed=False, out=out)


_INS = ["x", "positions", "dn_w_in", "dn_conv_w", "dn_a_log", "dn_dt_bias", "dn_norm_w", "dn_w_out",
        "mla_w_in", "mla_q_norm", "mla_w_qb", "mla_kv_norm", "mla_w_kvb", "mla_w_out",
        "ln1_g", "ln1_b", "ln2_g", "ln2_b", "router_w", "router_bias", "moe_w_gate", "moe_w_up", "moe_w_down"]


def kernel(**inputs):
    import concourse.bacc as _bacc
    from concourse.bass_utils import run_bass_kernel_spmd as _run

    nc = _bacc.Bacc("TRN2", target_bir_lowering=False, num_devices=1)
    arrays = {name: np.ascontiguousarray(inputs[name]) for name in _INS}
    arrays["const"] = constants()
    dram = {name: nc.dram_tensor(name, a.shape, mybir.dt.from_np(a.dtype), kind="ExternalInput").ap() for name, a in arrays.items()}
    out = nc.dram_tensor("out", (1, SEQ, D), F32, kind="ExternalOutput").ap()
    program(nc, dram, out)
    return _run(nc, [arrays], core_ids=[0]).results[0]["out"]
```

```python
from contextlib import ExitStack

import numpy as np

import concourse.bass as bass
from concourse import mybir

ALU = mybir.AluOpType
ACT = mybir.ActivationFunctionType
AX = mybir.AxisListType
F32 = mybir.dt.float32

P = 128
D = 1024
SEQ = 512
TT = SEQ // P
KD = D // P
ALPHA = 4.0 ** 0.25
LN_EPS = 1e-5
RMS_EPS = 1e-6

NK, NV, DH = 8, 16, 128
K_OFF, V_OFF, Z_OFF, BA_OFF = NK * DH, 2 * NK * DH, 2 * NK * DH + NV * DH, 2 * NK * DH + 2 * NV * DH
TAPS = 5
Z_TILES = (1, 2, 0, 3)
LEVELS = 7
NEG_EG, EG, BETA, COEF, EGL, GRAW = range(6)

C_ID, C_ONE, C_TF, C_TB, C_SF, C_SB = (P * n for n in range(6))
C_LEV = 6 * P
C_JLT = C_LEV + 2 * LEVELS * 64
C_FREQ = C_JLT + 16
C_BELOW = C_FREQ + 32
C_NUM = C_BELOW + 256
C_ALL = C_NUM + 16


def constants():
    c = np.zeros((P, C_ALL), np.float32)
    r, q = np.arange(P)[:, None], np.arange(P)[None, :]
    c[:, C_ID:C_ID + P] = r == q
    c[:, C_ONE:C_ONE + P] = 1.0
    c[:, C_TF:C_TF + P] = r <= q
    c[:, C_TB:C_TB + P] = r >= q
    c[:, C_SF:C_SF + P] = r > q
    c[:, C_SB:C_SB + P] = r < q
    for d in range(2):
        for l in range(LEVELS):
            b = 1 << l
            m = (r // (2 * b) == q // (2 * b)) & ((r // b) % 2 == 1 - d) & ((q // b) % 2 == d)
            cols = [x for x in range(P) if (x // b) % 2 == d]
            at = C_LEV + (d * LEVELS + l) * 64
            c[:, at:at + 64] = m[:, cols]
    i, j = np.arange(4)[:, None], np.arange(4)[None, :]
    c[:, C_JLT:C_JLT + 16] = (j < i).reshape(1, 16)
    c[:, C_BELOW:C_BELOW + 256] = (np.arange(16)[None, :] < np.arange(16)[:, None]).reshape(1, 256)
    c[:, C_NUM:C_NUM + 16] = np.arange(16)[None]
    inv = (1.0 / (10000.0 ** (np.arange(0, 64, 2, dtype=np.float32) / np.float32(64)))).astype(np.float32)
    c[:, C_FREQ:C_FREQ + 32] = inv[None]
    return c




class Uses:

    def __init__(self, names):
        self.at, self.per, self.before, last = {}, {}, {}, {}
        for name, bank in names:
            self.before[name] = last.get(bank)
            last[bank] = name
            self.at[name] = (bank, self.per.get(bank, 0))
            self.per[bank] = self.per.get(bank, 0) + 1


def phase(nc, ctx, prefix=""):
    made = []

    def end():
        nc.clear_and_free_semaphores(made)
        nc.all_engine_barrier()

    def sem(name):
        made.append(nc.alloc_semaphore(name=prefix + name))
        return made[-1]

    ctx.callback(end)
    return sem


PROJECT = [("proj0", 0), ("proj1", 1), ("proj2", 0), ("proj3", 1)]
PREPARE = [("D0", 2), ("D1", 3), ("tr0", 4), ("tr1", 5), ("tr2", 6), ("tr3", 7), ("D2", 2), ("D3", 3)]
PREPARE_LATE = [("kT", 2), ("qT", 3), ("KK", 2), ("KQ", 3)]


def dn_uses(with_next):
    names = [("taps", 2)] if with_next else []
    if with_next:
        names += PROJECT
    for l in range(LEVELS):
        for g in range(4):
            names += [(f"X{l}{g}", 4 + g % 2)] + [(f"U{l}{g}", 6 + g % 2)] * (l > 0)
    names += [("z0", 0), ("z1", 1)]
    for s in range(4):
        for d in range(2):
            if s:
                names.append((f"kq{s}{d}", 4 + d))
            names += [(f"w{s}{d}", 2 + d), (f"os{s}{d}", 6 + d)]
    if with_next:
        names += PREPARE
    names += [("oT0", 2), ("oT1", 3)] + [(f"y{n}", n % 2) for n in range(8)]
    if with_next:
        names += PREPARE_LATE
    return Uses(names)


RSQRT_STEPS = 11


def rsqrt(nc, step, out, x, tmp):
    i32 = mybir.dt.int32
    step(nc.vector.tensor_scalar(out.bitcast(i32), x.bitcast(i32), 1, None, ALU.logical_shift_right))
    step(nc.vector.tensor_scalar(out.bitcast(i32), out.bitcast(i32), -1.0, float(0x5F3759DF), ALU.mult, ALU.add))
    for _ in range(3):
        step(nc.vector.tensor_tensor(tmp, out, out, ALU.mult))
        step(nc.vector.scalar_tensor_tensor(out=tmp, in0=tmp, scalar=-0.5, in1=x, op0=ALU.mult, op1=ALU.mult))
        step(nc.vector.scalar_tensor_tensor(out=out, in0=tmp, scalar=1.5, in1=out, op0=ALU.add, op1=ALU.mult))


def delta_net(nc, t, dram):
    F = Uses(PROJECT + [("taps", 2)])
    FIRST_HEAD = Uses(PREPARE + PREPARE_LATE)
    MAIN, LAST = dn_uses(True), dn_uses(False)
    c, ps, res, xT = t["const"], t["ps"], t["res"], t["xT"]
    ident, ones = c[:, C_ID:C_ID + P], c[:, C_ONE:C_ONE + P]
    tri = [c[:, C_TF:C_TF + P], c[:, C_TB:C_TB + P]]
    after = [c[:, C_SF:C_SF + P], c[:, C_SB:C_SB + P]]
    before = [after[1], after[0]]

    with ExitStack() as ctx:
        def sb(name, shape):
            return ctx.enter_context(nc.sbuf_tensor(name, shape, F32))

        sem = phase(nc, ctx)

        wqkv = sb("wqkv", [P, 4, KD, P])
        wz = sb("wz", [P, KD, 2 * P])
        wo = sb("wo", [P, 2, D])
        tapr = sb("tapr", [TAPS, 4, P])
        taps = sb("taps", [P, 4, TAPS])
        conv = sb("conv", [P, 4, SEQ])
        th = sb("th", [P, 2, SEQ])
        sq = sb("sq", [P, 2, SEQ])
        kq_sq = sb("kq_sq", [P, 2, SEQ])
        kq = sb("kq", [P, 2, TT, P])
        kqT = sb("kqT", [P, 2, TT, P])
        v = sb("v", [P, 2, TT, P])
        zs = sb("zs", [P, TT, 2, P])
        ss, rs, nt = (sb(n, [P, 8]) for n in ("ss", "rs", "nt"))
        kq_ss, kq_rs = sb("kq_ss", [P, 8]), sb("kq_rs", [P, 8])
        triG = sb("triG", [P, 2, TT, P])
        dec = sb("dec", [P, 4, TT, P])
        kkm = sb("kkm", [P, 2, TT, P])
        kqm = sb("kqm", [P, 2, TT, P])
        A = sb("A", [P, 4, TT, P])
        T = sb("T", [P, 4, TT, P])
        U = sb("U", [P, 4, TT, P])
        X = sb("X", [P, LEVELS, 2, TT, P])
        am = sb("am", [P, TT, 64])
        St = sb("St", [P, 2, 2, P])
        r = sb("r", [P, 2, 2, P])
        vn = sb("vn", [P, 2, 2, P])
        vs = sb("vs", [P, 2, 2, P])
        o = sb("o", [P, TT, 2, P])
        oT = sb("oT", [P, 2, TT, P])
        gt = sb("gt", [P, 6, TT, 2 * NV])
        gb = sb("gb", [P, 5 * TT, 2, 2])
        raw = sb("raw", [P, TT, 2, 2])
        nw = sb("nw", [P, 1])
        bvec = sb("bvec", [P, 2, 2 * NV])
        wba = sb("wba", [P, KD, 4 * NV])
        ba = sb("ba", [P, TT, 4 * NV])
        tmp = sb("tmp", [P, 4, TT, 2 * NV])

        full = [sem(f"dn_full{b}") for b in range(8)]
        ident_in, small_in, ba_in = sem("ident_in"), sem("small_in"), sem("ba_in")
        w_in = [sem(f"w_in{n}") for n in range(4)]
        z_in, o_in, taps_in = sem("z_in"), sem("o_in"), sem("taps_in")
        link, alink = sem("dve_link"), sem("act_link")
        xT_ready = sem("xT_ready")
        gates_ready, raw_ready, beta_ready = sem("gates_ready"), sem("raw_ready"), sem("beta_ready")
        sums_ready = sem("sums_ready")
        gb_ready, triG_ready, dec_ready, at_ready, qkd_ready = (sem(n) for n in ("gb_ready", "triG_ready", "dec_ready", "at_ready", "qkd_ready"))
        eye_ready = sem("eye_ready")
        taps_ready, conv_ready, th_ready, silu_ready = (sem(n) for n in ("taps_ready", "conv_ready", "th_ready", "silu_ready"))
        sq_ready, ss_ready, kq_ready, kqT_ready, v_ready = (sem(n) for n in ("sq_ready", "ss_ready", "kq_ready", "kqT_ready", "v_ready"))
        mask_ready, head_raw_ready = sem("mask_ready"), sem("head_raw_ready")
        xm_ready, upd_ready = sem("xm_ready"), sem("upd_ready")
        zt_ready, zs_ready = sem("zt_ready"), sem("zs_ready")
        r_ready, vs_ready, vn_ready, S_ready, o_step = (sem(n) for n in ("r_ready", "vs_ready", "vn_ready", "S_ready", "o_step"))
        oq_ready, ba_ready, dve_sums = sem("oq_ready"), sem("ba_ready"), sem("dve_sums")
        osq_ready, oss_ready, og_ready, oT_ready, y_ready = (sem(n) for n in ("osq_ready", "oss_ready", "og_ready", "oT_ready", "y_ready"))
        x_zero, zeroed, zero_filled = sem("x_zero"), sem("zeroed"), sem("zero_filled")
        zeros = o[0:CAP].rearrange("p t h n -> p (t h n)")

        earlier = {0: 2, 1: 2, 2: 2, 3: 1, 4: 4, 5: 4, 6: 0, 7: 0}
        base = {b: n + FIRST_HEAD.per.get(b, 0) for b, n in earlier.items()}

        def read_of(name, i):
            h = i + 1
            if name[:-1] in ("D", "tr", "proj", "z", "y", "oT"):
                n = int(name[-1])
                if name[:-1] == "tr":
                    return (v_ready, h * 2 + n - 1) if n >= 2 else (kq_ready, h * 2 + 2 - n)
                return {"D": (dec_ready, h * 4 + n + 1), "proj": (conv_ready, h * 4 + n + 1), "z": (zs_ready, i * 2 + n + 1),
                        "y": (y_ready, 1 + i * 8 + n + 1), "oT": (oT_ready, 1 + i * 2 + n + 1)}[name[:-1]]
            if name in ("kT", "qT"):
                return kqT_ready, h * 2 + (1 if name == "kT" else 2)
            if name in ("KK", "KQ"):
                return mask_ready, h * 4 + (2 if name == "KK" else 4)
            if name == "taps":
                return taps_ready, i + 2
            a, b = int(name[-2]), int(name[-1])
            if name[0] in "XU":
                return (xm_ready if name[0] == "X" else upd_ready), i * 28 + a * 4 + b + 1
            if name[:2] == "kq":
                return oq_ready, i * 6 + (a - 1) * 2 + b + 1
            if name[0] == "w":
                return vn_ready, i * 8 + a * 2 + b + 1
            return o_step, 1 + i * 8 + a * 2 + b + 1

        def last_read(b, i):
            if b < 2:
                return y_ready, 1 + i * 8
            return {2: (mask_ready, i * 4 + 2), 3: (mask_ready, i * 4 + 4), 4: (kq_ready, i * 2 + 2), 5: (kq_ready, i * 2 + 1),
                    6: (v_ready, i * 2 + 1), 7: (v_ready, i * 2 + 2)}[b]

        def nth(uses, name, i):
            b, k = uses.at[name]
            if uses is FIRST_HEAD:
                return b, earlier[b] + k
            return b, base[b] + i * MAIN.per[b] + k

        def level(a, d, l, other=0):
            b = 1 << l
            return a.rearrange("p (a h b) -> p a h b", h=2, b=b)[:, :, (d + other) % 2, :]

        def z_pair(a, n):
            a = a[:].rearrange("p t h n -> p t (h n)")
            return a[:, 0:4:3] if n else a[:, 1:3]

        def last_rows(half):
            return slice(64 * half, 64 * half + 64)

        w_dram = dram["dn_w_in"][0].rearrange("(k p) n -> p k n", p=P)
        wo_dram = dram["dn_w_out"][0].rearrange("(h p) n -> p h n", p=P)
        cw_dram = dram["dn_conv_w"][0]

        block = ctx.enter_context(nc.Block())

        @block.sync
        def _(sp):
            x_dram = dram["x"][0].rearrange("(t p) n -> p t n", p=P)
            sp.dma_start(ident, dram["const"][:, C_ID:C_ID + P]).then_inc(ident_in, 16)
            for tt in range(TT):
                sp.dma_start(res[:, tt], x_dram[:, tt]).then_inc(t["x_in"][tt], 16)
            sp.dma_start(wba[:], w_dram[:, :, BA_OFF:BA_OFF + 4 * NV]).then_inc(ba_in, 16)
            sp.dma_start(c[:, C_ONE:], dram["const"][:, C_ONE:]).then_inc(small_in, 16)
            sp.dma_start(bvec[:, 0], dram["dn_a_log"][0].rearrange("d h -> (d h)").partition_broadcast(P)).then_inc(small_in, 16)
            sp.dma_start(bvec[:, 1], dram["dn_dt_bias"][0].rearrange("d h -> (d h)").partition_broadcast(P)).then_inc(small_in, 16)
            sp.dma_start(nw[:], dram["dn_norm_w"].rearrange("a p -> p a")).then_inc(small_in, 16)

            def load_w(n, late):
                at = (lambda off, w: slice(off, off + w)) if isinstance(n, int) else (lambda off, w: bass.ds(off, w))
                for ct in range(4):
                    off = [n * P, K_OFF + n * P, V_OFF + n * 2 * P, V_OFF + n * 2 * P + P][ct]
                    if late:
                        sp.wait_ge(conv_ready, (n - 1) * 4 + ct + 1)
                    sp.dma_start(wqkv[:, ct], w_dram[:, :, at(off, P)]).then_inc(w_in[ct], 16)
                if late:
                    sp.wait_ge(taps_ready, n)
                for a, (off, w) in enumerate([(n * P, P), (K_OFF + n * P, P), (V_OFF + n * 2 * P, 2 * P)]):
                    sp.dma_start(tapr[:, a:a + w // P].rearrange("p a b -> p (a b)"), cw_dram[:, at(off, w)]).then_inc(taps_in, 16)

            def load_late(n, late):
                at = (lambda off, w: slice(off, off + w)) if isinstance(n, int) else (lambda off, w: bass.ds(off, w))
                if late:
                    sp.wait_ge(zs_ready, n * 2)
                sp.dma_start(wz[:], w_dram[:, :, at(Z_OFF + n * 2 * P, 2 * P)]).then_inc(z_in, 16)
                if late:
                    sp.wait_ge(y_ready, 1 + n * 8)
                src = wo_dram[:, at(n * 2, 2), :]
                sp.dma_start(wo[:], src).then_inc(o_in, 16)

            load_w(0, False)
            load_late(0, False)
            load_w(1, True)
            sp.wait_ge(zeroed, 1)
            for slots in (t["slots_x"], t["slots_y"]):
                blocks = slots.rearrange("(b p) n -> p b n", p=CAP)
                sp.dma_start(blocks, zeros.rearrange("p (a n) -> p a n", a=1).to_broadcast([CAP, BLOCKS, D])).then_inc(zero_filled, 16)
            with sp.Fori(1, NK - 1) as n:
                load_w(n + 1, True)
                load_late(n, True)
            load_late(NK - 1, True)
            sp.wait_ge(zero_filled, 32)

        @block.tensor
        def _(pe):
            def begin(uses, name, i):
                b, k = uses.at[name]
                if k:
                    pe.wait_ge(*read_of(uses.before[name], i))
                elif uses is not FIRST_HEAD:
                    pe.wait_ge(*last_read(b, i))
                return ps[b]

            def done(mm, uses, name):
                mm.then_inc(full[uses.at[name][0]], 1)

            pe.wait_ge(ident_in, 16)
            for n in range(8):
                tt, half = n // 2, n % 2
                if half == 0:
                    pe.wait_ge(t["x_in"][tt], 16)
                b = 4 + n % 2
                if n >= 2:
                    pe.wait_ge(xT_ready, n - 1)
                for k in range(4):
                    mm = pe.transpose(ps[b][:, k * P:(k + 1) * P], res[:, tt, (half * 4 + k) * P:(half * 4 + k + 1) * P], ident)
                mm.then_inc(full[b], 1)
            pe.wait_ge(ba_in, 16)
            pe.wait_ge(xT_ready, 8)
            for tt in range(TT):
                for k in range(KD):
                    mm = pe.matmul(ps[2][:, tt * 64:(tt + 1) * 64], xT[:, k, tt * P:(tt + 1) * P], wba[:, k], start=k == 0, stop=k == KD - 1)
            mm.then_inc(full[2], 1)

            def project(uses, i, n, ct, part=(0, KD)):
                if part[0] == 0:
                    pe.wait_ge(w_in[ct], (n + 1) * 16)
                    begin(uses, f"proj{ct}", i)
                bank = ps[uses.at[f"proj{ct}"][0]]
                for k in range(*part):
                    mm = pe.matmul(bank[:], wqkv[:, ct, k], xT[:, k], start=k == 0, stop=k == KD - 1)
                if part[1] == KD:
                    done(mm, uses, f"proj{ct}")

            def tap_rows(uses, i, n):
                pe.wait_ge(taps_in, (n + 1) * 48)
                bank = begin(uses, "taps", i)
                for ct in range(4):
                    mm = pe.matmul(bank[:, ct * TAPS:(ct + 1) * TAPS], tapr[:, ct], ident[0:TAPS, 0:TAPS], start=True, stop=True)
                done(mm, uses, "taps")

            def log_sums():
                pe.wait_ge(small_in, 64)
                pe.wait_ge(raw_ready, 1)
                for d in range(2):
                    pe.matmul(ps[3][:, 0:P].rearrange("p (t g) -> p t g", t=TT)[:, :, d * NV:(d + 1) * NV], tri[d], gt[:, GRAW, :, d * NV:(d + 1) * NV], start=True, stop=True)
                mm = pe.matmul(ps[3][:, P:2 * P], ones, gt[:, GRAW].rearrange("p t g -> p (t g)"), start=True, stop=True)
                mm.then_inc(full[3], 1)

            pe.wait_ge(taps_in, 48)
            pe.wait_ge(ba_ready, 1)
            for ct in range(4):
                mm = pe.transpose(ps[2][:, ct * TAPS:(ct + 1) * TAPS], tapr[:, ct], ident[0:TAPS, 0:TAPS])
            mm.then_inc(full[2], 1)
            for ct in range(4):
                if ct == 1:
                    log_sums()
                pe.wait_ge(w_in[ct], 16)
                b = ct % 2
                if ct >= 2:
                    pe.wait_ge(conv_ready, ct - 1)
                for kk in range(KD):
                    mm = pe.matmul(ps[b][:], wqkv[:, ct, kk], xT[:, kk], start=kk == 0, stop=kk == KD - 1)
                mm.then_inc(full[b], 1)

            def prepare(uses, i, n):
                def decay(g):
                    pe.wait_ge(triG_ready, n * 4 + g + 1)
                    bank = begin(uses, f"D{g}", i)
                    done(pe.matmul(bank[:], after[g // 2], triG[:, g % 2].rearrange("p t n -> p (t n)"), start=True, stop=True), uses, f"D{g}")

                decay(0)
                decay(1)
                for ct in range(4):
                    pe.wait_ge(silu_ready, n * 4 + ct + 1)
                    bank = begin(uses, f"tr{ct}", i)
                    for tt in range(TT):
                        mm = pe.transpose(bank[:, tt * P:(tt + 1) * P], conv[:, ct, tt * P:(tt + 1) * P], ident)
                    done(mm, uses, f"tr{ct}")
                decay(2)
                decay(3)

            def turn_kq(uses, i, n):
                for ct, name in ((1, "kT"), (0, "qT")):
                    pe.wait_ge(kq_ready, n * 2 + (1 if ct else 2))
                    bank = begin(uses, name, i)
                    for tt in range(TT):
                        mm = pe.transpose(bank[:, tt * P:(tt + 1) * P], kq[:, ct, tt], ident)
                    done(mm, uses, name)

            def scores(uses, i, n):
                for ct, name in ((1, "KK"), (0, "KQ")):
                    pe.wait_ge(kqT_ready, n * 2 + (1 if ct else 2))
                    bank = begin(uses, name, i)
                    for tt in range(TT):
                        mm = pe.matmul(bank[:, tt * P:(tt + 1) * P], kqT[:, 1, tt], kqT[:, ct, tt], start=True, stop=True)
                    done(mm, uses, name)

            def body(i, uses, with_next):
                fill = []
                if with_next:
                    for ct in range(4):
                        for a in range(0, KD, 2):
                            fill.append((project, (uses, i, i + 1, ct, (a, a + 2))))
                    tap_rows(uses, i, i + 1)

                def filler(n=1):
                    for _ in range(n):
                        if fill:
                            f, a = fill.pop(0)
                            f(*a)

                filler(4)

                pe.wait_ge(eye_ready, i * 8 + 8)

                def make_x(n):
                    l, g = divmod(n, 4)
                    d = g // 2
                    if l == 0:
                        pe.wait_ge(at_ready, i * 4 + g + 1)
                    else:
                        pe.wait_ge(upd_ready, i * 28 + n - 4 + 1)
                    bank = begin(uses, f"X{l}{g}", i)
                    r = last_rows(1 - d) if l == LEVELS - 1 else slice(0, P)
                    for tt in range(TT):
                        if l == 0:
                            mm = pe.transpose(bank[:, tt * P:(tt + 1) * P], A[:, g, tt], ident)
                        else:
                            mm = pe.matmul(bank[r, tt * 64:(tt + 1) * 64], A[:, g, tt, r], level(T[:, g, tt], d, l), start=True, stop=True)
                    done(mm, uses, f"X{l}{g}")

                def make_u(n):
                    l, g = divmod(n, 4)
                    d = g // 2
                    pe.wait_ge(xm_ready, i * 28 + n + 1)
                    bank = begin(uses, f"U{l}{g}", i)
                    for tt in range(TT):
                        if l < LEVELS - 1:
                            pe.matmul(bank[:, tt * 64:(tt + 1) * 64], U[:, g, tt], level(X[:, l, g % 2, tt], d, l), start=True, stop=True)
                        r = last_rows(d) if l == LEVELS - 1 else slice(0, P)
                        mm = pe.matmul(bank[r, 256 + tt * 64:256 + (tt + 1) * 64], X[:, l, g % 2, tt, r], level(U[:, g, tt], d, l, 1), start=True, stop=True)
                    done(mm, uses, f"U{l}{g}")

                for n in range(LEVELS * 4 + 2):
                    if n < LEVELS * 4:
                        make_x(n)
                    if n >= 2 + 4:
                        make_u(n - 2)
                    if n in (0, 1, 2, 3, 6, 8, 9, 10, 12, 13, 14, 15):
                        filler(1)
                filler(99)

                pe.wait_ge(z_in, (i + 1) * 16)

                def make_z(n):
                    tt = Z_TILES[n]
                    name = f"z{n // 2}"
                    if n % 2 == 0:
                        begin(uses, name, i)
                    bank = ps[uses.at[name][0]]
                    for k in range(KD):
                        mm = pe.matmul(bank[:, (n % 2) * 256:(n % 2) * 256 + 256], xT[:, k, tt * P:(tt + 1) * P], wz[:, k], start=k == 0, stop=k == KD - 1)
                    if n % 2:
                        done(mm, uses, name)

                for step in range(4):
                    for d in range(2):
                        tt = 3 - step if d else step
                        if step:
                            pe.wait_ge(S_ready, i * 6 + (step - 1) * 2 + d + 1)
                            bank = begin(uses, f"kq{step}{d}", i)
                            S2 = St[:, d].rearrange("p h n -> p (h n)")
                            pe.matmul(bank[:, 0:256], kqT[:, 1, tt], S2, start=True, stop=True)
                            mm = pe.matmul(bank[:, 256:512], kqT[:, 0, tt], S2, start=True, stop=True)
                            done(mm, uses, f"kq{step}{d}")
                    make_z(step)
                    for d in range(2):
                        tt = 3 - step if d else step
                        if step:
                            pe.wait_ge(r_ready, i * 6 + (step - 1) * 2 + d + 1)
                        else:
                            pe.wait_ge(upd_ready, i * 28 + 28)
                            pe.wait_ge(v_ready, i * 2 + 2)
                        bank = begin(uses, f"w{step}{d}", i)
                        for h in range(2):
                            mm = pe.matmul(bank[:, h * P:(h + 1) * P], U[:, d * 2 + h, tt], r[:, d, h] if step else v[:, h, tt], start=True, stop=True)
                        done(mm, uses, f"w{step}{d}")
                    for d in range(2):
                        tt = 3 - step if d else step
                        bank = begin(uses, f"os{step}{d}", i)
                        if step < 3:
                            pe.wait_ge(vs_ready, i * 6 + step * 2 + d + 1)
                            pe.matmul(bank[:, 256:512], kq[:, 1, tt], vs[:, d].rearrange("p h n -> p (h n)"), start=True, stop=True)
                        pe.wait_ge(vn_ready, i * 8 + step * 2 + d + 1)
                        pe.wait_ge(qkd_ready, i * 4 + 4)
                        for h in range(2):
                            mm = pe.matmul(bank[:, h * P:(h + 1) * P], dec[:, d * 2 + h, tt], vn[:, d, h], start=True, stop=True)
                        done(mm, uses, f"os{step}{d}")

                if with_next:
                    prepare(uses, i, i + 1)
                for h in range(2):
                    pe.wait_ge(og_ready, i + 1)
                    bank = begin(uses, f"oT{h}", i)
                    for tt in range(TT):
                        mm = pe.transpose(bank[:, tt * P:(tt + 1) * P], zs[:, tt, h], ident)
                    done(mm, uses, f"oT{h}")
                pe.wait_ge(o_in, (i + 1) * 16)
                pe.wait_ge(oT_ready, 1 + i * 2 + 2)
                for n in range(8):
                    tt, half = n // 2, n % 2
                    bank = begin(uses, f"y{n}", i)
                    for h in range(2):
                        mm = pe.matmul(bank[:], oT[:, h, tt], wo[:, h, half * 512:(half + 1) * 512], start=h == 0, stop=h == 1)
                    done(mm, uses, f"y{n}")
                    if with_next and n == 3:
                        turn_kq(uses, i, i + 1)
                    if with_next and n == 5:
                        scores(uses, i, i + 1)

            pe.wait_ge(taps_ready, 1)
            pe.wait_ge(dve_sums, 1)
            prepare(FIRST_HEAD, -1, 0)
            turn_kq(FIRST_HEAD, -1, 0)
            scores(FIRST_HEAD, -1, 0)
            pe.wait_ge(conv_ready, 4)
            with pe.Fori(0, NK - 1) as i:
                body(i, MAIN, True)
            body(NK - 1, LAST, False)

        @block.scalar
        def _(act):
            def got(uses, name, i):
                b, n = nth(uses, name, i)
                act.wait_ge(full[b], n + 1)
                return ps[b]

            act.sem_inc(oT_ready, 1)
            for n in range(8):
                b = 4 + n % 2
                act.wait_ge(full[b], n // 2 + 1)
                tt, half = n // 2, n % 2
                act.copy(xT[:, half * 4:half * 4 + 4, tt * P:(tt + 1) * P], ps[b][:].rearrange("p (k n) -> p k n", k=4)).then_inc(xT_ready, 1)

            act.wait_ge(full[2], 1)
            act.copy(ba[:].rearrange("p t g -> p (t g)"), ps[2][:, 0:256]).then_inc(ba_ready, 1)
            act.wait_ge(ba_ready, 1)
            act.activation(tmp[:, 0], ba[:, :, 0:32], ACT.Exp, scale=-1.0).then_inc(beta_ready, 1)
            act.wait_ge(small_in, 64)
            act.activation(bvec[:, 0], bvec[:, 0], ACT.Exp).then_inc(beta_ready, 1)
            act.wait_ge(gates_ready, 1)
            act.activation(tmp[:, 2], tmp[:, 2], ACT.Exp).then_inc(alink, 1)
            act.wait_ge(alink, 1)
            act.activation(tmp[:, 2], tmp[:, 2], ACT.Ln, bias=1.0).then_inc(beta_ready, 1)
            act.wait_ge(gates_ready, 2)
            act.activation(gt[:, EG], tmp[:, 0], ACT.Exp).then_inc(sums_ready, 1)
            act.activation(gt[:, EGL], tmp[:, 3], ACT.Exp).then_inc(sums_ready, 1)
            act.activation(tmp[:, 1], tmp[:, 1], ACT.Exp).then_inc(sums_ready, 1)

            def act_silu(n, ct):
                act.wait_ge(conv_ready, n * 4 + ct + 1)
                if not (isinstance(n, int) and n == 0 and ct < 2):
                    act.wait_ge(silu_ready, n * 4 + ct - 1)
                act.activation(th[:, ct % 2], conv[:, ct], ACT.Tanh, scale=0.5).then_inc(th_ready, 1)

            def take_raw(n):
                if not isinstance(n, int):
                    act.wait_ge(triG_ready, n * 4)
                else:
                    act.wait_ge(raw_ready, 1)
                fields = gt[:, GRAW].rearrange("p t (d h) -> p t d h", d=2)
                act.copy(raw[:], fields[:, :, :, 0:2] if isinstance(n, int) else fields[:, :, :, bass.ds(2 * n, 2)]).then_inc(head_raw_ready, 1)

            def take_gates(n):
                act.wait_ge(gates_ready, 3)
                act.wait_ge(o_step, 1 + n * 8)
                fields = gt[:, 0:5].rearrange("p f t (d h) -> p (f t) d h", d=2)
                act.copy(gb[:], fields[:, :, :, 0:2] if isinstance(n, int) else fields[:, :, :, bass.ds(2 * n, 2)]).then_inc(gb_ready, 1)

            def prepare(uses, i, n):
                def decay(g):
                    bank = got(uses, f"D{g}", i)
                    act.activation(dec[:, g].rearrange("p t n -> p (t n)"), bank[:], ACT.Exp).then_inc(dec_ready, 1)

                decay(0)
                decay(1)
                for ct in range(2):
                    bank = got(uses, f"tr{ct}", i)
                    if not isinstance(n, int):
                        act.wait_ge(ss_ready, n)
                    act.activation(kq_sq[:, ct], bank[:], ACT.Square).then_inc(sq_ready, 1)
                for h in range(2):
                    bank = got(uses, f"tr{2 + h}", i)
                    act.mul(v[:, h].rearrange("p t n -> p (t n)"), bank[:], 0.5).then_inc(v_ready, 1)
                decay(2)
                decay(3)

            def prepare_late(uses, i, n):
                for g in range(4):
                    eye = ident.rearrange("p (a n) -> p a n", a=1).to_broadcast([P, TT, P])
                    act.copy(T[:, g], eye).then_inc(eye_ready, 1)
                    act.copy(U[:, g], eye).then_inc(eye_ready, 1)
                for ct, name in ((1, "kT"), (0, "qT")):
                    bank = got(uses, name, i)
                    act.copy(kqT[:, ct].rearrange("p t n -> p (t n)"), bank[:]).then_inc(kqT_ready, 1)

            def body(i, uses, with_next):
                if with_next:
                    take_raw(i + 1)
                    for ct in range(4):
                        act_silu(i + 1, ct)

                def z_tanh(n):
                    bank = got(uses, f"z{n}", i)
                    act.wait_ge(oss_ready, 1 + i)
                    act.activation(sq[:, n], bank[:], ACT.Tanh, scale=0.5).then_inc(zt_ready, 1)

                def square_o(n):
                    act.wait_ge(o_step, 1 + i * 8 + 6 + 2 * n)
                    act.wait_ge(zs_ready, i * 2 + n + 1)
                    act.activation(sq[:, n].rearrange("p (t m) -> p t m", t=2), z_pair(o, n), ACT.Square).then_inc(osq_ready, 1)

                for step in range(4):
                    if step == 3:
                        square_o(0)
                    for d in range(2):
                        tt = 3 - step if d else step
                        bank = got(uses, f"w{step}{d}", i)
                        if step < 3:
                            for h in range(2):
                                ins = act.mul(vs[:, d, h], bank[:, h * P:(h + 1) * P], gb[:, COEF * TT + tt, d, h:h + 1])
                            ins.then_inc(vs_ready, 1)
                        for h in range(2):
                            ins = act.mul(vn[:, d, h], bank[:, h * P:(h + 1) * P], gb[:, BETA * TT + tt, d, h:h + 1])
                        ins.then_inc(vn_ready, 1)
                    if step == 1:
                        z_tanh(0)
                    if step == 3:
                        z_tanh(1)

                square_o(1)
                if with_next:
                    take_gates(i + 1)
                    prepare(uses, i, i + 1)
                for h in range(2):
                    bank = got(uses, f"oT{h}", i)
                    act.wait_ge(y_ready, 1 + i * 8)
                    act.mul(oT[:, h].rearrange("p t n -> p (t n)"), bank[:], nw[:, 0:1]).then_inc(oT_ready, 1)
                if with_next:
                    prepare_late(uses, i, i + 1)

            take_raw(0)
            take_gates(0)
            for ct in range(4):
                act_silu(0, ct)
            prepare(FIRST_HEAD, -1, 0)
            prepare_late(FIRST_HEAD, -1, 0)
            with act.Fori(0, NK - 1) as i:
                body(i, MAIN, True)
            body(NK - 1, LAST, False)

        @block.gpsimd
        def _(pool):
            nc.gpsimd.memset(zeros, 0.0).then_inc(zeroed, 1)
            nc.gpsimd.memset(X[:], 0.0).then_inc(x_zero, 1)

            def prepare(uses, i, n):
                for g in range(4):
                    d, h = divmod(g, 2)
                    if g == 0:
                        pool.wait_ge(head_raw_ready, n + 1)
                    if g >= 2:
                        b, k = nth(uses, f"D{g - 2}", i)
                        pool.wait_ge(full[b], k + 1)
                    log_decay = raw[:, :, d, h:h + 1].to_broadcast([P, TT, P])
                    nc.gpsimd.tensor_tensor(triG[:, g % 2], tri[d].rearrange("p (a n) -> p a n", a=1).to_broadcast([P, TT, P]), log_decay, ALU.mult).then_inc(triG_ready, 1)

            def body(i, uses, with_next):
                for g in range(4):
                    pool.wait_ge(at_ready, i * 4 + g + 1)
                    pool.wait_ge(mask_ready, i * 4 + 4)
                    nc.gpsimd.tensor_tensor(dec[:, g], dec[:, g], kqm[:, g // 2], ALU.mult).then_inc(qkd_ready, 1)
                if with_next:
                    prepare(uses, i, i + 1)

            prepare(FIRST_HEAD, -1, 0)
            with pool.Fori(0, NK - 1) as i:
                body(i, MAIN, True)
            body(NK - 1, LAST, False)

        @block.vector
        def _(dve):
            links = {"base": 0, "i": 0, "per": 0, "k": 0}

            def step(ins):
                links["k"] += 1
                ins.then_inc(link, 1)
                dve.wait_ge(link, links["base"] + links["i"] * links["per"] + links["k"])

            def got(uses, name, i):
                b, n = nth(uses, name, i)
                dve.wait_ge(full[b], n + 1)
                return ps[b]

            for signal in (y_ready, o_step, oss_ready):
                dve.sem_inc(signal, 1)
            def grid(a):
                return a.rearrange("p (a n) -> p a n", a=1).to_broadcast([P, TT, 2 * NV])

            dve.wait_ge(small_in, 64)
            dve.wait_ge(ba_ready, 1)
            step(nc.vector.tensor_tensor(tmp[:, 1], ba[:, :, 32:64], grid(bvec[:, 1]), ALU.add))
            step(nc.vector.scalar_tensor_tensor(out=tmp[:, 2].rearrange("p t g -> p (t g)"), in0=tmp[:, 1].rearrange("p t g -> p (t g)"), scalar=-1.0,
                                                in1=tmp[:, 1].rearrange("p t g -> p (t g)"), op0=ALU.mult, op1=ALU.min))
            nc.vector.tensor_scalar(tmp[:, 3], tmp[:, 1], 0.0, None, ALU.max).then_inc(gates_ready, 1)
            dve.wait_ge(beta_ready, 1)
            step(nc.vector.tensor_scalar(tmp[:, 0], tmp[:, 0], 1.0, None, ALU.add))
            step(nc.vector.reciprocal(gt[:, BETA], tmp[:, 0]))
            dve.wait_ge(beta_ready, 3)
            dve.wait_ge(gates_ready, 1)
            step(nc.vector.tensor_tensor(tmp[:, 2], tmp[:, 2], tmp[:, 3], ALU.add))
            nc.vector.scalar_tensor_tensor(out=gt[:, GRAW], in0=tmp[:, 2], scalar=-1.0, in1=grid(bvec[:, 0]), op0=ALU.mult, op1=ALU.mult).then_inc(raw_ready, 1)
            dve.wait_ge(full[3], 1)
            step(nc.vector.tensor_copy(tmp[:, 0].rearrange("p t g -> p (t g)"), ps[3][:, 0:P]))
            nc.vector.tensor_copy(tmp[:, 3].rearrange("p t g -> p (t g)"), ps[3][:, P:2 * P]).then_inc(dve_sums, 1)
            dve.wait_ge(dve_sums, 1)
            nc.vector.tensor_tensor(tmp[:, 1], tmp[:, 3], tmp[:, 0], ALU.subtract).then_inc(gates_ready, 1)
            dve.wait_ge(sums_ready, 3)
            nc.vector.tensor_scalar(gt[:, NEG_EG], gt[:, EG], -1.0, None, ALU.mult)
            nc.vector.tensor_tensor(gt[:, COEF], gt[:, BETA], tmp[:, 1], ALU.mult).then_inc(gates_ready, 1)
            for tt in range(TT):
                dve.wait_ge(xT_ready, 2 * tt + 2)
                step(nc.vector.tensor_scalar(res[:, tt], res[:, tt], ALPHA, None, ALU.mult))

            def convolve(uses, i, n, ct, first=False, taps_of=(2, 0, 1, 3, 4)):
                if 2 not in taps_of:
                    bank = ps[ct % 2]
                elif first:
                    b, k = F.at[f"proj{ct}"]
                    dve.wait_ge(full[b], k + 1)
                    bank = ps[b]
                else:
                    bank = got(uses, f"proj{ct}", i)
                    if ct >= 2:
                        dve.wait_ge(v_ready, i * 2 + ct - 1)
                w = taps[:, ct]
                if 2 in taps_of:
                    dve.wait_ge(taps_ready, n + 1)
                    step(nc.vector.tensor_scalar(conv[:, ct], bank[:], w[:, 2:3], None, ALU.mult))
                for j in taps_of:
                    if j == 2:
                        continue
                    d = j - 2
                    lo, hi = max(0, -d), SEQ - max(0, d)
                    ins = nc.vector.scalar_tensor_tensor(out=conv[:, ct, lo:hi], in0=bank[:, lo + d:hi + d], scalar=w[:, j:j + 1], in1=conv[:, ct, lo:hi], op0=ALU.mult, op1=ALU.add)
                    if j == 4:
                        ins.then_inc(conv_ready, 1)
                    else:
                        step(ins)

            def silu(n, ct):
                dve.wait_ge(th_ready, n * 4 + ct + 1)
                nc.vector.scalar_tensor_tensor(out=conv[:, ct], in0=th[:, ct % 2], scalar=1.0, in1=conv[:, ct], op0=ALU.add, op1=ALU.mult).then_inc(silu_ready, 1)

            def tap_columns(bank):
                nc.vector.tensor_copy(taps[:].rearrange("p a b -> p (a b)"), bank[:, 0:4 * TAPS]).then_inc(taps_ready, 1)

            dve.wait_ge(full[2], 2)
            tap_columns(ps[2])
            for ct in range(4):
                convolve(None, 0, 0, ct, first=True)
                if ct:
                    silu(0, ct - 1)
            silu(0, 3)
            dve.wait_ge(x_zero, 1)

            def normalise(uses, i, n):
                dve.wait_ge(sq_ready, n * 2 + 2)
                nc.vector.tensor_reduce(kq_ss[:], kq_sq[:].rearrange("p a (t n) -> p (a t) n", t=TT), AX.X, ALU.add).then_inc(ss_ready, 1)
                dve.wait_ge(ss_ready, n + 1)
                step(nc.vector.tensor_scalar(kq_ss[:], kq_ss[:], 4.0 * RMS_EPS, None, ALU.add))
                rsqrt(nc, step, kq_rs[:], kq_ss[:], nt[:])
                step(nc.vector.tensor_scalar(kq_rs[:, 0:TT], kq_rs[:, 0:TT], DH ** -0.5, None, ALU.mult))
                for ct in (1, 0):
                    b = uses.at[f"tr{ct}"][0]
                    rb = kq_rs[:, ct * TT:(ct + 1) * TT].rearrange("p (t a) -> p t a", a=1).to_broadcast([P, TT, P])
                    bank = ps[b][:].rearrange("p (t n) -> p t n", t=TT)
                    nc.vector.tensor_tensor(kq[:, ct], bank, rb, ALU.mult).then_inc(kq_ready, 1)

            def mask_scores(uses, i, n):
                bank = got(uses, "KK", i)
                for d in range(2):
                    m = before[d].rearrange("p (a n) -> p a n", a=1).to_broadcast([P, TT, P])
                    ins = nc.vector.tensor_tensor(kkm[:, d], bank[:].rearrange("p (t n) -> p t n", t=TT), m, ALU.mult)
                    ins.then_inc(mask_ready, 1)
                bank = got(uses, "KQ", i)
                for d in range(2):
                    m = tri[d].rearrange("p (a n) -> p a n", a=1).to_broadcast([P, TT, P])
                    ins = nc.vector.tensor_tensor(kqm[:, d], bank[:].rearrange("p (t n) -> p t n", t=TT), m, ALU.mult)
                    ins.then_inc(mask_ready, 1)

            def make_A(n):
                dve.wait_ge(mask_ready, n * 4 + 2)
                for g in range(4):
                    d, h = divmod(g, 2)
                    dve.wait_ge(dec_ready, n * 4 + g + 1)
                    step(nc.vector.tensor_tensor(A[:, g], dec[:, g], kkm[:, d], ALU.mult))
                    beta = gb[:, BETA * TT:(BETA + 1) * TT, d, h:h + 1].to_broadcast([P, TT, P])
                    nc.vector.tensor_tensor(A[:, g], A[:, g], beta, ALU.mult).then_inc(at_ready, 1)


            def body(i, uses, with_next, per):
                links.update(i=i, per=per, k=0)
                if with_next:
                    tap_columns(got(uses, "taps", i))
                jobs = []
                if with_next:
                    for ct in range(4):
                        for j in (2, 0, 1, 3, 4):
                            jobs.append(lambda ct=ct, j=j: convolve(uses, i, i + 1, ct, taps_of=(j,)))
                            if j == 2 and ct:
                                jobs.append(lambda ct=ct: silu(i + 1, ct - 1))
                    jobs.append(lambda: silu(i + 1, 3))

                dve.wait_ge(eye_ready, i * 8 + 8)

                def mask_x(n):
                    l, g = divmod(n, 4)
                    d = g // 2
                    b = 1 << l
                    bank = got(uses, f"X{l}{g}", i)
                    at = C_LEV + (d * LEVELS + l) * 64
                    m = c[:, at:at + 64].rearrange("p (o a) -> p o a", o=1).to_broadcast([P, TT, 64]).rearrange("p t (a b) -> p t a b", b=b)
                    r = last_rows(1 - d) if l == LEVELS - 1 else slice(0, P)
                    xv = X[r, l, g % 2].rearrange("p t (a h b) -> p t a h b", h=2, b=b)[:, :, :, d, :]
                    if l == 0:
                        product = bank[:].rearrange("p (t a h b) -> p t a h b", t=TT, h=2, b=b)[:, :, :, d, :]
                    else:
                        product = bank[r, 0:256].rearrange("p (t a b) -> p t a b", t=TT, b=b)
                    nc.vector.tensor_tensor(xv, product, m[r], ALU.mult).then_inc(xm_ready, 1)

                def update(n):
                    l, g = divmod(n, 4)
                    d = g // 2
                    b = 1 << l
                    r = last_rows(d) if l == LEVELS - 1 else slice(0, P)
                    if l == 0:
                        dve.wait_ge(xm_ready, i * 28 + n + 1)
                        x, y = level(X[:, l, g % 2].rearrange("p t n -> p (t n)"), d, l), am[:].rearrange("p t (a b) -> p (t a) b", b=b)
                    else:
                        bank = got(uses, f"U{l}{g}", i)
                        x, y = (bank[r, at:at + 256].rearrange("p (a b) -> p a b", b=b) for at in (0, 256))
                    if l < LEVELS - 1:
                        Te = level(T[:, g].rearrange("p t n -> p (t n)"), d, l)
                        nc.vector.tensor_tensor(Te, Te, x, ALU.subtract).then_inc(link, 1)
                        links["k"] += 1
                    Uo = level(U[r, g].rearrange("p t n -> p (t n)"), d, l, 1)
                    if l == 0:
                        m = c[:, C_LEV + (1 - d) * LEVELS * 64:C_LEV + (1 - d) * LEVELS * 64 + 64].rearrange("p (o a) -> p o a", o=1).to_broadcast([P, TT, 64])
                        if g:
                            dve.wait_ge(upd_ready, i * 28 + n)
                        step(nc.vector.tensor_tensor(am[:].rearrange("p t (a b) -> p t a b", b=b), A[:, g].rearrange("p t (a h b) -> p t a h b", h=2, b=b)[:, :, :, 1 - d, :],
                                                     m.rearrange("p t (a b) -> p t a b", b=b), ALU.mult))
                    nc.vector.tensor_tensor(Uo, Uo, y, ALU.subtract).then_inc(upd_ready, 1)

                for n in range(LEVELS * 4 + 2):
                    if n >= 2:
                        update(n - 2)
                    if n < LEVELS * 4:
                        mask_x(n)
                    if jobs:
                        jobs.pop(0)()
                while jobs:
                    jobs.pop(0)()

                def z_silu(n):
                    dve.wait_ge(zt_ready, i * 2 + n + 1)
                    b = uses.at[f"z{n}"][0]
                    by_tile = lambda a: a.rearrange("p (t m) -> p t m", t=2)
                    nc.vector.scalar_tensor_tensor(out=z_pair(zs, n), in0=by_tile(sq[:, n]), scalar=1.0, in1=by_tile(ps[b][:]), op0=ALU.add, op1=ALU.mult).then_inc(zs_ready, 1)

                def gate_o(n):
                    dve.wait_ge(zs_ready, i * 2 + n + 1)
                    dve.wait_ge(o_step, 1 + i * 8 + 6 + 2 * n)
                    nc.vector.tensor_tensor(z_pair(zs, n), z_pair(zs, n), z_pair(o, n), ALU.mult)
                    dve.wait_ge(osq_ready, i * 2 + n + 1)
                    return nc.vector.tensor_reduce(ss[:, 4 * n:4 * n + 4], sq[:, n].rearrange("p (t m) -> p t m", m=P), AX.X, ALU.add)

                dve.wait_ge(zero_filled, 32)
                for st in range(4):
                    for d in range(2):
                        tt = 3 - st if d else st
                        if st:
                            bank = got(uses, f"kq{st}{d}", i)
                            for h in range(2):
                                ins = nc.vector.scalar_tensor_tensor(out=r[:, d, h], in0=bank[:, h * P:(h + 1) * P], scalar=gb[:, NEG_EG * TT + tt, d, h:h + 1],
                                                                     in1=v[:, h, tt], op0=ALU.mult, op1=ALU.add)
                            ins.then_inc(r_ready, 1)
                            if st >= 2:
                                dve.wait_ge(o_step, 1 + i * 8 + st * 2)
                            for h in range(2):
                                q = bank[:, 256 + h * P:256 + (h + 1) * P]
                                e = gb[:, EG * TT + tt, d, h:h + 1]
                                if st < 2:
                                    ins = nc.vector.tensor_scalar(o[:, tt, h], q, e, None, ALU.mult)
                                else:
                                    ins = nc.vector.scalar_tensor_tensor(out=o[:, tt, h], in0=q, scalar=e, in1=o[:, tt, h], op0=ALU.mult, op1=ALU.add)
                            ins.then_inc(oq_ready, 1)
                    if st == 3:
                        gate_o(0)
                    for d in range(2):
                        tt = 3 - st if d else st
                        bank = got(uses, f"os{st}{d}", i)
                        if 0 < st < 3:
                            dve.wait_ge(S_ready, i * 6 + (st - 1) * 2 + d + 1)
                        if st < 3:
                            for h in range(2):
                                if st == 0:
                                    ins = nc.vector.tensor_copy(St[:, d, h], bank[:, 256 + h * P:256 + (h + 1) * P])
                                else:
                                    ins = nc.vector.scalar_tensor_tensor(out=St[:, d, h], in0=St[:, d, h], scalar=gb[:, EGL * TT + tt, d, h:h + 1],
                                                                         in1=bank[:, 256 + h * P:256 + (h + 1) * P], op0=ALU.mult, op1=ALU.add)
                            ins.then_inc(S_ready, 1)
                        flat = o[:, tt].rearrange("p h n -> p (h n)")
                        if st:
                            dve.wait_ge(oq_ready, i * 6 + (st - 1) * 2 + d + 1)
                        if st == 0:
                            ins = nc.vector.tensor_copy(flat, bank[:, 0:256])
                        else:
                            ins = nc.vector.tensor_tensor(flat, flat, bank[:, 0:256], ALU.add)
                        ins.then_inc(o_step, 1)
                    if st == 1:
                        z_silu(0)
                z_silu(1)

                gate_o(1).then_inc(oss_ready, 1)
                dve.wait_ge(oss_ready, 1 + i + 1)
                step(nc.vector.tensor_scalar(ss[:], ss[:], 4.0 / DH, 4.0 * RMS_EPS, ALU.mult, ALU.add))
                rsqrt(nc, step, rs[:], ss[:], nt[:])
                for n in range(2):
                    rb = rs[:, 4 * n:4 * n + 4].rearrange("p (t h a) -> p t h a", t=2, a=1).to_broadcast([P, 2, 2, P])
                    pair = zs[:, 0:4:3] if n else zs[:, 1:3]
                    ins = nc.vector.tensor_tensor(pair, pair, rb, ALU.mult)
                ins.then_inc(og_ready, 1)
                if with_next:
                    normalise(uses, i, i + 1)
                for n in range(8):
                    tt, half = n // 2, n % 2
                    bank = got(uses, f"y{n}", i)
                    y = res[:, tt, half * 512:(half + 1) * 512]
                    nc.vector.tensor_tensor(y, y, bank[:], ALU.add).then_inc(y_ready, 1)
                    if with_next and n == 5:
                        mask_scores(uses, i, i + 1)
                    if not with_next:
                        if n:
                            row_stats(nc, t, n - 1)
                        dve.wait_ge(y_ready, 1 + i * 8 + n + 1)
                if not with_next:
                    row_stats(nc, t, 7)
                if with_next:
                    make_A(i + 1)
                    assert links["k"] == per, links["k"]

            normalise(FIRST_HEAD, -1, 0)
            mask_scores(FIRST_HEAD, -1, 0)
            make_A(0)
            links["base"] = links["k"]
            per = DN_DVE_STEPS
            with dve.Fori(0, NK - 1) as i:
                body(i, MAIN, True, per)
            body(NK - 1, LAST, False, per)


DN_DVE_STEPS = 3 + 4 * 4 + 1 + 4 + 24 + 1 + 2 + 2 * RSQRT_STEPS


class Steps:

    def __init__(self, dve, link):
        self.dve, self.link, self.k = dve, link, 0

    def __call__(self, ins):
        self.k += 1
        ins.then_inc(self.link, 1)
        self.dve.wait_ge(self.link, self.k)


def row_stats(nc, t, n):
    return nc.vector.bn_stats(t["stats"][:, n // 2, n % 2], t["res"][:, n // 2, (n % 2) * 512:(n % 2 + 1) * 512])


class RowNorm:

    def __init__(self, nc, t, sb, sem):
        self.nc, self.t = nc, t
        self.g, self.b, self.mv = sb("g", [P, D]), sb("b", [P, D]), sb("mv", [P, TT, 2])
        self.var, self.rstd, self.neg, self.shift, self.nt = (sb(n, [P, TT]) for n in ("var", "rstd", "neg", "shift", "nt"))
        self.rows_in, self.scale_ready, self.scaled, self.gained, self.normed, self.last_normed = (
            sem(n) for n in ("rows_in", "scale_ready", "scaled", "gained", "normed", "last_normed"))

    def load(self, sp, gain, bias):
        sp.dma_start(self.g[:], gain.partition_broadcast(P)).then_inc(self.rows_in, 16)
        sp.dma_start(self.b[:], bias.partition_broadcast(P)).then_inc(self.rows_in, 16)

    def wait(self, engine, tt):
        if tt == TT - 1:
            engine.wait_ge(self.last_normed, 1)
        else:
            engine.wait_ge(self.normed, tt + 1)

    def on_vector(self, dve, step):
        nc, res = self.nc, self.t["res"]
        for tt in range(TT):
            ins = nc.vector.bn_aggr(self.mv[:, tt], self.t["stats"][:, tt].rearrange("p h s -> p (h s)"))
        step(ins)
        nc.vector.tensor_scalar(self.neg[:], self.mv[:, :, 0], -1.0, None, ALU.mult)
        step(nc.vector.tensor_scalar(self.var[:], self.mv[:, :, 1], LN_EPS, None, ALU.add))
        rsqrt(nc, step, self.rstd[:], self.var[:], self.nt[:])
        nc.vector.tensor_tensor(self.shift[:], self.neg[:], self.rstd[:], ALU.mult).then_inc(self.scale_ready, 1)
        dve.wait_ge(self.rows_in, 32)
        for tt in range(TT - 1):
            step(nc.vector.scalar_tensor_tensor(out=res[:, tt], in0=res[:, tt], scalar=self.neg[:, tt:tt + 1], in1=self.g[:], op0=ALU.add, op1=ALU.mult))
            nc.vector.scalar_tensor_tensor(out=res[:, tt], in0=res[:, tt], scalar=self.rstd[:, tt:tt + 1], in1=self.b[:], op0=ALU.mult, op1=ALU.add).then_inc(self.normed, 1)

    def on_scalar(self, act):
        last = self.t["res"][:, TT - 1]
        act.wait_ge(self.scale_ready, 1)
        act.activation(last, last, ACT.Identity, scale=self.rstd[:, TT - 1:TT], bias=self.shift[:, TT - 1:TT]).then_inc(self.scaled, 1)

    def on_gpsimd(self, pool):
        last = self.t["res"][:, TT - 1]
        pool.wait_ge(self.rows_in, 32)
        pool.wait_ge(self.scaled, 1)
        self.nc.gpsimd.tensor_tensor(last, last, self.g[:], ALU.mult).then_inc(self.gained, 1)
        pool.wait_ge(self.gained, 1)
        self.nc.gpsimd.tensor_tensor(last, last, self.b[:], ALU.add).then_inc(self.last_normed, 1)


def norm(nc, t, dram, gname, bname, layer, name, out=None):
    c, ps, res, xT = t["const"], t["ps"], t["res"], t["xT"]
    ident = c[:, C_ID:C_ID + P]
    with ExitStack() as ctx:
        def sb(n, shape):
            return ctx.enter_context(nc.sbuf_tensor(f"{name}_{n}", shape, F32))

        sem = phase(nc, ctx, name + "_")
        rows = RowNorm(nc, t, sb, sem)
        turned, xT_ready, stored, link = (sem(n) for n in ("turned", "xT_ready", "stored", "link"))
        block = ctx.enter_context(nc.Block())

        @block.sync
        def _(sp):
            rows.load(sp, dram[gname][layer], dram[bname][layer])
            if out is None:
                sp.dma_start(t["mla_w_in"][:], dram["mla_w_in"][0].rearrange("(k p) n -> p k n", p=P)).then_inc(t["mla_w_loaded"], 16)
            else:
                for tt in range(TT):
                    rows.wait(sp, tt)
                    sp.dma_start(out[0, tt * P:(tt + 1) * P], res[:, tt]).then_inc(stored, 16)
                sp.wait_ge(stored, 16 * TT)

        @block.gpsimd
        def _(pool):
            rows.on_gpsimd(pool)

        @block.scalar
        def _(act):
            rows.on_scalar(act)
            if out is None:
                for n in range(8):
                    tt, half = n // 2, n % 2
                    act.wait_ge(turned, n + 1)
                    act.copy(xT[:, half * 4:half * 4 + 4, tt * P:(tt + 1) * P], ps[n % 4][:].rearrange("p (k n) -> p k n", k=4)).then_inc(xT_ready, 1)

        if out is None:
            @block.tensor
            def _(pe):
                for n in range(8):
                    tt, half = n // 2, n % 2
                    rows.wait(pe, tt)
                    if n >= 4:
                        pe.wait_ge(xT_ready, n - 3)
                    for k in range(4):
                        mm = pe.transpose(ps[n % 4][:, k * P:(k + 1) * P], res[:, tt, (half * 4 + k) * P:(half * 4 + k + 1) * P], ident)
                    mm.then_inc(turned, 1)

        @block.vector
        def _(dve):
            step = Steps(dve, link)
            rows.on_vector(dve, step)
            if out is None:
                for tt in range(TT):
                    dve.wait_ge(turned, 2 * tt + 2)
                    rows.wait(dve, tt)
                    nc.vector.tensor_scalar(res[:, tt], res[:, tt], ALPHA, None, ALU.mult)


NE, FF = 16, 256
CAP = 96
EXTRA = 2 * SEQ // (CAP + 1)
BLOCKS = NE + EXTRA
PIECES = (SEQ - 1) // CAP
RING = 3


def expert_rows(dram, layer):
    return (dram["moe_w_gate"][layer].rearrange("e (k p) f -> p e k f", p=P), dram["moe_w_up"][layer].rearrange("e (k p) f -> p e k f", p=P),
            dram["moe_w_down"][layer].rearrange("e (k p) n -> p e k n", p=P))


def mixture(nc, t, dram, gname, bname, layer, name):
    c, ps, res, xT = t["const"], t["ps"], t["res"], t["xT"]
    ident = c[:, C_ID:C_ID + P]
    with ExitStack() as ctx:
        def sb(n, shape, dt=F32):
            return ctx.enter_context(nc.sbuf_tensor(f"{name}_{n}", shape, dt))

        wgu, wd = sb("wgu", [P, RING, KD, 2, FF]), sb("wd", [P, RING, 2, D])
        x_rows, y_rows = sb("x_rows", [CAP, 3, D]), sb("y_rows", [CAP, 3, D])
        xgT = sb("xgT", [P, 3, KD, CAP])
        silu, hid, hidT = sb("silu", [CAP, FF]), sb("hid", [CAP, FF]), sb("hidT", [P, 2, CAP])
        counts = sb("counts", [1, 1], mybir.dt.uint32)
        owner = sb("owner", [1, EXTRA], mybir.dt.uint32)
        place, gate2 = sb("place", [P, 2, TT], mybir.dt.uint32), sb("gate2", [P, 2, TT])
        route_and_run(nc, t, dram, gname, bname, layer, name, locals())
        extra_blocks(nc, t, dram, layer, name, locals())
        combine(nc, t, name, locals())


def route_and_run(nc, t, dram, gname, bname, layer, name, m):
    c, ps, res, xT = t["const"], t["ps"], t["res"], t["xT"]
    ident, ones, before = c[:, C_ID:C_ID + P], c[:, C_ONE:C_ONE + P], c[:, C_SB:C_SB + P]
    wgu, wd, x_rows, y_rows, xgT, silu, hid, hidT = (m[n] for n in ("wgu", "wd", "x_rows", "y_rows", "xgT", "silu", "hid", "hidT"))
    place, gate2, counts, owner = m["place"], m["gate2"], m["counts"], m["owner"]
    slots_x, slots_y = t["slots_x"], t["slots_y"]
    g_dram, u_dram, d_dram = expert_rows(dram, layer)

    with ExitStack() as ctx:
        def sb(n, shape, dt=F32):
            return ctx.enter_context(nc.sbuf_tensor(f"{name}_{n}", shape, dt))

        sem = phase(nc, ctx, name + "_")
        rows = RowNorm(nc, t, sb, sem)
        rw, rb = sb("rw", [P, KD, NE]), sb("rb", [P, NE])
        s, sel, decay, w, chosen = (sb(n, [P, TT, NE]) for n in ("s", "sel", "decay", "w", "chosen"))
        beat, tie = sb("beat", [P, 16, 4, 4]), sb("tie", [P, 16, 4, 4])
        cnt = sb("cnt", [P, 64])
        gs, gcnt, total = sb("gs", [P, TT, 4]), sb("gcnt", [P, 16]), sb("total", [P, TT])
        rank, piece, slot, moved = (sb(n, [P, TT, NE]) for n in ("rank", "piece", "slot", "moved"))
        load, extra, base, ends = (sb(n, [P, NE]) for n in ("load", "extra", "base", "ends"))
        below = sb("below", [P, NE, NE])
        slot2 = sb("slot2", [P, 2, TT])
        owner_f = sb("owner_f", [P, EXTRA])

        router_in, turned, xT_ready, logits, e_ready, link = (sem(n) for n in ("router_in", "turned", "xT_ready", "logits", "e_ready", "link"))
        chosen_ready, ranked, place_ready, scattered = (sem(n) for n in ("chosen_ready", "ranked", "place_ready", "scattered"))
        gu_in, d_in = [sem(f"gu_in{n}") for n in range(RING)], [sem(f"d_in{n}") for n in range(RING)]
        rows_loaded, stored = [sem(f"rows_loaded{n}") for n in range(3)], [sem(f"stored{n}") for n in range(3)]
        rowsT_full, rowsT_ready = sem("rowsT_full"), [sem("rowsT_act"), sem("rowsT_dve")]
        gu_full, silu_ready, hid_ready, hidT_full, hidT_ready = (sem(n) for n in ("gu_full", "silu_ready", "hid_ready", "hidT_full", "hidT_ready"))
        down_full, y_ready = sem("down_full"), [sem("y_act"), sem("y_dve")]
        block = ctx.enter_context(nc.Block())

        def pick(a, e):
            return a[:, e] if isinstance(e, int) else a[:, bass.ds(e, 1)].rearrange("p a k f -> p (a k) f")

        def rows_of(a, e):
            return a[e * CAP:(e + 1) * CAP] if isinstance(e, int) else a[bass.ds(e * CAP, CAP)]

        @block.sync
        def _(sp):
            rows.load(sp, dram[gname][layer], dram[bname][layer])
            sp.dma_start(rw[:], dram["router_w"].rearrange("(k p) e -> p k e", p=P)).then_inc(router_in, 16)
            sp.dma_start(rb[:], dram["router_bias"].partition_broadcast(P)).then_inc(router_in, 16)

            def load_weights(e, r):
                late = not isinstance(e, int)
                if late:
                    sp.wait_ge(gu_full, e - RING + 1)
                sp.dma_start(wgu[:, r, :, 0], pick(g_dram, e)).then_inc(gu_in[r], 16)
                sp.dma_start(wgu[:, r, :, 1], pick(u_dram, e)).then_inc(gu_in[r], 16)
                if late:
                    sp.wait_ge(down_full, e - RING + 1)
                sp.dma_start(wd[:, r], pick(d_dram, e)).then_inc(d_in[r], 16)

            for e in range(RING):
                load_weights(e, e)
            with sp.Fori(1, NE // RING) as q:
                for r in range(RING):
                    load_weights(q * RING + r, r)
            for e in range(NE // RING * RING, NE):
                r = e % RING
                sp.wait_ge(gu_full, e - RING + 1)
                sp.dma_start(wgu[:, r, :, 0], pick(g_dram, e)).then_inc(gu_in[r], 16)
                sp.dma_start(wgu[:, r, :, 1], pick(u_dram, e)).then_inc(gu_in[r], 16)
                sp.wait_ge(down_full, e - RING + 1)
                sp.dma_start(wd[:, r], pick(d_dram, e)).then_inc(d_in[r], 16)

        @block.gpsimd
        def _(pool):
            rows.on_gpsimd(pool)
            pool.wait_ge(place_ready, 1)
            for k in range(2):
                for tt in range(TT):
                    nc.gpsimd.indirect_dma_start(slots_x, bass.IndirectOffsetOnAxis(place[:, k, tt:tt + 1], 0), res[:, tt], None,
                                                 bounds_check=BLOCKS * CAP - 1).then_inc(scattered, 16)

        @block.tensor
        def _(pe):
            def turn(tt):
                rows.wait(pe, tt)
                for half in range(2):
                    n = tt * 2 + half
                    if n >= 4:
                        pe.wait_ge(xT_ready, n - 3)
                    for k in range(4):
                        mm = pe.transpose(ps[n % 4][:, k * P:(k + 1) * P], res[:, tt, (half * 4 + k) * P:(half * 4 + k + 1) * P], ident)
                    mm.then_inc(turned, 1)

            def route(tt):
                pe.wait_ge(xT_ready, 2 * tt + 2)
                for k in range(KD):
                    mm = pe.matmul(ps[4][:, tt * NE:(tt + 1) * NE], xT[:, k, tt * P:(tt + 1) * P], rw[:, k], start=k == 0, stop=k == KD - 1)
                return mm

            turn(0)
            pe.wait_ge(router_in, 32)
            for tt in range(1, TT):
                turn(tt)
                route(tt - 1)
            route(TT - 1).then_inc(logits, 1)
            pe.wait_ge(chosen_ready, 1)
            for tt in range(TT):
                for other in range(tt):
                    pe.matmul(ps[5][:, tt * NE:(tt + 1) * NE], ones, chosen[:, other], start=other == 0, stop=False)
                pe.matmul(ps[5][:, tt * NE:(tt + 1) * NE], before, chosen[:, tt], start=tt == 0, stop=True)
            for tt in range(TT):
                mm = pe.matmul(ps[5][:, 64:64 + NE], ones, chosen[:, tt], start=tt == 0, stop=tt == TT - 1)
            mm.then_inc(ranked, 1)

            def turn_rows(e, r, n):
                pe.wait_ge(rows_loaded[r], (n + 1) * 16)
                if not (isinstance(e, int) and e == 0):
                    for half in range(2):
                        pe.wait_ge(rowsT_ready[half], e)
                for k in range(KD):
                    mm = pe.transpose(ps[k // 4][:, k % 4 * CAP:(k % 4 + 1) * CAP], x_rows[:, r, k * P:(k + 1) * P], ident[0:CAP, 0:CAP])
                    if k % 4 == 3:
                        mm.then_inc(rowsT_full, 1)

            def gate_up(e, r, n):
                pe.wait_ge(gu_in[r], (n + 1) * 32)
                for half in range(2):
                    pe.wait_ge(rowsT_ready[half], e + 1)
                for k in range(KD):
                    mm = pe.matmul(ps[2][0:CAP], xgT[:, r, k], wgu[:, r, k].rearrange("p a f -> p (a f)"), start=k == 0, stop=k == KD - 1)
                mm.then_inc(gu_full, 1)

            def turn_hidden(e):
                pe.wait_ge(hid_ready, e + 1)
                for f in range(2):
                    mm = pe.transpose(ps[3][:, f * CAP:(f + 1) * CAP], hid[:, f * P:(f + 1) * P], ident[0:CAP, 0:CAP])
                mm.then_inc(hidT_full, 1)

            def down(e, r, n, first=False):
                pe.wait_ge(d_in[r], (n + 1) * 16)
                pe.wait_ge(hidT_ready, e + 1)
                if not first:
                    pe.wait_ge(y_ready[0], e)
                    pe.wait_ge(y_ready[1], e)
                for half in range(2):
                    for f in range(2):
                        mm = pe.matmul(ps[4 + half][0:CAP], hidT[:, f], wd[:, r, f, half * 512:(half + 1) * 512], start=f == 0, stop=f == 1)
                mm.then_inc(down_full, 1)

            turn_rows(0, 0, 0)
            gate_up(0, 0, 0)
            turn_rows(1, 1, 0)
            def round_(q, first):
                for r in range(RING):
                    e = q * RING + r
                    turn_hidden(e)
                    gate_up(e + 1, (r + 1) % RING, q + (r + 1) // RING)
                    turn_rows(e + 2, (r + 2) % RING, q + (r + 2) // RING)
                    down(e, r, q, first and r == 0)
            round_(0, True)
            with pe.Fori(1, NE // RING) as q:
                round_(q, False)
            turn_hidden(NE - 1)
            down(NE - 1, (NE - 1) % RING, (NE - 1) // RING)

        @block.scalar
        def _(act):
            rows.on_scalar(act)
            for n in range(8):
                tt, half = n // 2, n % 2
                act.wait_ge(turned, n + 1)
                act.copy(xT[:, half * 4:half * 4 + 4, tt * P:(tt + 1) * P], ps[n % 4][:].rearrange("p (k n) -> p k n", k=4)).then_inc(xT_ready, 1)
            act.wait_ge(logits, 1)
            act.activation(decay[:].rearrange("p t e -> p (t e)"), ps[4][:, 0:64], ACT.Exp, scale=-1.0).then_inc(e_ready, 1)
            act.wait_ge(scattered, 16 * 2 * TT)

            def load_rows(e, r):
                act.dma_start(x_rows[:, r], rows_of(slots_x, e)).then_inc(rows_loaded[r], 16)

            def rowsT(e, r):
                act.wait_ge(rowsT_full, 2 * e + 1)
                act.copy(xgT[:, r, 0:4].rearrange("p k n -> p (k n)"), ps[0][:, 0:4 * CAP]).then_inc(rowsT_ready[0], 1)

            def activate(e):
                act.wait_ge(gu_full, e + 1)
                if not (isinstance(e, int) and e == 0):
                    act.wait_ge(hid_ready, e)
                act.activation(silu[:], ps[2][0:CAP, 0:FF], ACT.Silu).then_inc(silu_ready, 1)

            def results(e, r, n, first):
                act.wait_ge(down_full, e + 1)
                if not first:
                    act.wait_ge(stored[r], n * 16)
                act.copy(y_rows[:, r, 0:512], ps[4][0:CAP]).then_inc(y_ready[0], 1)
                act.wait_ge(y_ready[0], e + 1)
                act.wait_ge(y_ready[1], e + 1)
                act.dma_start(rows_of(slots_y, e), y_rows[:, r]).then_inc(stored[r], 16)

            for e in range(3):
                load_rows(e, e)
            rowsT(0, 0)
            rowsT(1, 1)
            activate(0)

            def round_(q, first):
                for r in range(RING):
                    e = q * RING + r
                    if not (isinstance(e, int) and e + 3 > NE):
                        if first or r < 2:
                            load_rows(e + 3, r)
                    rowsT(e + 2, (r + 2) % RING)
                    activate(e + 1)
                    results(e, r, q, first)
            round_(0, True)
            with act.Fori(1, NE // RING - 1) as q:
                for r in range(RING):
                    e = q * RING + r
                    load_rows(e + 3, r)
                    rowsT(e + 2, (r + 2) % RING)
                    activate(e + 1)
                    results(e, r, q, False)
            q = NE // RING - 1
            for r in range(RING):
                e = q * RING + r
                if e + 3 <= NE:
                    load_rows(e + 3, r)
                rowsT(e + 2, (r + 2) % RING)
                activate(e + 1)
                results(e, r, q, False)
            results(NE - 1, (NE - 1) % RING, (NE - 1) // RING, False)
            for r in range(RING):
                act.wait_ge(stored[r], 16 * len(range(r, NE, RING)))

        @block.vector
        def _(dve):
            step = Steps(dve, link)
            rows.on_vector(dve, step)
            dve.wait_ge(e_ready, 1)
            dve.wait_ge(router_in, 32)
            step(nc.vector.tensor_scalar(decay[:], decay[:], 1.0, None, ALU.add))
            step(nc.vector.reciprocal(s[:], decay[:]))
            step(nc.vector.tensor_tensor(sel[:], s[:], rb[:].rearrange("p (a e) -> p a e", a=1).to_broadcast([P, TT, NE]), ALU.add))

            def losses(values, n, count):
                one = values.rearrange("p (g a j) -> p g a j", a=1, j=4).to_broadcast([P, n, 4, 4])
                other = values.rearrange("p (g i a) -> p g i a", i=4, a=1).to_broadcast([P, n, 4, 4])
                nc.vector.tensor_tensor(beat[:, 0:n], one, other, ALU.is_gt)
                step(nc.vector.tensor_tensor(tie[:, 0:n], one, other, ALU.is_equal))
                lower = c[:, C_JLT:C_JLT + 16].rearrange("p (a i) -> p a i", a=1).to_broadcast([P, n, 16])
                tied = tie[:, 0:n].rearrange("p g i j -> p g (i j)")
                step(nc.vector.tensor_tensor(tied, tied, lower, ALU.mult))
                step(nc.vector.tensor_tensor(beat[:, 0:n], beat[:, 0:n], tie[:, 0:n], ALU.add))
                step(nc.vector.tensor_reduce(count, beat[:, 0:n].rearrange("p g i j -> p (g i) j"), AX.X, ALU.add))

            ch = chosen[:].rearrange("p t e -> p (t e)")
            losses(sel[:].rearrange("p t e -> p (t e)"), 16, cnt[:])
            step(nc.vector.tensor_scalar(ch, cnt[:], 2.0, None, ALU.is_lt))
            step(nc.vector.tensor_tensor(w[:], chosen[:], sel[:], ALU.mult))
            step(nc.vector.tensor_reduce(gs[:].rearrange("p t g -> p (t g)"), w[:].rearrange("p t (g e) -> p (t g) e", e=4), AX.X, ALU.add))
            losses(gs[:].rearrange("p t g -> p (t g)"), 4, gcnt[:])
            step(nc.vector.tensor_scalar(gcnt[:], gcnt[:], 1.0, None, ALU.is_lt))
            in_group = chosen[:].rearrange("p t (g e) -> p (t g) e", e=4)
            nc.vector.tensor_tensor(in_group, in_group, gcnt[:].rearrange("p (g a) -> p g a", a=1).to_broadcast([P, 16, 4]), ALU.mult).then_inc(chosen_ready, 1)
            dve.wait_ge(chosen_ready, 1)
            step(nc.vector.tensor_tensor(w[:], chosen[:], s[:], ALU.mult))
            step(nc.vector.tensor_reduce(total[:], w[:], AX.X, ALU.add))
            step(nc.vector.reciprocal(total[:], total[:]))
            step(nc.vector.tensor_tensor(w[:], w[:], total[:].rearrange("p (t a) -> p t a", a=1).to_broadcast([P, TT, NE]), ALU.mult))

            dve.wait_ge(ranked, 1)
            nc.vector.tensor_copy(rank[:].rearrange("p t e -> p (t e)"), ps[5][:, 0:64])
            step(nc.vector.tensor_copy(load[:], ps[5][:, 64:64 + NE]))
            nc.vector.tensor_scalar(extra[:], load[:], float(CAP), None, ALU.is_gt)
            step(nc.vector.tensor_scalar(piece[:], rank[:], float(CAP), None, ALU.is_ge))
            for n in range(2, PIECES + 1):
                nc.vector.scalar_tensor_tensor(out=extra[:], in0=load[:], scalar=float(n * CAP), in1=extra[:], op0=ALU.is_gt, op1=ALU.add)
                flat = lambda a: a[:].rearrange("p t e -> p (t e)")
                step(nc.vector.scalar_tensor_tensor(out=flat(piece), in0=flat(rank), scalar=float(n * CAP), in1=flat(piece), op0=ALU.is_ge, op1=ALU.add))
            earlier = c[:, C_BELOW:C_BELOW + NE * NE].rearrange("p (a b) -> p a b", a=NE)
            step(nc.vector.tensor_tensor(below[:], earlier, extra[:].rearrange("p (a b) -> p a b", a=1).to_broadcast([P, NE, NE]), ALU.mult))
            step(nc.vector.tensor_reduce(base[:], below[:], AX.X, ALU.add))
            step(nc.vector.tensor_tensor(ends[:], base[:], extra[:], ALU.add))

            def over_tiles(a):
                return a.rearrange("p (a e) -> p a e", a=1).to_broadcast([P, TT, NE])

            number = c[:, C_NUM:C_NUM + NE]
            step(nc.vector.tensor_tensor(base[:], base[:], number, ALU.subtract))
            step(nc.vector.tensor_tensor(moved[:], piece[:], over_tiles(base[:]), ALU.add))
            step(nc.vector.tensor_scalar(moved[:], moved[:], float(NE - 1), None, ALU.add))
            step(nc.vector.tensor_scalar(slot[:], piece[:], 1.0, None, ALU.is_ge))
            step(nc.vector.tensor_tensor(slot[:], slot[:], moved[:], ALU.mult))
            step(nc.vector.tensor_tensor(slot[:], slot[:], over_tiles(number), ALU.add))
            step(nc.vector.tensor_tensor(slot[:], slot[:], piece[:], ALU.subtract))
            step(nc.vector.scalar_tensor_tensor(out=flat(slot), in0=flat(slot), scalar=float(CAP), in1=flat(rank), op0=ALU.mult, op1=ALU.add))
            big = float(BLOCKS * CAP)
            step(nc.vector.scalar_tensor_tensor(out=flat(moved), in0=flat(slot), scalar=1.0, in1=flat(chosen), op0=ALU.add, op1=ALU.mult))
            nc.vector.tensor_reduce(slot2[:, 0], moved[:], AX.X, ALU.max)
            step(nc.vector.tensor_scalar(rank[:], slot[:], -1.0, big, ALU.mult, ALU.add))
            step(nc.vector.tensor_tensor(rank[:], rank[:], chosen[:], ALU.mult))
            step(nc.vector.tensor_reduce(slot2[:, 1], rank[:], AX.X, ALU.max))
            nc.vector.tensor_scalar(slot2[:, 0], slot2[:, 0], -1.0, None, ALU.add)
            step(nc.vector.tensor_scalar(slot2[:, 1], slot2[:, 1], -1.0, big, ALU.mult, ALU.add))
            nc.vector.tensor_copy(place[:], slot2[:]).then_inc(place_ready, 1)
            for k in range(2):
                at = slot2[:, k].rearrange("p (t a) -> p t a", a=1).to_broadcast([P, TT, NE])
                step(nc.vector.tensor_tensor(moved[:], slot[:], at, ALU.is_equal))
                step(nc.vector.tensor_tensor(moved[:], moved[:], w[:], ALU.mult))
                step(nc.vector.tensor_reduce(gate2[:, k], moved[:], AX.X, ALU.add))
            for n in range(EXTRA):
                ins = nc.vector.tensor_scalar(below[:, n], ends[:], float(n), None, ALU.is_le)
            step(ins)
            step(nc.vector.tensor_reduce(owner_f[:], below[:, 0:EXTRA], AX.X, ALU.add))
            step(nc.vector.tensor_scalar(owner_f[:], owner_f[:], float(NE - 1), None, ALU.min))
            nc.vector.tensor_copy(owner[:], owner_f[0:1])
            nc.vector.tensor_copy(counts[:], ends[0:1, NE - 1:NE])
            dve.wait_ge(scattered, 16 * 2 * TT)
            dve.wait_ge(turned, 8)
            rows.wait(dve, TT - 2)
            rows.wait(dve, TT - 1)
            for tt in range(TT):
                nc.vector.tensor_scalar(res[:, tt], res[:, tt], ALPHA, None, ALU.mult)

            def rowsT(e, r):
                dve.wait_ge(rowsT_full, 2 * e + 2)
                nc.vector.tensor_copy(xgT[:, r, 4:8].rearrange("p k n -> p (k n)"), ps[1][:, 0:4 * CAP]).then_inc(rowsT_ready[1], 1)

            def hidden(e):
                dve.wait_ge(silu_ready, e + 1)
                nc.vector.tensor_tensor(hid[:], silu[:], ps[2][0:CAP, FF:2 * FF], ALU.mult).then_inc(hid_ready, 1)

            def hiddenT(e):
                dve.wait_ge(hidT_full, e + 1)
                nc.vector.tensor_copy(hidT[:].rearrange("p f n -> p (f n)"), ps[3][:, 0:2 * CAP]).then_inc(hidT_ready, 1)

            def results(e, r, n, first):
                dve.wait_ge(down_full, e + 1)
                if not first:
                    dve.wait_ge(stored[r], n * 16)
                nc.vector.tensor_copy(y_rows[:, r, 512:1024], ps[5][0:CAP]).then_inc(y_ready[1], 1)

            rowsT(0, 0)
            rowsT(1, 1)
            hidden(0)

            def round_(q, first):
                for r in range(RING):
                    e = q * RING + r
                    hiddenT(e)
                    rowsT(e + 2, (r + 2) % RING)
                    hidden(e + 1)
                    results(e, r, q, first)
            round_(0, True)
            with dve.Fori(1, NE // RING) as q:
                round_(q, False)
            hiddenT(NE - 1)
            results(NE - 1, (NE - 1) % RING, (NE - 1) // RING, False)


def extra_blocks(nc, t, dram, layer, name, m):
    c, ps = t["const"], t["ps"]
    ident = c[:, C_ID:C_ID + P]
    wgu, wd, x_rows, y_rows, xgT, silu, hid, hidT, owner, counts = (m[n] for n in ("wgu", "wd", "x_rows", "y_rows", "xgT", "silu", "hid", "hidT", "owner", "counts"))
    g_dram, u_dram, d_dram = expert_rows(dram, layer)
    with ExitStack() as ctx:
        sem = phase(nc, ctx, name + "_x_")
        block_in, stored, rowsT_full, rowsT_ready, gu_full, silu_ready, hid_ready, hidT_full, hidT_ready, down_full, y_ready = (
            sem(n) for n in ("block_in", "stored", "rowsT_full", "rowsT_ready", "gu_full", "silu_ready", "hid_ready", "hidT_full", "hidT_ready", "down_full", "y_ready"))
        block = ctx.enter_context(nc.Block())

        def crowded(engine):
            return engine.value_load(counts[0:1, 0:1], min_val=0, max_val=EXTRA) > 0

        @block.sync
        def _(sp):
            with sp.If(crowded(sp)):
                sp.sem_inc(stored, 1)
                with sp.Fori(0, EXTRA) as n:
                    sp.wait_ge(stored, 1 + n * 16)
                    e = sp.value_load(owner[0:1, bass.ds(n, 1)], min_val=0, max_val=NE - 1)
                    pick = lambda a: a[:, bass.ds(e, 1)].rearrange("p a k f -> p (a k) f")
                    sp.dma_start(wgu[:, 0, :, 0], pick(g_dram)).then_inc(block_in, 16)
                    sp.dma_start(wgu[:, 0, :, 1], pick(u_dram)).then_inc(block_in, 16)
                    sp.dma_start(wd[:, 0], pick(d_dram)).then_inc(block_in, 16)
                    sp.dma_start(x_rows[:, 0], t["slots_x"][bass.ds((n + NE) * CAP, CAP)]).then_inc(block_in, 16)
                    sp.wait_ge(y_ready, n + 1)
                    sp.dma_start(t["slots_y"][bass.ds((n + NE) * CAP, CAP)], y_rows[:, 0]).then_inc(stored, 16)
                sp.wait_ge(stored, 1 + EXTRA * 16)

        @block.tensor
        def _(pe):
            with pe.If(crowded(pe)):
                with pe.Fori(0, EXTRA) as n:
                    pe.wait_ge(block_in, (n + 1) * 64)
                    for k in range(KD):
                        mm = pe.transpose(ps[k // 4][:, k % 4 * CAP:(k % 4 + 1) * CAP], x_rows[:, 0, k * P:(k + 1) * P], ident[0:CAP, 0:CAP])
                    mm.then_inc(rowsT_full, 1)
                    pe.wait_ge(rowsT_ready, n + 1)
                    for k in range(KD):
                        mm = pe.matmul(ps[2][0:CAP], xgT[:, 0, k], wgu[:, 0, k].rearrange("p a f -> p (a f)"), start=k == 0, stop=k == KD - 1)
                    mm.then_inc(gu_full, 1)
                    pe.wait_ge(hid_ready, n + 1)
                    for f in range(2):
                        mm = pe.transpose(ps[3][:, f * CAP:(f + 1) * CAP], hid[:, f * P:(f + 1) * P], ident[0:CAP, 0:CAP])
                    mm.then_inc(hidT_full, 1)
                    pe.wait_ge(hidT_ready, n + 1)
                    for half in range(2):
                        for f in range(2):
                            mm = pe.matmul(ps[4 + half][0:CAP], hidT[:, f], wd[:, 0, f, half * 512:(half + 1) * 512], start=f == 0, stop=f == 1)
                    mm.then_inc(down_full, 1)

        @block.scalar
        def _(act):
            with act.If(crowded(act)):
                with act.Fori(0, EXTRA) as n:
                    act.wait_ge(gu_full, n + 1)
                    act.activation(silu[:], ps[2][0:CAP, 0:FF], ACT.Silu).then_inc(silu_ready, 1)

        @block.vector
        def _(dve):
            with dve.If(crowded(dve)):
                with dve.Fori(0, EXTRA) as n:
                    dve.wait_ge(rowsT_full, n + 1)
                    for half in range(2):
                        ins = nc.vector.tensor_copy(xgT[:, 0, half * 4:half * 4 + 4].rearrange("p k n -> p (k n)"), ps[half][:, 0:4 * CAP])
                    ins.then_inc(rowsT_ready, 1)
                    dve.wait_ge(silu_ready, n + 1)
                    nc.vector.tensor_tensor(hid[:], silu[:], ps[2][0:CAP, FF:2 * FF], ALU.mult).then_inc(hid_ready, 1)
                    dve.wait_ge(hidT_full, n + 1)
                    nc.vector.tensor_copy(hidT[:].rearrange("p f n -> p (f n)"), ps[3][:, 0:2 * CAP]).then_inc(hidT_ready, 1)
                    dve.wait_ge(down_full, n + 1)
                    for half in range(2):
                        ins = nc.vector.tensor_copy(y_rows[:, 0, half * 512:(half + 1) * 512], ps[4 + half][0:CAP])
                    ins.then_inc(y_ready, 1)


def combine(nc, t, name, m):
    res, place, gate2 = t["res"], m["place"], m["gate2"]
    with ExitStack() as ctx:
        sem = phase(nc, ctx, name + "_c_")
        fetched_rows = ctx.enter_context(nc.sbuf_tensor(f"{name}_fetched", [P, 2, TT, D], F32))
        fetched = [[sem(f"fetched{k}{n}") for n in range(TT)] for k in range(2)]
        added = sem("added")
        block = ctx.enter_context(nc.Block())

        @block.gpsimd
        def _(pool):
            for tt in range(TT):
                for k in range(2):
                    nc.gpsimd.indirect_dma_start(fetched_rows[:, k, tt], None, t["slots_y"], bass.IndirectOffsetOnAxis(place[:, k, tt:tt + 1], 0),
                                                 bounds_check=BLOCKS * CAP - 1).then_inc(fetched[k][tt], 16)

        @block.vector
        def _(dve):
            for tt in range(TT):
                for k in range(2):
                    dve.wait_ge(fetched[k][tt], 16)
                    if k:
                        dve.wait_ge(added, 2 * tt + 1)
                    nc.vector.scalar_tensor_tensor(out=res[:, tt], in0=fetched_rows[:, k, tt], scalar=gate2[:, k, tt:tt + 1], in1=res[:, tt], op0=ALU.mult, op1=ALU.add).then_inc(added, 1)
                dve.wait_ge(added, 2 * tt + 2)
                row_stats(nc, t, 2 * tt)
                row_stats(nc, t, 2 * tt + 1)


NH, NOPE, ROPE, QR, KVR = 8, 128, 64, 384, 256
KQ_, KKV = QR // P, KVR // P


PROJ_QR, PROJ_K, PROJ_LATE = [("qr", 5), ("qn", 6)], [("kn", 7)], [("qrT", 1), ("v", 0)]


def mla_uses(first, last=False):
    names = [(f"S{n}", 4 + n) for n in range(4)]
    if not first:
        names += [(f"y{n}", n % 4) for n in range(8)]
    return Uses(names + PROJ_QR * (not last) + [(f"T{n}", n) for n in range(4)] + PROJ_K * (not last) + [("pv", 4)] + PROJ_LATE * (not last))


def latent_attention(nc, t, dram):
    c, ps, res, xT = t["const"], t["ps"], t["res"], t["xT"]
    ident = c[:, C_ID:C_ID + P]
    HEAD0 = Uses(PROJ_QR + PROJ_K + PROJ_LATE)
    FIRST, MAIN, LAST = mla_uses(True), mla_uses(False), mla_uses(False, True)
    scale = (NOPE + ROPE) ** -0.5
    with ExitStack() as ctx:
        def sb(n, shape, dt=F32):
            return ctx.enter_context(nc.sbuf_tensor(f"mla_{n}", shape, dt))

        sem = phase(nc, ctx, "mla_")

        W = QR + KVR + ROPE
        w_in, h = t["mla_w_in"], sb("h", [P, TT, W])
        junk = sb("junk", [P, QR])
        pos_i, pos = sb("pos_i", [P, TT], mybir.dt.int32), sb("pos", [P, TT])
        ang, turns, sin, cos = (sb(n, [P, TT, 32]) for n in ("ang", "turns", "sin", "cos"))
        ss, rs, nt = (sb(n, [P, 2 * TT]) for n in ("ss", "rs", "nt"))
        qw, kvw = sb("qw", [P, KQ_]), sb("kvw", [P, KKV])
        cqT, ckvT, krT = sb("cqT", [P, KQ_, SEQ]), sb("ckvT", [P, KKV, SEQ]), sb("krT", [P, SEQ])
        kr = sb("kr", [P, TT, 2, ROPE])
        rt = sb("rt", [P, 4, TT, 32])
        wq, wkv, wo = sb("wq", [P, KQ_, NOPE + ROPE]), sb("wkv", [P, KKV, 2 * P]), sb("wo", [P, D])
        qnT, knT, v = sb("qnT", [P, SEQ]), sb("knT", [P, SEQ]), sb("v", [P, TT, P])
        qr, qrT = sb("qr", [P, TT, ROPE]), sb("qrT", [P, 2, P])
        mx, nb, sums, inv = (sb(n, [P, TT]) for n in ("mx", "nb", "sums", "inv"))
        p, pT, oT = sb("p", [P, TT, SEQ]), sb("pT", [P, TT, SEQ]), sb("oT", [P, SEQ])

        full = [sem(f"full{b}") for b in range(8)]
        w_loaded, small_in = t["mla_w_loaded"], sem("small_in")
        wq_in, wkv_in, wo_in = sem("wq_in"), sem("wkv_in"), sem("wo_in")
        h_full, h_ready, sq_ready, norm_ready, kr_ready, cT_full, cT_ready, krT_ready = (
            sem(n) for n in ("h_full", "h_ready", "sq_ready", "norm_ready", "kr_ready", "cT_full", "cT_ready", "krT_ready"))
        ang_ready, trig_ready, link = sem("ang_ready"), sem("trig_ready"), sem("link")
        rope_read, qr_ready, qrT_ready, kv_ready, nb_ready, p_ready, pn_ready, oT_ready, y_ready = (
            sem(n) for n in ("rope_read", "qr_ready", "qrT_ready", "kv_ready", "nb_ready", "p_ready", "pn_ready", "oT_ready", "y_ready"))
        pT_ready = [sem("pT_ready_act"), sem("pT_ready_dve")]
        block = ctx.enter_context(nc.Block())

        def nth(uses, name, i):
            b, k = uses.at[name]
            if uses is HEAD0:
                return b, k
            k += HEAD0.per.get(b, 0)
            return b, (k if uses is FIRST else k + FIRST.per[b] + (i - 1) * MAIN.per[b])

        def read_of(name, i):
            n = int(name[-1]) if name[-1].isdigit() else 0
            h = i + 1
            if name[0] == "S":
                return p_ready, 4 * i + n + 1
            if name[0] == "T":
                return pT_ready[n % 2], 2 * i + n // 2 + 1
            if name[0] == "y":
                return y_ready, 1 + 8 * (i - 1) + n + 1
            return {"qr": (rope_read, h + 1), "qn": (kv_ready, 3 * h + 1), "kn": (kv_ready, 3 * h + 2), "v": (kv_ready, 3 * h + 3),
                    "qrT": (qrT_ready, h + 1), "pv": (oT_ready, i + 1)}[name]

        last_use = ["v", "qrT", "T2", "T3", "pv", "qr", "qn", "kn"]

        def rotate(step, out, x, last):
            a, b = x[:, :, 0:32], x[:, :, 32:64]
            step(nc.vector.tensor_tensor(rt[:, 0], a, cos[:], ALU.mult))
            step(nc.vector.tensor_tensor(rt[:, 1], b, sin[:], ALU.mult))
            step(nc.vector.tensor_tensor(rt[:, 2], b, cos[:], ALU.mult))
            last(nc.vector.tensor_tensor(rt[:, 3], a, sin[:], ALU.mult))
            step(nc.vector.tensor_tensor(out[:, :, 0:32], rt[:, 0], rt[:, 1], ALU.subtract))
            return nc.vector.tensor_tensor(out[:, :, 32:64], rt[:, 2], rt[:, 3], ALU.add)

        @block.sync
        def _(sp):
            sp.dma_start(pos_i[:], dram["positions"][0].rearrange("(t p) -> p t", p=P), allow_slow_non_contiguous=True).then_inc(small_in, 16)
            sp.dma_start(qw[:], dram["mla_q_norm"][0].rearrange("(k p) -> p k", p=P), allow_slow_non_contiguous=True).then_inc(small_in, 16)
            sp.dma_start(kvw[:], dram["mla_kv_norm"][0].rearrange("(k p) -> p k", p=P), allow_slow_non_contiguous=True).then_inc(small_in, 16)
            q_dram = dram["mla_w_qb"][0].rearrange("(k p) n -> p k n", p=P)
            kv_dram = dram["mla_w_kvb"][0].rearrange("(k p) n -> p k n", p=P)
            o_dram = dram["mla_w_out"][0]

            def load_projections(i):
                q, kv = (q_dram[:, :, i * 192:(i + 1) * 192], kv_dram[:, :, i * 256:(i + 1) * 256]) if isinstance(i, int) \
                    else (q_dram[:, :, bass.ds(i * 192, 192)], kv_dram[:, :, bass.ds(i * 256, 256)])
                if not (isinstance(i, int) and i == 0):
                    sp.wait_ge(kv_ready, 3 * i)
                    sp.wait_ge(qrT_ready, i)
                sp.dma_start(wq[:], q).then_inc(wq_in, 16)
                sp.dma_start(wkv[:], kv).then_inc(wkv_in, 16)

            def load_output(i):
                if not (isinstance(i, int) and i == 0):
                    sp.wait_ge(y_ready, 1 + 8 * i)
                sp.dma_start(wo[:], o_dram[i * P:(i + 1) * P] if isinstance(i, int) else o_dram[bass.ds(i * P, P)]).then_inc(wo_in, 16)

            load_projections(0)
            load_output(0)
            load_projections(1)
            with sp.Fori(1, NH - 1) as i:
                load_projections(i + 1)
                load_output(i)
            load_output(NH - 1)

        @block.tensor
        def _(pe):
            pe.wait_ge(w_loaded, 16)
            for tt in range(TT):
                for half in range(2):
                    for k in range(KD):
                        mm = pe.matmul(ps[2 * tt + half][:, 0:352], xT[:, k, tt * P:(tt + 1) * P], w_in[:, k, half * 352:(half + 1) * 352], start=k == 0, stop=k == KD - 1)
                mm.then_inc(h_full, 1)
            pe.wait_ge(h_ready, TT)
            for tt in range(TT):
                pe.wait_ge(norm_ready, tt + 1)
                if tt >= 2:
                    pe.wait_ge(cT_ready, 2 * tt - 2)
                for k in range(KQ_):
                    mm = pe.transpose(ps[3 * (tt % 2)][:, k * P:(k + 1) * P], h[:, tt, k * P:(k + 1) * P], ident)
                mm.then_inc(cT_full, 1)
                for k in range(KKV):
                    mm = pe.transpose(ps[3 * (tt % 2) + 1][:, k * P:(k + 1) * P], h[:, tt, QR + k * P:QR + (k + 1) * P], ident)
                mm.then_inc(cT_full, 1)
            pe.wait_ge(kr_ready, 1)
            for tt in range(TT):
                mm = pe.transpose(ps[2][:, tt * P:(tt + 1) * P], kr[:, tt].rearrange("p a n -> p (a n)"), ident)
            mm.then_inc(cT_full, 1)
            pe.wait_ge(cT_ready, 2 * TT)
            pe.wait_ge(krT_ready, 1)

            def bank_of(uses, i):
                def begin(name):
                    b, k = uses.at[name]
                    if k:
                        pe.wait_ge(*read_of(uses.before[name], i))
                    elif uses is not HEAD0 and (uses is not FIRST or b in HEAD0.per):
                        pe.wait_ge(*read_of(last_use[b], i - 1))
                    return ps[b]

                def done(mm, name):
                    mm.then_inc(full[uses.at[name][0]], 1)
                return begin, done

            def project_q(begin, done, h):
                pe.wait_ge(wq_in, (h + 1) * 16)
                bank = begin("qr")
                for tt in range(TT):
                    for k in range(KQ_):
                        mm = pe.matmul(bank[:, tt * 64:(tt + 1) * 64], cqT[:, k, tt * P:(tt + 1) * P], wq[:, k, NOPE:NOPE + ROPE], start=k == 0, stop=k == KQ_ - 1)
                done(mm, "qr")
                bank = begin("qn")
                for k in range(KQ_):
                    mm = pe.matmul(bank[:], wq[:, k, 0:NOPE], cqT[:, k], start=k == 0, stop=k == KQ_ - 1)
                done(mm, "qn")

            def project_k(begin, done, h):
                pe.wait_ge(wkv_in, (h + 1) * 16)
                bank = begin("kn")
                for k in range(KKV):
                    mm = pe.matmul(bank[:], wkv[:, k, 0:P], ckvT[:, k], start=k == 0, stop=k == KKV - 1)
                done(mm, "kn")

            def project_late(begin, done, h):
                pe.wait_ge(qr_ready, h + 1)
                bank = begin("qrT")
                for n in range(2):
                    mm = pe.transpose(bank[:, n * P:(n + 1) * P], qr[:, 2 * n:2 * n + 2].rearrange("p a n -> p (a n)"), ident)
                done(mm, "qrT")
                bank = begin("v")
                for tt in range(TT):
                    for k in range(KKV):
                        mm = pe.matmul(bank[:, tt * P:(tt + 1) * P], ckvT[:, k, tt * P:(tt + 1) * P], wkv[:, k, P:2 * P], start=k == 0, stop=k == KKV - 1)
                done(mm, "v")

            def body(i, uses):
                begin, done = bank_of(uses, i)
                pe.wait_ge(kv_ready, 3 * i + 2)
                pe.wait_ge(qrT_ready, i + 1)
                for n in range(TT):
                    bank = begin(f"S{n}")
                    pe.matmul(bank[:], qnT[:, n * P:(n + 1) * P], knT[:], start=True, stop=False)
                    half = slice(ROPE * (n % 2), ROPE * (n % 2) + ROPE)
                    done(pe.matmul(bank[:], qrT[half, n // 2], krT[half], start=False, stop=True), f"S{n}")
                if uses is not FIRST:
                    pe.wait_ge(wo_in, i * 16)
                    output(begin, done, i)
                if uses is not LAST:
                    project_q(begin, done, i + 1)
                for n in range(TT):
                    pe.wait_ge(pn_ready, 4 * i + n + 1)
                    bank = begin(f"T{n}")
                    for k in range(TT):
                        mm = pe.transpose(bank[:, k * P:(k + 1) * P], p[:, n, k * P:(k + 1) * P], ident)
                    done(mm, f"T{n}")
                if uses is not LAST:
                    project_k(begin, done, i + 1)
                for n in range(2):
                    pe.wait_ge(pT_ready[n], 2 * i + 2)
                pe.wait_ge(kv_ready, 3 * i + 3)
                bank = begin("pv")
                for k in range(TT):
                    mm = pe.matmul(bank[:], v[:, k], pT[:, k], start=k == 0, stop=k == TT - 1)
                done(mm, "pv")
                if uses is not LAST:
                    project_late(begin, done, i + 1)

            def output(begin, done, i):
                pe.wait_ge(oT_ready, i)
                for n in range(8):
                    tt, half = n // 2, n % 2
                    done(pe.matmul(begin(f"y{n}")[:], oT[:, tt * P:(tt + 1) * P], wo[:, half * 512:(half + 1) * 512], start=True, stop=True), f"y{n}")

            begin, done = bank_of(HEAD0, -1)
            project_q(begin, done, 0)
            project_k(begin, done, 0)
            project_late(begin, done, 0)
            body(0, FIRST)
            with pe.Fori(1, NH - 1) as i:
                body(i, MAIN)
            body(NH - 1, LAST)
            pe.wait_ge(wo_in, NH * 16)
            pe.wait_ge(oT_ready, NH)
            for n in range(8):
                tt, half = n // 2, n % 2
                if n >= 4:
                    pe.wait_ge(y_ready, 1 + 8 * (NH - 1) + n - 3)
                else:
                    pe.wait_ge(pT_ready[n % 2], 2 * NH)
                pe.matmul(ps[n % 4][:], oT[:, tt * P:(tt + 1) * P], wo[:, half * 512:(half + 1) * 512], start=True, stop=True).then_inc(full[n % 4], 1)

        @block.scalar
        def _(act):
            act.wait_ge(ang_ready, 1)
            act.activation(sin[:], ang[:], ACT.Sin).then_inc(trig_ready, 1)
            act.activation(cos[:], turns[:], ACT.Sin).then_inc(trig_ready, 1)
            for tt in range(TT):
                act.wait_ge(h_full, tt + 1)
                for half in range(2):
                    ins = act.copy(h[:, tt, half * 352:(half + 1) * 352], ps[2 * tt + half][:, 0:352])
                ins.then_inc(h_ready, 1)
                act.wait_ge(h_ready, tt + 1)
                act.activation(junk[:], h[:, tt, 0:QR], ACT.Square, accum_out=ss[:, tt:tt + 1]).then_inc(sq_ready, 1)
                act.wait_ge(sq_ready, 2 * tt + 1)
                act.activation(junk[:, 0:KVR], h[:, tt, QR:QR + KVR], ACT.Square, accum_out=ss[:, TT + tt:TT + tt + 1]).then_inc(sq_ready, 1)
                act.wait_ge(sq_ready, 2 * tt + 2)
            act.wait_ge(small_in, 48)
            for tt in range(TT):
                act.wait_ge(cT_full, 2 * tt + 1)
                for k in range(KQ_):
                    ins = act.mul(cqT[:, k, tt * P:(tt + 1) * P], ps[3 * (tt % 2)][:, k * P:(k + 1) * P], qw[:, k:k + 1])
                ins.then_inc(cT_ready, 1)
                act.wait_ge(cT_full, 2 * tt + 2)
                for k in range(KKV):
                    ins = act.mul(ckvT[:, k, tt * P:(tt + 1) * P], ps[3 * (tt % 2) + 1][:, k * P:(k + 1) * P], kvw[:, k:k + 1])
                ins.then_inc(cT_ready, 1)
            act.wait_ge(cT_full, 2 * TT + 1)
            act.copy(krT[:], ps[2][:]).then_inc(krT_ready, 1)

            def got(uses, name, i):
                b, n = nth(uses, name, i)
                act.wait_ge(full[b], n + 1)
                return ps[b]

            def take(uses, i, names):
                for name in names:
                    out = {"qn": qnT[:], "kn": knT[:], "v": v[:].rearrange("p t n -> p (t n)")}[name]
                    act.copy(out, got(uses, name, i)[:]).then_inc(kv_ready, 1)

            def body(i, uses):
                for n in range(TT):
                    act.wait_ge(nb_ready, 4 * i + n + 1)
                    bank = ps[4 + n]
                    act.activation(p[:, n], bank[:], ACT.Exp, scale=scale, bias=nb[:, n:n + 1], accum_out=sums[:, n:n + 1]).then_inc(p_ready, 1)
                if uses is not LAST:
                    take(uses, i, ("qn",))
                for n in (0, 2):
                    bank = got(uses, f"T{n}", i)
                    act.copy(pT[:, :, n * P:(n + 1) * P], bank[:].rearrange("p (k n) -> p k n", k=TT)).then_inc(pT_ready[0], 1)
                if uses is not LAST:
                    take(uses, i, ("kn",))
                act.copy(oT[:], got(uses, "pv", i)[:]).then_inc(oT_ready, 1)
                if uses is not LAST:
                    take(uses, i, ("v",))

            take(HEAD0, -1, ("qn", "kn", "v"))
            body(0, FIRST)
            with act.Fori(1, NH - 1) as i:
                body(i, MAIN)
            body(NH - 1, LAST)

        @block.vector
        def _(dve):
            state = {"base": 0, "i": 0, "per": 0, "k": 0}

            def step(ins):
                state["k"] += 1
                ins.then_inc(link, 1)
                dve.wait_ge(link, state["base"] + state["i"] * state["per"] + state["k"])

            dve.sem_inc(y_ready, 1)
            dve.wait_ge(small_in, 48)
            step(nc.vector.tensor_copy(pos[:], pos_i[:]))
            step(nc.vector.tensor_tensor(ang[:], pos[:].rearrange("p (t a) -> p t a", a=1).to_broadcast([P, TT, 32]),
                                         c[:, C_FREQ:C_FREQ + 32].rearrange("p (a f) -> p a f", a=1).to_broadcast([P, TT, 32]), ALU.mult))
            big = 12582912.0
            step(nc.vector.tensor_scalar(turns[:], ang[:], float(1 / (2 * np.pi)), big, ALU.mult, ALU.add))
            step(nc.vector.tensor_scalar(turns[:], turns[:], big, None, ALU.subtract))
            for part in TWO_PI:
                step(nc.vector.scalar_tensor_tensor(out=ang[:], in0=turns[:], scalar=-part, in1=ang[:], op0=ALU.mult, op1=ALU.add))
            pi = float(np.nextafter(np.float32(np.pi), np.float32(0)))
            step(nc.vector.tensor_scalar(turns[:], ang[:], float(np.pi / 2), None, ALU.add))
            step(nc.vector.tensor_scalar(rt[:, 0], turns[:], pi, None, ALU.is_gt))
            step(nc.vector.scalar_tensor_tensor(out=turns[:], in0=rt[:, 0], scalar=float(-2 * np.pi), in1=turns[:], op0=ALU.mult, op1=ALU.add))
            step(nc.vector.tensor_scalar(turns[:], turns[:], pi, -pi, ALU.min, ALU.max))
            nc.vector.tensor_scalar(ang[:], ang[:], pi, -pi, ALU.min, ALU.max).then_inc(ang_ready, 1)
            dve.wait_ge(trig_ready, 2)
            dve.wait_ge(h_ready, TT)
            step(rotate(step, kr[:, :, 0], h[:, :, QR + KVR:], step))
            nc.vector.tensor_copy(kr[:, :, 1], kr[:, :, 0]).then_inc(kr_ready, 1)
            dve.wait_ge(sq_ready, 2 * TT)
            step(nc.vector.tensor_scalar(ss[:, 0:TT], ss[:, 0:TT], 1.0 / QR, RMS_EPS, ALU.mult, ALU.add))
            step(nc.vector.tensor_scalar(ss[:, TT:], ss[:, TT:], 1.0 / KVR, RMS_EPS, ALU.mult, ALU.add))
            rsqrt(nc, step, rs[:], ss[:], nt[:])
            for tt in range(TT):
                nc.vector.tensor_scalar(h[:, tt, 0:QR], h[:, tt, 0:QR], rs[:, tt:tt + 1], None, ALU.mult)
                nc.vector.tensor_scalar(h[:, tt, QR:QR + KVR], h[:, tt, QR:QR + KVR], rs[:, TT + tt:TT + tt + 1], None, ALU.mult).then_inc(norm_ready, 1)

            def add_output(i, n, b):
                y = res[:, n // 2, (n % 2) * 512:(n % 2 + 1) * 512]
                nc.vector.tensor_tensor(y, y, ps[b][:], ALU.add).then_inc(y_ready, 1)

            def got(uses, name, i):
                b, n = nth(uses, name, i)
                dve.wait_ge(full[b], n + 1)
                return ps[b]

            def turn_q(uses, i, h):
                def read(ins):
                    ins.then_inc(rope_read, 1)
                    dve.wait_ge(rope_read, h + 1)

                bank = got(uses, "qr", i)
                rotate(step, qr, bank[:, 0:TT * ROPE].rearrange("p (t n) -> p t n", t=TT), read).then_inc(qr_ready, 1)
                nc.vector.tensor_copy(qrT[:].rearrange("p a n -> p (a n)"), got(uses, "qrT", i)[:, 0:2 * P]).then_inc(qrT_ready, 1)

            def body(i, uses):
                for n in range(TT):
                    bank = got(uses, f"S{n}", i)
                    step(nc.vector.tensor_reduce(mx[:, n:n + 1], bank[:], AX.X, ALU.max))
                    nc.vector.tensor_scalar(nb[:, n:n + 1], mx[:, n:n + 1], -scale, None, ALU.mult).then_inc(nb_ready, 1)
                if uses is not FIRST:
                    for n in range(8):
                        got(uses, f"y{n}", i)
                        if n == 0:
                            dve.wait_ge(y_ready, 1 + 8 * (i - 1))
                        add_output(i - 1, n, n % 4)
                for n in range(TT):
                    dve.wait_ge(p_ready, 4 * i + n + 1)
                    step(nc.vector.reciprocal(inv[:, n:n + 1], sums[:, n:n + 1]))
                    nc.vector.tensor_scalar(p[:, n], p[:, n], inv[:, n:n + 1], None, ALU.mult).then_inc(pn_ready, 1)
                for n in (1, 3):
                    bank = got(uses, f"T{n}", i)
                    nc.vector.tensor_copy(pT[:, :, n * P:(n + 1) * P], bank[:].rearrange("p (k n) -> p k n", k=TT)).then_inc(pT_ready[1], 1)
                if uses is not LAST:
                    turn_q(uses, i, i + 1)

            turn_q(HEAD0, -1, 0)
            state["base"] += state["k"]
            state["k"] = 0
            body(0, FIRST)
            per = state["k"]
            state.update(per=per)

            def round_(i, uses):
                state.update(i=i, k=0)
                body(i, uses)
                assert uses is LAST or state["k"] == per
            with dve.Fori(1, NH - 1) as i:
                round_(i, MAIN)
            round_(NH - 1, LAST)
            for n in range(8):
                dve.wait_ge(full[n % 4], nth(LAST, f"T{n % 4}", NH - 1)[1] + 2 + n // 4)
                dve.wait_ge(y_ready, 1 + 8 * (NH - 1))
                add_output(NH - 1, n, n % 4)
                if n:
                    row_stats(nc, t, n - 1)
                dve.wait_ge(y_ready, 1 + 8 * (NH - 1) + n + 1)
            row_stats(nc, t, 7)


TWO_PI = (6.28125, 0.0019340515136718750, float(2 * np.pi - 6.28125 - 0.0019340515136718750))


def program(nc, dram, out):
    with ExitStack() as ctx:
        t = {
            "const": ctx.enter_context(nc.sbuf_tensor("masks", [P, C_ALL], F32)),
            "res": ctx.enter_context(nc.sbuf_tensor("res", [P, TT, D], F32)),
            "xT": ctx.enter_context(nc.sbuf_tensor("xT", [P, KD, SEQ], F32)),
            "ps": [ctx.enter_context(nc.psum_tensor(f"bank{b}", [P, 512], F32)) for b in range(8)],
            "slots_x": nc.dram_tensor("slots_x", (BLOCKS * CAP, D), F32, kind="Internal").ap(),
            "slots_y": nc.dram_tensor("slots_y", (BLOCKS * CAP, D), F32, kind="Internal").ap(),
            "stats": ctx.enter_context(nc.sbuf_tensor("stats", [P, TT, 2, 6], F32)),
            "mla_w_loaded": ctx.enter_context(nc.semaphore("mla_w_loaded")),
            "x_in": [ctx.enter_context(nc.semaphore(f"x_in_{n}")) for n in range(TT)],
        }
        delta_net(nc, t, dram)
        mixture(nc, t, dram, "ln1_g", "ln1_b", 0, "moe0")
        with nc.sbuf_tensor("mla_w_in_sb", [P, KD, QR + KVR + ROPE], F32) as t["mla_w_in"]:
            norm(nc, t, dram, "ln2_g", "ln2_b", 0, "norm1")
            latent_attention(nc, t, dram)
        mixture(nc, t, dram, "ln1_g", "ln1_b", 1, "moe1")
        norm(nc, t, dram, "ln2_g", "ln2_b", 1, "norm3", out=out)


_INS = ["x", "positions", "dn_w_in", "dn_conv_w", "dn_a_log", "dn_dt_bias", "dn_norm_w", "dn_w_out",
        "mla_w_in", "mla_q_norm", "mla_w_qb", "mla_kv_norm", "mla_w_kvb", "mla_w_out",
        "ln1_g", "ln1_b", "ln2_g", "ln2_b", "router_w", "router_bias", "moe_w_gate", "moe_w_up", "moe_w_down"]


def kernel(**inputs):
    import concourse.bacc as _bacc
    from concourse.bass_utils import run_bass_kernel_spmd as _run

    nc = _bacc.Bacc("TRN2", target_bir_lowering=False, num_devices=1)
    arrays = {name: np.ascontiguousarray(inputs[name]) for name in _INS}
    arrays["const"] = constants()
    dram = {name: nc.dram_tensor(name, a.shape, mybir.dt.from_np(a.dtype), kind="ExternalInput").ap() for name, a in arrays.items()}
    out = nc.dram_tensor("out", (1, SEQ, D), F32, kind="ExternalOutput").ap()
    program(nc, dram, out)
    return _run(nc, [arrays], core_ids=[0]).results[0]["out"]
```
